# Optimizing a Trainium2 kernel written in Bass

```python
import math
import jax
import jax.numpy as jnp
from jax import lax
import numpy as np
import jax, jax.numpy as jnp

D_MODEL = 1024
BATCH = 1
SEQ = 256
DEPTH = 1

N_HEADS = 8
N_KV_HEADS = 2
HEAD_DIM = 64
WINDOW = 128
BLOCK = 128
ATTN_Q = N_HEADS * HEAD_DIM
ATTN_KV = N_KV_HEADS * HEAD_DIM
N_BUCKETS = 32
MAX_EXACT = N_BUCKETS // 2
MAX_DISTANCE = 128
GM_WIDTH = 512
GM_GROUPS = 4
GM_GROUP_DIM = GM_WIDTH // GM_GROUPS
GM_CHUNK = 128
IN_WIDTH = ATTN_Q + 2 * ATTN_KV + 2 * GM_WIDTH + 2 * D_MODEL
N_GROUPS = 4
EXPERTS_PER_GROUP = 8
N_EXPERTS = N_GROUPS * EXPERTS_PER_GROUP
TOP_K = 2
D_EXPERT = 512
MOE_BLOCK = 128

EPS = 1e-6
NEG = -1e30


def rms_norm(x, g):
    xf = x.astype(jnp.float32)
    y = xf * lax.rsqrt(jnp.mean(xf * xf, axis=-1, keepdims=True) + EPS)
    return (y * g.astype(jnp.float32)).astype(x.dtype)

def layer_norm(x, g, b):
    xf = x.astype(jnp.float32)
    mu = jnp.mean(xf, axis=-1, keepdims=True)
    var = jnp.mean(jnp.square(xf - mu), axis=-1, keepdims=True)
    y = (xf - mu) * lax.rsqrt(var + EPS)
    return (y * g.astype(jnp.float32) + b.astype(jnp.float32)).astype(x.dtype)

def t5_bucket(dist):
    n = jnp.maximum(dist, 0)
    nf = jnp.maximum(n, 1).astype(jnp.float32)
    large = MAX_EXACT + (jnp.log(nf / MAX_EXACT) / math.log(MAX_DISTANCE / MAX_EXACT)
                         * (N_BUCKETS - MAX_EXACT)).astype(jnp.int32)
    large = jnp.minimum(large, N_BUCKETS - 1)
    return jnp.where(n < MAX_EXACT, n, large)

def band(t):
    prev = jnp.concatenate([jnp.zeros_like(t[:, :1]), t[:, :-1]], axis=1)
    return jnp.concatenate([prev, t], axis=2)

def sliding_window_attention(q, k, v, positions, sinks, rel_bias):
    B, S, _ = q.shape
    nb = S // BLOCK
    grp = N_HEADS // N_KV_HEADS
    q = q.reshape(B, nb, BLOCK, N_KV_HEADS, grp, HEAD_DIM)
    kb = band(k.reshape(B, nb, BLOCK, N_KV_HEADS, HEAD_DIM))
    vb = band(v.reshape(B, nb, BLOCK, N_KV_HEADS, HEAD_DIM))
    pq = positions.reshape(B, nb, BLOCK)
    pk = band(pq)
    bucket = t5_bucket(pq[..., :, None] - pk[..., None, :])
    bias = rel_bias[bucket].reshape(B, nb, BLOCK, 2 * BLOCK, N_KV_HEADS, grp)
    bias = bias.transpose(0, 1, 4, 5, 2, 3).astype(jnp.float32)
    qi = jnp.arange(BLOCK)[:, None] + BLOCK
    kj = jnp.arange(2 * BLOCK)[None, :]
    local = (kj <= qi) & (qi - kj < WINDOW)
    first = (jnp.arange(nb)[:, None, None] > 0) | (kj[None] >= BLOCK)
    mask = (local[None] & first)[None, :, None, None]
    scale = HEAD_DIM ** -0.5
    s = jnp.einsum('bnqhgd,bnshd->bnhgqs', q, kb).astype(jnp.float32)
    s = jnp.where(mask, s * scale + bias, NEG)
    sink = sinks.astype(jnp.float32).reshape(N_KV_HEADS, grp)[None, None, :, :, None, None]
    m = jnp.maximum(jnp.max(s, axis=-1, keepdims=True), sink)
    p = jnp.exp(s - m)
    p = p / (jnp.sum(p, axis=-1, keepdims=True) + jnp.exp(sink - m))
    o = jnp.einsum('bnhgqs,bnshd->bnqhgd', p.astype(v.dtype), vb)
    return o.reshape(B, S, ATTN_Q)

def spatial_gating(u, v, ln_g, ln_b, w_s, b_s):
    B, S, _ = v.shape
    nc = S // GM_CHUNK
    vn = layer_norm(v, ln_g, ln_b).reshape(B, nc, GM_CHUNK, GM_GROUPS, GM_GROUP_DIM)
    w = w_s * jnp.tril(jnp.ones((GM_CHUNK, GM_CHUNK), w_s.dtype))
    sv = jnp.einsum('gts,bnsgc->bntgc', w, vn) + b_s.T[:, :, None]
    return u * sv.reshape(B, S, GM_WIDTH)

def hierarchical_moe(h, w_rg, b_rg, w_re, b_re, w_gate, w_up, w_down):
    B, S, D = h.shape
    T = B * S
    hf = h.reshape(T, D)
    lg = (hf @ w_rg).astype(jnp.float32) + b_rg.astype(jnp.float32)
    g_idx = jnp.argmax(lg, axis=-1)
    p_g = jnp.take_along_axis(jax.nn.softmax(lg, axis=-1), g_idx[:, None], axis=-1)[:, 0]
    le = ((hf @ w_re).astype(jnp.float32) + b_re.astype(jnp.float32)).reshape(T, N_GROUPS, EXPERTS_PER_GROUP)
    le = jnp.take_along_axis(le, g_idx[:, None, None], axis=1)[:, 0]
    top_p, top_i = lax.top_k(jax.nn.softmax(le, axis=-1), TOP_K)
    top_p = top_p / jnp.sum(top_p, axis=-1, keepdims=True)
    weights = p_g[:, None] * top_p
    expert_id = g_idx[:, None] * EXPERTS_PER_GROUP + top_i
    A = T * TOP_K
    e_flat = expert_id.reshape(A)
    tok_flat = jnp.repeat(jnp.arange(T, dtype=jnp.int32), TOP_K)
    w_flat = weights.reshape(A)
    order = jnp.argsort(e_flat)
    e_sorted, tok_sorted, w_sorted = e_flat[order], tok_flat[order], w_flat[order]
    counts = jnp.bincount(e_flat, length=N_EXPERTS)
    starts = jnp.cumsum(counts) - counts
    padded = (counts + MOE_BLOCK - 1) // MOE_BLOCK * MOE_BLOCK
    pends = jnp.cumsum(padded)
    pstarts = pends - padded
    dest = pstarts[e_sorted] + (jnp.arange(A) - starts[e_sorted])
    R = (A + MOE_BLOCK - 1) // MOE_BLOCK * MOE_BLOCK + N_EXPERTS * MOE_BLOCK
    NB = R // MOE_BLOCK
    row_tok = jnp.zeros((R,), jnp.int32).at[dest].set(tok_sorted)
    row_w = jnp.zeros((R,), jnp.float32).at[dest].set(w_sorted)
    block_e = jnp.minimum(jnp.searchsorted(pends, jnp.arange(NB) * MOE_BLOCK, side='right'), N_EXPERTS - 1)
    xr = hf[row_tok].reshape(NB, MOE_BLOCK, D)

    def expert_block(args):
        xb, e = args
        return (jax.nn.silu(xb @ w_gate[e]) * (xb @ w_up[e])) @ w_down[e]

    yr = lax.map(expert_block, (xr, block_e)).reshape(R, D)
    out = jax.ops.segment_sum(yr.astype(jnp.float32) * row_w[:, None], row_tok, num_segments=T)
    return out.astype(h.dtype).reshape(B, S, D)

def first_inputs(seed: int = 0) -> dict:
    key = jax.random.key(seed)
    ks = jax.random.split(key, 26)

    def nrm(k, shape, scale):
        return jax.random.normal(k, shape, jnp.float32) * scale

    L = DEPTH
    return {
        'x': nrm(ks[0], (BATCH, SEQ, D_MODEL), 1.0),
        'c': nrm(ks[1], (BATCH, D_MODEL), 1.0),
        'positions': jnp.broadcast_to(jnp.arange(SEQ, dtype=jnp.int32), (BATCH, SEQ)),
        'rel_bias': nrm(ks[2], (N_BUCKETS, N_HEADS), 0.5),
        'w_ada': nrm(ks[3], (L, D_MODEL, 6 * D_MODEL), D_MODEL ** -0.5),
        'b_ada': nrm(ks[4], (L, 6 * D_MODEL), 0.02),
        'norm1_g': 1.0 + nrm(ks[5], (L, D_MODEL), 0.02),
        'w_in': nrm(ks[6], (L, D_MODEL, IN_WIDTH), D_MODEL ** -0.5),
        'sinks': nrm(ks[7], (L, N_HEADS), 0.5),
        'gm_ln_g': 1.0 + nrm(ks[8], (L, GM_WIDTH), 0.02),
        'gm_ln_b': nrm(ks[9], (L, GM_WIDTH), 0.02),
        'gm_w_s': nrm(ks[10], (L, GM_GROUPS, GM_CHUNK, GM_CHUNK), GM_CHUNK ** -0.5),
        'gm_b_s': 1.0 + nrm(ks[11], (L, GM_GROUPS, GM_CHUNK), 0.02),
        'p_a': nrm(ks[12], (L, ATTN_Q, D_MODEL), ATTN_Q ** -0.5),
        'p_b': nrm(ks[13], (L, GM_WIDTH, D_MODEL), GM_WIDTH ** -0.5),
        'w_o': nrm(ks[14], (L, D_MODEL, D_MODEL), D_MODEL ** -0.5),
        'norm2_g': 1.0 + nrm(ks[15], (L, D_MODEL), 0.02),
        'w_router_g': nrm(ks[16], (L, D_MODEL, N_GROUPS), D_MODEL ** -0.5),
        'b_router_g': nrm(ks[17], (L, N_GROUPS), 0.01),
        'w_router_e': nrm(ks[18], (L, D_MODEL, N_EXPERTS), D_MODEL ** -0.5),
        'b_router_e': nrm(ks[19], (L, N_EXPERTS), 0.01),
        'w_gate': nrm(ks[20], (L, N_EXPERTS, D_MODEL, D_EXPERT), D_MODEL ** -0.5),
        'w_up': nrm(ks[21], (L, N_EXPERTS, D_MODEL, D_EXPERT), D_MODEL ** -0.5),
        'w_down': nrm(ks[22], (L, N_EXPERTS, D_EXPERT, D_MODEL), D_EXPERT ** -0.5),
        'final_g': 1.0 + nrm(ks[23], (D_MODEL,), 0.02),
    }

def first_block(x, c, positions, rel_bias, w_ada, b_ada, norm1_g, w_in, sinks, gm_ln_g, gm_ln_b,
              gm_w_s, gm_b_s, p_a, p_b, w_o, norm2_g, w_router_g, b_router_g, w_router_e,
              b_router_e, w_gate, w_up, w_down, final_g):
    splits = np.cumsum([ATTN_Q, ATTN_KV, ATTN_KV, GM_WIDTH, GM_WIDTH, D_MODEL]).tolist()
    cs = jax.nn.silu(c)
    for l in range(DEPTH):
        mod = cs @ w_ada[l] + b_ada[l]
        sh1, sc1, g1, sh2, sc2, g2 = [m[:, None, :] for m in jnp.split(mod, 6, axis=-1)]
        h = rms_norm(x, norm1_g[l]) * (1.0 + sc1) + sh1
        q, k, v, gu, gv, ga, gb = jnp.split(h @ w_in[l], splits, axis=-1)
        y_a = sliding_window_attention(q, k, v, positions, sinks[l], rel_bias)
        y_b = spatial_gating(jax.nn.gelu(gu), jax.nn.gelu(gv), gm_ln_g[l], gm_ln_b[l], gm_w_s[l], gm_b_s[l])
        merged = jax.nn.sigmoid(ga) * (y_a @ p_a[l]) + jax.nn.sigmoid(gb) * (y_b @ p_b[l])
        x = x + g1 * (merged @ w_o[l])
        h = rms_norm(x, norm2_g[l]) * (1.0 + sc2) + sh2
        x = x + g2 * hierarchical_moe(h, w_router_g[l], b_router_g[l], w_router_e[l], b_router_e[l],
                                      w_gate[l], w_up[l], w_down[l])
    return rms_norm(x, final_g)


DEPTH_2 = 2

CHUNK = 64
CONV_CH = 512
CONV_WIDTH = 3
GLA_HEADS = 4
GLA_DK = 64
GLA_DV = 128
GLA_KW = GLA_HEADS * GLA_DK
GLA_VW = GLA_HEADS * GLA_DV
GATE_RANK = 16
GATE_NORMALIZER = 16.0
GATE_LOG_MIN = -1.0
MIX_WIDTH = CONV_CH + GLA_VW
IN_WIDTH_2 = 3 * CONV_CH + 2 * GLA_KW + 2 * GLA_VW + GATE_RANK
IN_SPLITS = (
    CONV_CH,
    2 * CONV_CH,
    3 * CONV_CH,
    3 * CONV_CH + GLA_KW,
    3 * CONV_CH + 2 * GLA_KW,
    3 * CONV_CH + 2 * GLA_KW + GLA_VW,
    3 * CONV_CH + 2 * GLA_KW + 2 * GLA_VW,
)
D_FF = 2816
N_EXPERTS_2 = 8
D_FF_EXPERT = 2816
N_DENSE = (DEPTH_2 + 1) // 2
N_MOE = DEPTH_2 // 2
DEEPNORM_ALPHA = (2.0 * DEPTH_2) ** 0.25
DEEPNORM_BETA = (8.0 * DEPTH_2) ** -0.25
LN_EPS = 1e-5
RMS_EPS = 1e-6


def _layernorm(x, g, b):
    xf = x.astype(jnp.float32)
    mu = jnp.mean(xf, axis=-1, keepdims=True)
    var = jnp.mean(jnp.square(xf - mu), axis=-1, keepdims=True)
    return ((xf - mu) * lax.rsqrt(var + LN_EPS) * g.astype(jnp.float32)
            + b.astype(jnp.float32)).astype(x.dtype)

def _causal_depthwise_conv(z, w):
    return lax.conv_general_dilated(
        z, w[:, None, :].astype(z.dtype), window_strides=(1,),
        padding=[(CONV_WIDTH - 1, 0)],
        dimension_numbers=("NWC", "WIO", "NWC"),
        feature_group_count=z.shape[-1])

def _gla_chunked(q, k, v, gk):
    bsz, seq = q.shape[0], q.shape[1]
    n_chunks = seq // CHUNK
    shp_k = (bsz, n_chunks, CHUNK, GLA_HEADS, GLA_DK)
    shp_v = (bsz, n_chunks, CHUNK, GLA_HEADS, GLA_DV)
    q = q.astype(jnp.float32).reshape(shp_k) * (GLA_DK ** -0.5)
    k = k.astype(jnp.float32).reshape(shp_k)
    v = v.astype(jnp.float32).reshape(shp_v)
    b = jnp.cumsum(gk.astype(jnp.float32).reshape(shp_k), axis=2)
    b_last = b[:, :, -1:]
    q_in = q * jnp.exp(b)
    k_in = k * jnp.exp(-b)
    k_out = k * jnp.exp(b_last - b)
    causal = jnp.tril(jnp.ones((CHUNK, CHUNK), dtype=bool))
    scores = jnp.einsum("bnihd,bnjhd->bnhij", q_in, k_in)
    scores = jnp.where(causal, scores, 0.0)
    o_intra = jnp.einsum("bnhij,bnjhv->bnihv", scores, v)
    kv_chunk = jnp.einsum("bnjhd,bnjhv->bnhdv", k_out, v)
    decay_chunk = jnp.exp(b_last[:, :, 0])

    def step(state, inp):
        kv_n, dec_n = inp
        return dec_n[..., None] * state + kv_n, state

    init = jnp.zeros((bsz, GLA_HEADS, GLA_DK, GLA_DV), jnp.float32)
    _, states = lax.scan(step, init, (jnp.swapaxes(kv_chunk, 0, 1), jnp.swapaxes(decay_chunk, 0, 1)))
    states = jnp.swapaxes(states, 0, 1)
    o_inter = jnp.einsum("bnihd,bnhdv->bnihv", q_in, states)
    return (o_intra + o_inter).reshape(bsz, seq, GLA_HEADS, GLA_DV)

def _mixer(u, w_in, conv_w, gk_w2, gk_b, gla_norm_w, w_out):
    bsz, seq, _ = u.shape
    proj = jnp.einsum("bsd,de->bse", u, w_in)
    c_b, c_c, c_h, q, k, v, g, g_low = jnp.split(proj, IN_SPLITS, axis=-1)
    y_conv = c_b * _causal_depthwise_conv(c_c * c_h, conv_w)
    gk = jax.nn.log_sigmoid((jnp.einsum("bsr,rk->bsk", g_low, gk_w2) + gk_b).astype(jnp.float32))
    gk = jnp.maximum(gk / GATE_NORMALIZER, GATE_LOG_MIN)
    o = _gla_chunked(q.reshape(bsz, seq, GLA_HEADS, GLA_DK),
                     k.reshape(bsz, seq, GLA_HEADS, GLA_DK),
                     v.reshape(bsz, seq, GLA_HEADS, GLA_DV),
                     gk.reshape(bsz, seq, GLA_HEADS, GLA_DK))
    o = o * lax.rsqrt(jnp.mean(jnp.square(o), axis=-1, keepdims=True) + RMS_EPS)
    o = o * gla_norm_w.astype(jnp.float32) * jax.nn.silu(
        g.astype(jnp.float32).reshape(bsz, seq, GLA_HEADS, GLA_DV))
    y_gla = o.reshape(bsz, seq, GLA_VW).astype(u.dtype)
    y = jnp.concatenate([y_conv, y_gla], axis=-1)
    return jnp.einsum("bse,ed->bsd", y, w_out)

def _dense_swiglu(u, w_gate, w_up, w_down):
    h = jax.nn.silu(jnp.einsum("bsd,df->bsf", u, w_gate)) * jnp.einsum("bsd,df->bsf", u, w_up)
    return jnp.einsum("bsf,fd->bsd", h, w_down)

def _moe_swiglu(u, w_router, w_gate, w_up, w_down):
    bsz, seq, dm = u.shape
    n_tok = bsz * seq
    xt = u.reshape(n_tok, dm)
    logits = jnp.dot(xt, w_router).astype(jnp.float32)
    top_logits, top_idx = lax.top_k(logits, TOP_K)
    top_w = jax.nn.softmax(top_logits, axis=-1).astype(u.dtype)
    flat_e = top_idx.reshape(-1)
    order = jnp.argsort(flat_e)
    tok = order // TOP_K
    group_sizes = jnp.bincount(flat_e, length=N_EXPERTS_2).astype(jnp.int32)
    xs = xt[tok]
    h = jax.nn.silu(lax.ragged_dot(xs, w_gate, group_sizes)) * lax.ragged_dot(xs, w_up, group_sizes)
    ys = lax.ragged_dot(h, w_down, group_sizes) * top_w.reshape(-1)[order][:, None]
    out = jax.ops.segment_sum(ys, tok, num_segments=n_tok)
    return out.reshape(bsz, seq, dm)

def second_inputs(seed: int = 0) -> dict:
    key = jax.random.key(seed)
    ks = jax.random.split(key, 24)
    nrm = jax.random.normal
    f32 = jnp.float32
    x = nrm(ks[0], (BATCH, SEQ, D_MODEL), f32)
    c = nrm(ks[1], (BATCH, D_MODEL), f32)
    ada_w = nrm(ks[2], (DEPTH_2, D_MODEL, 6 * D_MODEL), f32) * (0.1 * D_MODEL ** -0.5)
    ada_b = nrm(ks[3], (DEPTH_2, 6 * D_MODEL), f32) * 0.02
    w_in = nrm(ks[4], (DEPTH_2, D_MODEL, IN_WIDTH_2), f32) * D_MODEL ** -0.5
    conv_w = nrm(ks[5], (DEPTH_2, CONV_WIDTH, CONV_CH), f32) * CONV_WIDTH ** -0.5
    gk_w2 = nrm(ks[6], (DEPTH_2, GATE_RANK, GLA_KW), f32) * GATE_RANK ** -0.5
    gk_b = nrm(ks[7], (DEPTH_2, GLA_KW), f32) * 0.02
    gla_norm_w = 1.0 + 0.02 * nrm(ks[8], (DEPTH_2, GLA_DV), f32)
    w_out = nrm(ks[9], (DEPTH_2, MIX_WIDTH, D_MODEL), f32) * (DEEPNORM_BETA * MIX_WIDTH ** -0.5)
    ln1_g = 1.0 + 0.02 * nrm(ks[10], (DEPTH_2, D_MODEL), f32)
    ln1_b = 0.02 * nrm(ks[11], (DEPTH_2, D_MODEL), f32)
    ln2_g = 1.0 + 0.02 * nrm(ks[12], (DEPTH_2, D_MODEL), f32)
    ln2_b = 0.02 * nrm(ks[13], (DEPTH_2, D_MODEL), f32)
    ffn_w_gate = nrm(ks[14], (N_DENSE, D_MODEL, D_FF), f32) * D_MODEL ** -0.5
    ffn_w_up = nrm(ks[15], (N_DENSE, D_MODEL, D_FF), f32) * D_MODEL ** -0.5
    ffn_w_down = nrm(ks[16], (N_DENSE, D_FF, D_MODEL), f32) * (DEEPNORM_BETA * D_FF ** -0.5)
    router_w = nrm(ks[17], (N_MOE, D_MODEL, N_EXPERTS_2), f32) * D_MODEL ** -0.5
    moe_w_gate = nrm(ks[18], (N_MOE, N_EXPERTS_2, D_MODEL, D_FF_EXPERT), f32) * D_MODEL ** -0.5
    moe_w_up = nrm(ks[19], (N_MOE, N_EXPERTS_2, D_MODEL, D_FF_EXPERT), f32) * D_MODEL ** -0.5
    moe_w_down = nrm(ks[20], (N_MOE, N_EXPERTS_2, D_FF_EXPERT, D_MODEL), f32) * (DEEPNORM_BETA * D_FF_EXPERT ** -0.5)
    return {"x": x, "c": c, "ada_w": ada_w, "ada_b": ada_b, "w_in": w_in, "conv_w": conv_w,
            "gk_w2": gk_w2, "gk_b": gk_b, "gla_norm_w": gla_norm_w, "w_out": w_out,
            "ln1_g": ln1_g, "ln1_b": ln1_b, "ln2_g": ln2_g, "ln2_b": ln2_b,
            "ffn_w_gate": ffn_w_gate, "ffn_w_up": ffn_w_up, "ffn_w_down": ffn_w_down,
            "router_w": router_w, "moe_w_gate": moe_w_gate, "moe_w_up": moe_w_up,
            "moe_w_down": moe_w_down}

def second_block(x, c, ada_w, ada_b, w_in, conv_w, gk_w2, gk_b, gla_norm_w, w_out,
              ln1_g, ln1_b, ln2_g, ln2_b, ffn_w_gate, ffn_w_up, ffn_w_down,
              router_w, moe_w_gate, moe_w_up, moe_w_down):
    cond = jax.nn.silu(c)
    for layer in range(DEPTH_2):
        mod = (jnp.dot(cond, ada_w[layer]) + ada_b[layer])[:, None, :]
        sh1, sc1, g1, sh2, sc2, g2 = jnp.split(mod, 6, axis=-1)
        u = x * (1.0 + sc1) + sh1
        mix = _mixer(u, w_in[layer], conv_w[layer], gk_w2[layer], gk_b[layer],
                     gla_norm_w[layer], w_out[layer])
        x = _layernorm(DEEPNORM_ALPHA * x + (1.0 + g1) * mix, ln1_g[layer], ln1_b[layer])
        u = x * (1.0 + sc2) + sh2
        j = layer // 2
        if layer % 2 == 0:
            ff = _dense_swiglu(u, ffn_w_gate[j], ffn_w_up[j], ffn_w_down[j])
        else:
            ff = _moe_swiglu(u, router_w[j], moe_w_gate[j], moe_w_up[j], moe_w_down[j])
        x = _layernorm(DEEPNORM_ALPHA * x + (1.0 + g2) * ff, ln2_g[layer], ln2_b[layer])
    return x


def setup_inputs(seed=0):
    out = dict(first_inputs(seed))
    for name, value in second_inputs(seed + 1).items():
        if name != "x":
            out[name + "_2"] = value
    return out


def reference(
    x, c, positions, rel_bias, w_ada, b_ada, norm1_g, w_in, sinks, gm_ln_g, gm_ln_b, gm_w_s,
    gm_b_s, p_a, p_b, w_o, norm2_g, w_router_g, b_router_g, w_router_e, b_router_e, w_gate,
    w_up, w_down, final_g, c_2, ada_w_2, ada_b_2, w_in_2, conv_w_2, gk_w2_2, gk_b_2,
    gla_norm_w_2, w_out_2, ln1_g_2, ln1_b_2, ln2_g_2, ln2_b_2, ffn_w_gate_2, ffn_w_up_2,
    ffn_w_down_2, router_w_2, moe_w_gate_2, moe_w_up_2, moe_w_down_2,
):
    x = first_block(
        x, c, positions, rel_bias, w_ada, b_ada, norm1_g, w_in, sinks, gm_ln_g, gm_ln_b, gm_w_s,
        gm_b_s, p_a, p_b, w_o, norm2_g, w_router_g, b_router_g, w_router_e, b_router_e, w_gate,
        w_up, w_down, final_g,
    )
    return second_block(
        x, c_2, ada_w_2, ada_b_2, w_in_2, conv_w_2, gk_w2_2, gk_b_2, gla_norm_w_2, w_out_2,
        ln1_g_2, ln1_b_2, ln2_g_2, ln2_b_2, ffn_w_gate_2, ffn_w_up_2, ffn_w_down_2, router_w_2,
        moe_w_gate_2, moe_w_up_2, moe_w_down_2,
    )


_drawn_inputs = setup_inputs


def setup_inputs(seed=0):
    import zlib

    import numpy as np

    out = dict(_drawn_inputs(seed))
    spreads = {}
    factors = {'sinks': 4.456,
     'gm_ln_g': 3.038,
     'gm_ln_b': 2.764,
     'b_router_g': 8.0,
     'b_router_e': 3.885,
     'gk_b_2': 7.548,
     'gla_norm_w_2': 5.591}
    for name, (base, spread) in spreads.items():
        noise = np.random.default_rng([zlib.crc32(name.encode()), seed]).standard_normal(out[name].shape)
        drawn = base * np.exp(spread * noise) if base else spread * noise
        out[name] = jnp.asarray(drawn.astype(out[name].dtype))
    for name, factor in factors.items():
        out[name] = (out[name] * factor).astype(out[name].dtype)
    return out
```

```python
from contextlib import ExitStack
import math

import numpy as np
import concourse.bass as bass
from concourse import mybir

F32 = mybir.dt.float32
I32 = mybir.dt.int32
ALU = mybir.AluOpType
ACT = mybir.ActivationFunctionType
AX = mybir.AxisListType.X

P = 128
D = 1024
KD = D // P
T = 256
TT = T // P
SLOTS = 4
FU = 256
SLOT = 3 * FU * KD
CH = 512

HEADS, HD, GROUP_HEADS = 8, 64, 4
POOL_HEADS = (6, 7)
ATTN_SCALE = HD ** -0.5
BUCKETS, MAX_EXACT, MAX_DISTANCE = 32, 16, 128
NEG = -1e30
RMS_EPS = 1e-6
LN_EPS = 1e-5

NG, EG = 4, 8
NE1 = NG * EG
F1 = 512
U1 = F1 // FU
NE2 = 8
F2 = 2816
U2 = F2 // FU

GH, DK, DV, CK = 4, 64, 128, 64
GK_DIV, GK_MIN = 16.0, -1.0
ALPHA = 4.0 ** 0.25

SH1, SC1, G1, SH2, SC2, G2 = range(6)
SQ, SK, SV, SGU, SGV, SGA, SGB = 0, 512, 640, 768, 1280, 1792, 2816


def bucket_starts():
    n = np.arange(1, 4 * MAX_DISTANCE)
    large = MAX_EXACT + (np.log(n.astype(np.float32) / np.float32(MAX_EXACT))
                         / np.float32(math.log(MAX_DISTANCE / MAX_EXACT))
                         * np.float32(BUCKETS - MAX_EXACT)).astype(np.int32)
    bucket = np.where(n < MAX_EXACT, n, np.minimum(large, BUCKETS - 1))
    return [float(n[np.argmax(bucket >= b)]) for b in range(1, BUCKETS)]


class Count:

    def __init__(self, sem):
        self.sem, self.n = sem, 0


class Ring:

    def __init__(self):
        self.seq, self.loads = 0, [0] * SLOTS

    def take(self, dmas):
        i, s = self.seq, self.seq % SLOTS
        self.seq += 1
        self.loads[s] += 16 * dmas
        return s, self.loads[s], (i - SLOTS + 1 if i >= SLOTS else None)

    def loop(self, n, body):
        base, loads = self.seq, list(self.loads)
        per = 3 * 16 * (body // SLOTS)
        self.seq += n * body
        self.loads = [v + per * n for v in self.loads]

        def at(r, j):
            s = j % SLOTS
            return s, r * per + (loads[s] + 48 * (j // SLOTS + 1)), r * body + (base + j - SLOTS + 1)
        return at


def build(nc, a, out):
    with ExitStack() as ctx:
        def sb(name, shape, dt=F32):
            return ctx.enter_context(nc.sbuf_tensor(name, shape, dt))

        def sem(name):
            return ctx.enter_context(nc.semaphore(name))

        ring = sb("ring", [P, SLOTS, SLOT])
        x = sb("x", [P, TT, D])
        hT = sb("hT", [P, KD, T])
        tok = sb("tok", [P, TT, D])
        csB = sb("csB", [P, KD, P])
        gB = sb("gB", [P, 2, D])
        rowB = sb("rowB", [P, 2, D])
        arena = sb("arena", [P, 13824])
        ident = sb("ident", [P, P])
        triu = sb("triu", [P, P])
        chunk_triu = sb("chunk_triu", [P, P])
        chunk_tril = sb("chunk_tril", [P, P])
        vecA = sb("vecA", [104, P])
        vecB = sb("vecB", [96, P])
        colA = sb("colA", [P, 104])
        colB = sb("colB", [P, 96])
        csT = sb("csT", [P, 2, KD])
        modT = sb("modT", [P, 48])
        scale_col = sb("scale_col", [P, KD])
        w_router = sb("w_router", [P, KD, 36])
        b_router = sb("b_router", [P, 36])
        w_router2 = sb("w_router2", [P, KD, NE2])
        poscol = sb("poscol", [P, TT], I32)
        relD = sb("relD", [P, BUCKETS * HEADS])
        starts = sb("starts", [P, BUCKETS])
        sinkB = sb("sinkB", [P, HEADS])
        stat = sb("stat", [P, 128])
        newton = sb("newton", [P, 12])
        rt = sb("rt", [P, 320])
        rev = sb("rev", [P, 8])
        combine = sb("combine", [P, TT, NE1])
        gkw2 = sb("gkw2", [16, T])
        gkbB = sb("gkbB", [P, T])
        glnB = sb("glnB", [P, DV])

        def view(start, *shape):
            n = int(np.prod(shape))
            v = arena[:, start:start + n]
            if len(shape) == 2:
                v = v.rearrange("p (a b) -> p a b", a=shape[0])
            if len(shape) == 3:
                v = v.rearrange("p (a b c) -> p a b c", a=shape[0], b=shape[1])
            return v

        bias = view(0, HEADS, 384)
        pT = view(0, 6, CH)
        prob = view(3072, 6, CH)
        qT = view(6144, 4, T)
        yaT = view(6144, 4, T)
        kT = view(7168, T)
        v_tok = view(7424, TT, P)
        gv = view(7680, TT, 512)
        guT = view(8704, 4, T)
        gaT = view(9728, KD, T)
        gbT = view(11776, KD, T)
        dist = view(9728, 384)
        mask_v = view(10112, 384)
        pool_add = (view(10496, 384), view(12416, 384))
        posf = view(10880, 4, T)
        posrow = view(11904, T).bitcast(I32)
        relB = view(12160, BUCKETS * HEADS)
        wsT = view(5120, 4, P)
        bsB = view(5632, 4, P)
        cbT = view(0, 4, T)
        ccT = view(1024, 4, T)
        ygT = view(1024, 4, T)
        zT = view(2048, 4, T + 2)
        q2T = view(3080, 2, T)
        k2T = view(3592, 2, T)
        k_tok = view(4104, TT, T)
        v2 = view(4616, TT, 512)
        sg_tok = view(5640, TT, 512)
        gk = view(6664, TT, T)
        gkt = view(7176, TT, T)
        gku = view(7688, TT, T)
        ebT = view(8200, 2, T)
        enbT = view(8712, 2, T)
        er = view(9224, TT, T)
        scT = view(9736, 2, 4, P)
        state = view(10760, 3, 2, DV)
        o_tok = view(11528, TT, 512)
        conv = view(11528, 4, T)
        glT = arena[0:16, 12552:12552 + T]
        silu_g = view(0, 2, 2 * T)
        hid = view(1024, 2, 2 * T)

        ps = ctx.enter_context(nc.psum_tensor("ps", [P, 8, CH], F32))

        ring_full = [sem(f"ring_full{i}") for i in range(SLOTS)]
        ring_free = sem("ring_free")
        v_full, v_free, a_full, a_free = sem("v_full"), sem("v_free"), sem("a_full"), sem("a_free")
        gate_full, up_full, silu_done, hid_ready = sem("gate_full"), sem("up_full"), sem("silu_done"), sem("hid_ready")
        y_free, bias_done = sem("y_free"), sem("bias_done")
        got_x, got_vec, got_pos, got_spatial, got_router, got_rows = (
            sem(s) for s in ("got_x", "got_vec", "got_pos", "got_spatial", "got_router", "got_rows"))
        got_layer = sem("got_layer")
        stored = sem("stored")
        consts_step, consts_ready = sem("consts_step"), sem("consts_ready")
        dist_ready, bias_pool, pool_step = sem("dist_ready"), sem("bias_pool"), sem("pool_step")
        act_step = sem("act_step")
        names = ("cols_ready", "cs_broadcast", "tokens_normed", "hT_ready", "qkv_ready", "vn_ready", "scores_ready",
                 "probs_ready", "pT_ready", "ya_ready", "yb_ready", "merged_ready", "rows_used", "hT2_used",
                 "router_logits", "glow_ready", "gk_abs", "gk_exp1", "gk_ready", "gla_in", "gla_scores",
                 "states_ready", "o_normed", "mix_ready", "sink_ready", "dve_step", "layer_used", "x_ready")
        S = {s: Count(sem(s)) for s in names}
        H = {s: c.sem for s, c in S.items()}
        silu_c, gelu_u, gelu_v, sig_ab, exps_done, sink_exp, gk_e, gk_l, gla_exp, silu_gate, router_exp = (
            sem(s) for s in ("silu_c", "gelu_u", "gelu_v", "sig_ab", "exps_done", "sink_exp", "gk_e", "gk_l",
                             "gla_exp", "silu_gate", "router_exp"))

        block = ctx.enter_context(nc.Block())

        def chunk_k(w, c0, c1):
            return w.rearrange("(k p) n -> p k n", p=P)[:, :, c0:c1]

        def slot(s, kt, cols):
            return ring[:, s, 0:kt * cols].rearrange("p (k n) -> p k n", k=kt)

        def slot_gate(s):
            return ring[:, s, 0:KD * FU].rearrange("p (k n) -> p k n", k=KD)

        def slot_up(s):
            return ring[:, s, KD * FU:2 * KD * FU].rearrange("p (k n) -> p k n", k=KD)

        def slot_down(s):
            return ring[:, s, 2 * KD * FU:3 * KD * FU].rearrange("p (k n) -> p k n", k=2)

        MOE1_SEQ = 12 + 7 + 5
        ADA2_SEQ = [MOE1_SEQ + NE1 * U1, MOE1_SEQ + NE1 * U1 + 12 + 9 + U2]
        FFN_SEQ = ADA2_SEQ[0] + 12 + 9
        MOE2_SEQ = ADA2_SEQ[1] + 12 + 8
        C_IN2 = [(0, 512), (512, 1024), (1024, 1536), (1536, 2048), (2048, 2560), (2560, 3088)]
        W_OUT_CUTS = [[(0, 512), (512, 768), (768, 1024)], [(0, 512), (512, 1024)]]

        @block.sync
        def _(sp):
            r = Ring()

            def load(parts):
                s, _, free = r.take(len(parts))
                if free is not None:
                    sp.wait_ge(ring_free, free)
                at = 0
                for src in parts:
                    kt, n = src.shape[1], src.shape[2]
                    sp.dma_start(ring[:, s, at:at + kt * n].rearrange("p (k n) -> p k n", k=kt), src)\
                      .then_inc(ring_full[s], 16)
                    at += kt * n

            def load_ada(w):
                wk = w.rearrange("(k p) n -> p k n", p=P)
                base, loads = r.seq, list(r.loads)
                assert base % SLOTS == 0
                if base < SLOTS:
                    for h in range(2):
                        for c in range(4):
                            load([wk[:, :, h * 3 * D + c * CH:h * 3 * D + (c + 1) * CH]])
                else:
                    with sp.Fori(0, 2) as h:
                        for c in range(4):
                            sp.wait_ge(ring_free, h * SLOTS + (base + c - SLOTS + 1))
                            sp.dma_start(slot(c, KD, CH), wk[:, :, bass.ds(h * (3 * D) + c * CH, CH)])\
                              .then_inc(ring_full[c], 16)
                    for _ in range(8):
                        r.take(1)
                for g in (G1, G2):
                    for c in range(2):
                        load([wk[:, :, g * D + c * CH:g * D + (c + 1) * CH]])

            def load_units(gate, up, down, c0):
                return [chunk_k(gate, c0, c0 + FU), chunk_k(up, c0, c0 + FU),
                        down[c0:c0 + FU, :].rearrange("(k p) n -> p k n", p=P)]

            def load_experts(gate, up, down, ne, body_e, units):
                body = body_e * units
                at = r.loop(ne // body_e, body)
                with sp.Fori(0, ne // body_e) as i:
                    for j in range(body):
                        s, _, free = at(i, j)
                        e, c0 = i * body_e + j // units, (j % units) * FU
                        sp.wait_ge(ring_free, free)
                        g = gate[bass.ds(e, 1), :, c0:c0 + FU].rearrange("o (k p) n -> p (o k) n", p=P)
                        u = up[bass.ds(e, 1), :, c0:c0 + FU].rearrange("o (k p) n -> p (o k) n", p=P)
                        d = down[bass.ds(e, 1), c0:c0 + FU, :].rearrange("o (k p) n -> p (o k) n", p=P)
                        sp.dma_start(slot_gate(s), g).then_inc(ring_full[s], 16)
                        sp.dma_start(slot_up(s), u).then_inc(ring_full[s], 16)
                        sp.dma_start(slot_down(s), d).then_inc(ring_full[s], 16)

            load_ada(a["w_ada"][0])
            w = a["w_in"][0]
            s, _, free = r.take(10)
            sp.wait_ge(ring_free, free)
            for half in range(2):
                q_src = w[:, half * 256:half * 256 + 256].rearrange("(k p) (j d) -> p j k d", p=P, d=HD)
                for j in range(4):
                    sp.dma_start(slot(s, KD, 768)[:, :, j * P + half * HD:j * P + half * HD + HD], q_src[:, j])\
                      .then_inc(ring_full[s], 16)
            sp.dma_start(slot(s, KD, 768)[:, :, 512:640], chunk_k(w, SK, SV)).then_inc(ring_full[s], 16)
            sp.dma_start(slot(s, KD, 768)[:, :, 640:768], chunk_k(w, SV, SGU)).then_inc(ring_full[s], 16)
            for c in range(6):
                load([chunk_k(w, SGU + c * CH, SGU + (c + 1) * CH)])
            for c in range(2):
                load([chunk_k(a["p_a"][0], c * CH, (c + 1) * CH)])
            load([chunk_k(a["p_b"][0], 0, D)])
            for c in range(2):
                load([chunk_k(a["w_o"][0], c * CH, (c + 1) * CH)])
            load_experts(a["w_gate"][0], a["w_up"][0], a["w_down"][0], NE1, 2, U1)
            for layer in range(2):
                load_ada(a["ada_w_2"][layer])
                w = a["w_in_2"][layer]
                for c0, c1 in C_IN2:
                    load([chunk_k(w, c0, c1)])
                for c0, c1 in W_OUT_CUTS[layer]:
                    load([chunk_k(a["w_out_2"][layer], c0, c1)])
                if layer == 0:
                    for u in range(U2):
                        load(load_units(a["ffn_w_gate_2"][0], a["ffn_w_up_2"][0], a["ffn_w_down_2"][0], u * FU))
            load_experts(a["moe_w_gate_2"][0], a["moe_w_up_2"][0], a["moe_w_down_2"][0], NE2, 4, U2)
            sp.wait_ge(H["x_ready"], 1)
            sp.dma_start(out[0].rearrange("(t p) d -> p t d", p=P), x[:, :, :]).then_inc(stored, 16)
            sp.wait_ge(stored, 16)

        @block.gpsimd
        def _(pool):
            n = [0]

            def const(ins, ready=False):
                n[0] += 1
                ins.then_inc(consts_step, 1)
                pool.wait_ge(consts_step, n[0])

            def pair(first, second):
                for i, v in enumerate((first, second)):
                    if v is not None:
                        pool.dma_start(rowB[:, i, :], v.partition_broadcast(P)).then_inc(got_rows, 16)

            bada = a["b_ada"][0]
            pair(bada[G1 * D:G1 * D + D], bada[G2 * D:G2 * D + D])
            const(pool.memset(ident[:, :], 0.0))
            const(pool.affine_select(out=ident[:, :], in_=ident[:, :], compare_op=ALU.not_equal, fill=1.0, base=0,
                                     pattern=[[-1, P]], channel_multiplier=1))
            for m in (triu, chunk_triu):
                const(pool.memset(m[:, :], 1.0))
                const(pool.affine_select(out=m[:, :], in_=m[:, :], compare_op=ALU.is_ge, fill=0.0, base=0,
                                         pattern=[[1, P]], channel_multiplier=-1))
            const(pool.memset(chunk_triu[0:CK, CK:P], 0.0))
            const(pool.memset(chunk_tril[:, :], 1.0))
            const(pool.affine_select(out=chunk_tril[:, :], in_=chunk_tril[:, :], compare_op=ALU.is_ge, fill=0.0,
                                     base=-1, pattern=[[-1, P]], channel_multiplier=1))
            const(pool.memset(chunk_tril[CK:P, 0:CK], 0.0))
            for i in range(8):
                const(pool.memset(rev[:, i:i + 1], float(8 - i)))
            const(pool.memset(starts[:, 0:1], -3e38))
            for b, s in enumerate(bucket_starts()):
                const(pool.memset(starts[:, b + 1:b + 2], s))
            const(pool.memset(bias[:, 6:8, :], 0.0))
            pool.memset(stat[:, 127:128], 1.0).then_inc(consts_ready, 1)
            pool.wait_ge(dist_ready, 1)
            k = 0
            for b in range(BUCKETS):
                for i, h in enumerate(POOL_HEADS):
                    ins = pool.tensor_scalar(pool_add[i], dist, starts[:, b:b + 1],
                                             relD[:, b * HEADS + h:b * HEADS + h + 1], ALU.is_ge, ALU.mult)
                ins.then_inc(pool_step, 1)
                k += 1
                pool.wait_ge(pool_step, k)
                for i, h in enumerate(POOL_HEADS):
                    ins = pool.tensor_tensor(bias[:, h, :], bias[:, h, :], pool_add[i], ALU.add)
                ins.then_inc(pool_step, 1)
                k += 1
                pool.wait_ge(pool_step, k)
            for h in POOL_HEADS:
                for part in range(3):
                    lo = part * P
                    sign, base = (-1, 0) if part != 1 else (1, -1)
                    ins = pool.affine_select(out=bias[:, h, lo:lo + P], in_=bias[:, h, lo:lo + P],
                                             compare_op=ALU.is_ge, fill=NEG, base=base,
                                             pattern=[[sign, P]], channel_multiplier=-sign)
            ins.then_inc(bias_pool, 1)
            pool.wait_ge(bias_done, 1)
            for h in range(6):
                for part in range(3):
                    lo = part * P
                    sign, base = (-1, 0) if part != 1 else (1, -1)
                    ins = pool.affine_select(out=bias[:, h, lo:lo + P], in_=bias[:, h, lo:lo + P],
                                             compare_op=ALU.is_ge, fill=NEG, base=base,
                                             pattern=[[sign, P]], channel_multiplier=-sign)
            ins.then_inc(bias_pool, 1)
            used = 1
            pool.wait_ge(H["rows_used"], used)
            pool.dma_start(rowB[:, 0, 0:512], a["gm_ln_g"][0].partition_broadcast(P)).then_inc(got_rows, 16)
            pool.dma_start(rowB[:, 0, 512:1024], a["gm_ln_b"][0].partition_broadcast(P)).then_inc(got_rows, 16)
            pool.wait_ge(H["rows_used"], 2)
            pool.dma_start(rowB[:, 0, :], a["final_g"].partition_broadcast(P)).then_inc(got_rows, 16)
            used = 3
            for layer in range(2):
                b = a["ada_b_2"][layer]
                for one, two in ((b[G1 * D:G1 * D + D], b[G2 * D:G2 * D + D]),
                                 (a["ln1_g_2"][layer], a["ln1_b_2"][layer]),
                                 (a["ln2_g_2"][layer], a["ln2_b_2"][layer])):
                    pool.wait_ge(H["rows_used"], used)
                    pair(one, two)
                    used += 1

        @block.scalar
        def _(act):
            def load(dst, src, s):
                act.dma_start(dst, src, allow_slow_non_contiguous=True).then_inc(s, 16)

            load(vecA[0:48, :], a["b_ada"][0].rearrange("(r p) -> r p", p=P), got_vec)
            load(vecA[48:56, :], a["c"][0].rearrange("(r p) -> r p", p=P), got_vec)
            load(vecA[56:64, :], a["norm1_g"][0].rearrange("(r p) -> r p", p=P), got_vec)
            load(vecA[64:72, :], a["norm2_g"][0].rearrange("(r p) -> r p", p=P), got_vec)
            load(vecA[72:80, :], a["c_2"][0].rearrange("(r p) -> r p", p=P), got_vec)
            load(vecA[80:104, :], a["conv_w_2"].rearrange("l j (r p) -> (l j r) p", p=P), got_vec)
            load(vecB[:, :], a["ada_b_2"].rearrange("l (r p) -> (l r) p", p=P), got_vec)
            load(x[:, :, :], a["x"][0].rearrange("(t p) d -> p t d", p=P), got_x)
            load(posrow, a["positions"][0].partition_broadcast(P), got_pos)
            load(poscol[:, :], a["positions"][0].rearrange("(t p) -> p t", p=P), got_pos)
            load(relB, a["rel_bias"].rearrange("b h -> (b h)").partition_broadcast(P), got_pos)
            load(sinkB[:, :], a["sinks"][0].partition_broadcast(P), got_pos)
            ws = prob[:, 0, :].rearrange("p (g s) -> p g s", g=4)
            load(ws, a["gm_w_s"][0].rearrange("g t s -> t g s"), got_spatial)
            load(bsB[:, :, :], a["gm_b_s"][0].rearrange("g t -> (g t)").partition_broadcast(P)
                 .rearrange("p (g t) -> p g t", g=4), got_spatial)
            load(w_router[:, :, 0:4], a["w_router_g"][0].rearrange("(k p) n -> p k n", p=P), got_router)
            load(w_router[:, :, 4:36], a["w_router_e"][0].rearrange("(k p) n -> p k n", p=P), got_router)
            load(w_router2[:, :, :], a["router_w_2"][0].rearrange("(k p) n -> p k n", p=P), got_router)
            load(b_router[:, 0:4], a["b_router_g"][0].partition_broadcast(P), got_router)
            load(b_router[:, 4:36], a["b_router_e"][0].partition_broadcast(P), got_router)

            def load_layer(layer):
                load(gkw2[:, :], a["gk_w2_2"][layer], got_layer)
                load(gkbB[:, :], a["gk_b_2"][layer].partition_broadcast(P), got_layer)
                load(glnB[:, :], a["gla_norm_w_2"][layer].partition_broadcast(P), got_layer)

            load_layer(0)
            na = [0]

            def group():
                act.wait_ge(a_full, na[0] + 1)
                na[0] += 1
                return 4 + (na[0] - 1) % 4

            act.wait_ge(H["cols_ready"], 1)
            act.activation(csT[:, 0, :], colA[:, 48:56], ACT.Silu)
            act.activation(csT[:, 1, :], colA[:, 72:80], ACT.Silu).then_inc(silu_c, 1)
            for g in range(2):
                bank = group()
                act.activation(guT[:, 2 * g:2 * g + 2, :], ps[:, bank, :].rearrange("p (a b) -> p a b", a=2),
                               ACT.Gelu_apprx_tanh).then_inc(a_free, 1)
            for t in range(TT):
                bank = group()
                act.activation(gv[:, t, :], ps[:, bank, :], ACT.Gelu_apprx_tanh).then_inc(a_free, 1)
            act.wait_ge(bias_pool, 2)
            for g in range(4):
                bank = group()
                act.activation(gaT[:, 2 * g:2 * g + 2, :], ps[:, bank, :].rearrange("p (a b) -> p a b", a=2),
                               ACT.Sigmoid).then_inc(a_free, 1)
            for g in range(4):
                bank = group()
                act.activation(gbT[:, 2 * g:2 * g + 2, :], ps[:, bank, :].rearrange("p (a b) -> p a b", a=2),
                               ACT.Sigmoid).then_inc(a_free, 1)
            for g in range(6):
                act.wait_ge(H["scores_ready"], g + 1)
                nh = 4 if g < 2 else 2
                st = 4 * g if g < 2 else 8 + 2 * (g - 2)
                for i in range(nh):
                    w = CH // nh
                    ins = act.activation(prob[:, g, i * w:(i + 1) * w], prob[:, g, i * w:(i + 1) * w], ACT.Exp,
                                         bias=stat[:, 16 + st + i:17 + st + i], accum_out=stat[:, 32 + st + i:33 + st + i])
                ins.then_inc(exps_done, 1)
            act.wait_ge(H["sink_ready"], 1)
            act.activation(stat[:, 64:80], stat[:, 48:64], ACT.Exp).then_inc(sink_exp, 1)

            units = [0]

            def experts(n, body):
                base = units[0]
                with act.Fori(0, n) as i:
                    for j in range(body):
                        u = i * body + (base + j)
                        act.wait_ge(gate_full, u + 1)
                        if base + j >= 2:
                            act.wait_ge(hid_ready, u - 1)
                        act.activation(silu_g[:, j % 2, :], ps[:, 4 + 2 * (j % 2), :], ACT.Silu).then_inc(silu_done, 1)
                units[0] += n * body

            act.wait_ge(H["router_logits"], 1)
            act.activation(rt[:, 96:104], rt[:, 80:88], ACT.Exp)
            act.activation(rt[:, 144:160], rt[:, 128:144], ACT.Exp).then_inc(router_exp, 1)
            act.wait_ge(H["mix_ready"], 1)
            experts(NE1 // 2, 2 * U1)
            for layer in range(2):
                for t in range(TT):
                    bank = group()
                    act.activation(sg_tok[:, t, :], ps[:, bank, :], ACT.Silu).then_inc(a_free, 1)
                act.wait_ge(H["gk_abs"], layer + 1)
                act.activation(gku, gku, ACT.Exp).then_inc(gk_e, 1)
                act.wait_ge(H["gk_exp1"], layer + 1)
                act.activation(gku, gku, ACT.Ln).then_inc(gk_l, 1)
                bank = group()
                act.activation(ebT, ps[:, bank, :].rearrange("p (a b) -> p a b", a=2), ACT.Exp).then_inc(act_step, 1)
                act.wait_ge(act_step, layer + 1)
                act.activation(enbT, ps[:, bank, :].rearrange("p (a b) -> p a b", a=2), ACT.Exp, scale=-1.0)\
                   .then_inc(a_free, 1)
                bank = group()
                act.activation(er, ps[:, bank, :].rearrange("p (a b) -> p a b", a=2), ACT.Exp).then_inc(a_free, 1)
                if layer == 0:
                    act.wait_ge(H["layer_used"], 1)
                    load_layer(1)
                    act.wait_ge(H["mix_ready"], 2)
                    for j in range(U2):
                        u = units[0] + j
                        act.wait_ge(gate_full, u + 1)
                        act.wait_ge(hid_ready, u - 1)
                        act.activation(silu_g[:, j % 2, :], ps[:, 4 + 2 * (j % 2), :], ACT.Silu)\
                           .then_inc(silu_done, 1)
                    units[0] += U2
                else:
                    act.wait_ge(H["router_logits"], 2)
                    act.activation(rt[:, 32:48], rt[:, 16:32], ACT.Exp).then_inc(router_exp, 1)
                    act.wait_ge(H["mix_ready"], 3)
                    experts(NE2 // 4, 4 * U2)

        @block.vector
        def _(dve):
            nv, nf = [0], [0]

            def step(ins, name="dve_step", wait=True):
                c = S[name]
                c.n += 1
                ins.then_inc(c.sem, 1)
                if wait:
                    dve.wait_ge(c.sem, c.n)
                return ins

            def group():
                nf[0] += 1
                dve.wait_ge(v_full, nf[0])
                nv[0] += 1
                return (nv[0] - 1) % 4

            def freed(ins):
                ins.then_inc(v_free, 1)

            def freed_wait(ins):
                ins.then_inc(v_free, 1)
                dve.wait_ge(v_free, nv[0])

            def bank2(b):
                return ps[:, b, :].rearrange("p (a b) -> p a b", a=2)

            def bank4(b):
                return ps[:, b, :].rearrange("p (a b) -> p a b", a=4)

            ones_wait = 1
            dve.wait_ge(consts_ready, 1)
            dve.wait_ge(got_pos, 64)
            posi = posf[:, 0:2, :].bitcast(I32)
            hi_r, lo_r = posi[:, 0, :], posi[:, 1, :]
            step(dve.tensor_scalar(hi_r, posrow, 16, None, ALU.arith_shift_right))
            step(dve.tensor_scalar(lo_r, posrow, 65535, None, ALU.bitwise_and))
            ci = stat[:, 0:4].bitcast(I32)
            step(dve.tensor_scalar(ci[:, 0:2], poscol[:, :], 16, None, ALU.arith_shift_right))
            step(dve.tensor_scalar(ci[:, 2:4], poscol[:, :], 65535, None, ALU.bitwise_and))
            step(dve.tensor_copy(stat[:, 4:8], ci))
            step(dve.tensor_copy(posf[:, 2, :], hi_r))
            step(dve.tensor_copy(posf[:, 3, :], lo_r))
            for t, (lo, w) in enumerate(((0, P), (P, T))):
                step(dve.tensor_scalar(dist[:, lo:lo + w], posf[:, 2, 0:w], stat[:, 4 + t:5 + t], -65536.0,
                                       ALU.subtract, ALU.mult))
                step(dve.tensor_scalar(mask_v[:, lo:lo + w], posf[:, 3, 0:w], stat[:, 6 + t:7 + t], -1.0,
                                       ALU.subtract, ALU.mult))
            step(dve.tensor_copy(relD[:, 0:HEADS], relB[:, 0:HEADS]), wait=False)
            step(dve.tensor_tensor(relD[:, HEADS:], relB[:, HEADS:], relB[:, 0:(BUCKETS - 1) * HEADS], ALU.subtract))
            dve.tensor_tensor(dist, dist, mask_v, ALU.add).then_inc(dist_ready, 1)
            dve.wait_ge(dist_ready, 1)
            step(dve.memset(bias[:, 0:6, :], 0.0))
            b = group()
            freed(dve.tensor_copy(colA[:, :], ps[:, b, 0:104]))
            b = group()
            freed_wait(dve.tensor_copy(colB[:, :], ps[:, b, 0:96]))
            step(dve.tensor_copy(stat[:, 120:121], colA[:, 0:1]), "cols_ready")
            for t in range(2):
                b = group()
                freed_wait(dve.tensor_tensor(wsT[:, 2 * t:2 * t + 2, :], ps[:, b, 0:256].rearrange("p (a b) -> p a b", a=2),
                                             triu[:, :].unsqueeze(1).to_broadcast([P, 2, P]), ALU.mult))

            def cs_broadcast(which):
                step(dve.tensor_copy(csB[:, :, :], csT[:, which, :].unsqueeze(2).to_broadcast([P, KD, P])),
                     "cs_broadcast", wait=False)

            dve.wait_ge(silu_c, 1)
            cs_broadcast(0)

            def ada(cols, one, with_bias, seq):
                base = nv[0]
                b0 = S["dve_step"].n
                with dve.Fori(0, 2) as h:
                    n = 0
                    for c in range(4):
                        bank = (base + c) % 4
                        dve.wait_ge(ring_free, h * 4 + (seq + c + 1))
                        dve.tensor_tensor(modT[:, bass.ds(h * 24 + 4 * c, 4)], ps[:, bank, 0:4],
                                          cols[:, bass.ds(h * 24 + 4 * c, 4)], ALU.add).then_inc(v_free, 1)
                        if with_bias:
                            for i in range(4):
                                bk = h * 16 + (4 * c + i)
                                dve.tensor_scalar(mask_v, dist, starts[:, bass.ds(bk, 1)], None, ALU.is_ge)\
                                   .then_inc(H["dve_step"], 1)
                                n += 1
                                dve.wait_ge(H["dve_step"], h * 32 + (b0 + n))
                                for hd in range(6):
                                    ins = dve.scalar_tensor_tensor(
                                        out=bias[:, hd, :], in0=mask_v, scalar=relD[:, bass.ds(bk * HEADS + hd, 1)],
                                        in1=bias[:, hd, :], op0=ALU.mult, op1=ALU.add)
                                ins.then_inc(H["dve_step"], 1)
                                n += 1
                                dve.wait_ge(H["dve_step"], h * 32 + (b0 + n))
                if with_bias:
                    S["dve_step"].n += 2 * n
                nv[0] += 8
                dve.wait_ge(v_free, nv[0])
                if with_bias:
                    dve.memset(stat[:, 121:122], 0.0).then_inc(bias_done, 1)
                for g in range(2):
                    for c in range(2):
                        b = group()
                        ins = dve.scalar_tensor_tensor(out=gB[:, g, c * CH:(c + 1) * CH], in0=ps[:, b, :], scalar=one,
                                                       in1=rowB[:, g, c * CH:(c + 1) * CH], op0=ALU.add, op1=ALU.add)
                        freed(ins)
                dve.wait_ge(v_free, nv[0])
                step(dve.memset(stat[:, 121:122], 0.0), "rows_used")

            dve.wait_ge(got_rows, 32)
            ada(colA, 0.0, True, 0)
            rows_got = 32

            def rstd(dst, src, mul, eps):
                n = src.shape[1]
                v, bits, t = (newton[:, 4 * i:4 * i + n] for i in range(3))
                step(dve.tensor_scalar(v, src, mul, eps, ALU.mult, ALU.add))
                step(dve.tensor_scalar(bits.bitcast(I32), v.bitcast(I32), 1, None, ALU.arith_shift_right))
                step(dve.tensor_scalar(dst.bitcast(I32), bits.bitcast(I32), -1.0, float(0x5f3759df),
                                       ALU.mult, ALU.add))
                for _ in range(4):
                    step(dve.tensor_tensor(t, dst, dst, ALU.mult))
                    step(dve.scalar_tensor_tensor(out=t, in0=t, scalar=-0.5, in1=v, op0=ALU.mult, op1=ALU.mult))
                    step(dve.scalar_tensor_tensor(out=dst, in0=t, scalar=1.5, in1=dst, op0=ALU.add, op1=ALU.mult))

            def rms(dst):
                for t in range(TT):
                    step(dve.tensor_tensor_reduce(out=tok[:, t, :], in0=x[:, t, :], in1=x[:, t, :], scale=1.0,
                                                  scalar=0.0, op0=ALU.mult, op1=ALU.add, accum_out=stat[:, 80 + t:81 + t]))
                rstd(stat[:, 82:84], stat[:, 80:82], 1.0 / D, RMS_EPS)
                for t in range(TT):
                    ins = dve.tensor_scalar(dst[:, t, :], x[:, t, :], stat[:, 82 + t:83 + t], None, ALU.mult)
                return ins

            def transposed(scale, shift):
                for t in range(TT):
                    for half in range(2):
                        b = group()
                        for j in range(4):
                            k = 4 * half + j
                            ins = dve.tensor_scalar(hT[:, k, t * P:(t + 1) * P], ps[:, b, j * P:(j + 1) * P],
                                                    scale[:, k:k + 1], shift[:, k:k + 1], ALU.mult, ALU.add)
                        freed(ins)
                dve.wait_ge(v_free, nv[0])
                step(dve.memset(stat[:, 122:123], 0.0), "hT_ready", wait=False)

            def sec(s):
                return modT[:, s * KD:(s + 1) * KD]

            dve.wait_ge(got_x, 16)
            step(rms(tok), "tokens_normed", wait=False)
            step(dve.scalar_tensor_tensor(out=scale_col[:, :], in0=sec(SC1), scalar=1.0, in1=colA[:, 56:64],
                                          op0=ALU.add, op1=ALU.mult))
            transposed(scale_col, sec(SH1))
            for g in range(2):
                b = group()
                freed(dve.tensor_copy(qT[:, 2 * g:2 * g + 2, :], bank2(b)))
            b = group()
            freed(dve.tensor_copy(kT, ps[:, b, 0:T]))
            b = group()
            freed(dve.tensor_copy(v_tok, ps[:, b, 0:T].rearrange("p (a b) -> p a b", a=2)))
            dve.wait_ge(v_free, nv[0])
            step(dve.memset(stat[:, 123:124], 0.0), "qkv_ready", wait=False)

            def layer_norm(w, v, g, b, eps):
                m = w // 512
                for t in range(TT):
                    for i in range(m):
                        at = 84 + 12 * t + 6 * i
                        ins = dve.bn_stats(stat[:, at:at + 6], v[:, t, i * 512:(i + 1) * 512])
                step(ins)
                for t in range(TT):
                    ins = dve.bn_aggr(stat[:, 108 + 2 * t:110 + 2 * t], stat[:, 84 + 12 * t:84 + 12 * t + 6 * m]
                                      .rearrange("p (a b) -> p a b", b=6))
                step(ins)
                step(dve.tensor_copy(stat[:, 80:82], stat[:, 108:112].rearrange("p (a b) -> p a b", b=2)[:, :, 1]))
                rstd(stat[:, 82:84], stat[:, 80:82], 1.0, eps)
                for t in range(TT):
                    step(dve.tensor_scalar(v[:, t, :], v[:, t, :], stat[:, 108 + 2 * t:109 + 2 * t],
                                           stat[:, 82 + t:83 + t], ALU.subtract, ALU.mult))
                    step(dve.tensor_tensor(v[:, t, :], v[:, t, :], g, ALU.mult))
                    step(dve.tensor_tensor(v[:, t, :], v[:, t, :], b, ALU.add))

            dve.wait_ge(a_free, 4)
            rows_got += 32
            dve.wait_ge(got_rows, rows_got)
            layer_norm(512, gv, rowB[:, 0, 0:512], rowB[:, 0, 512:1024], RMS_EPS)
            step(dve.memset(stat[:, 124:125], 0.0), "vn_ready")
            step(dve.memset(stat[:, 121:122], 0.0), "rows_used")
            dve.wait_ge(got_spatial, 32)
            for t in range(TT):
                b = group()
                step(dve.tensor_tensor(tok[:, t, 0:512].rearrange("p (a b) -> p a b", a=4), bank4(b), bsB[:, :, :], ALU.add))
                freed(dve.tensor_tensor(guT[:, :, t * P:(t + 1) * P], guT[:, :, t * P:(t + 1) * P],
                                        tok[:, t, 0:512].rearrange("p (a b) -> p a b", a=4), ALU.mult))
            dve.wait_ge(v_free, nv[0])
            step(dve.memset(stat[:, 125:126], 0.0), "yb_ready", wait=False)
            dve.wait_ge(bias_pool, 2)
            for g in range(6):
                nh = 4 if g < 2 else 2
                w = CH // nh
                h0 = 4 * g if g < 2 else 2 * (g - 2)
                st = h0 if g < 2 else 8 + h0
                bv = bias[:, h0:h0 + nh, 0:P] if g < 2 else bias[:, h0:h0 + nh, P:384]
                b = group()
                pg = prob[:, g, :].rearrange("p (a b) -> p a b", a=nh)
                freed_wait(dve.scalar_tensor_tensor(out=pg, in0=ps[:, b, :].rearrange("p (a b) -> p a b", a=nh),
                                                    scalar=ATTN_SCALE, in1=bv, op0=ALU.mult, op1=ALU.add))
                step(dve.tensor_reduce(stat[:, st:st + nh], pg, AX, ALU.max))
                step(dve.tensor_tensor(stat[:, st:st + nh], stat[:, st:st + nh], sinkB[:, h0:h0 + nh], ALU.max))
                step(dve.tensor_scalar(stat[:, 16 + st:16 + st + nh], stat[:, st:st + nh], -1.0, None, ALU.mult),
                     "scores_ready")
            for blk in range(2):
                ins = dve.tensor_tensor(stat[:, 48 + 8 * blk:56 + 8 * blk], sinkB[:, :],
                                        stat[:, 16 + 8 * blk:24 + 8 * blk], ALU.add)
            step(ins, "sink_ready")
            dve.wait_ge(sink_exp, 1)
            step(dve.tensor_tensor(stat[:, 32:48], stat[:, 32:48], stat[:, 64:80], ALU.add))
            step(dve.reciprocal(stat[:, 32:48], stat[:, 32:48]))
            for g in range(6):
                nh = 4 if g < 2 else 2
                st = 4 * g if g < 2 else 8 + 2 * (g - 2)
                pg = prob[:, g, :].rearrange("p (a b) -> p a b", a=nh)
                step(dve.tensor_tensor(pg, pg, stat[:, 32 + st:32 + st + nh].unsqueeze(2)
                                       .to_broadcast([P, nh, CH // nh]), ALU.mult), "probs_ready", wait=False)
            for g in range(6):
                b = group()
                freed_wait(dve.tensor_copy(pT[:, g, :], ps[:, b, :]))
                step(dve.memset(stat[:, 126:127], 0.0), "pT_ready", wait=False)
            for blk in range(2):
                b = group()
                freed(dve.tensor_copy(yaT[:, :, blk * P:(blk + 1) * P], bank4(b)))
            dve.wait_ge(v_free, nv[0])
            step(dve.memset(stat[:, 120:121], 0.0), "ya_ready", wait=False)
            dve.wait_ge(a_free, 12)
            for g in range(4):
                b = group()
                freed_wait(dve.tensor_tensor(gaT[:, 2 * g:2 * g + 2, :], gaT[:, 2 * g:2 * g + 2, :], bank2(b), ALU.mult))
            for g in range(4):
                b = group()
                freed_wait(dve.tensor_tensor(gbT[:, 2 * g:2 * g + 2, :], gbT[:, 2 * g:2 * g + 2, :], bank2(b), ALU.mult))
                ins = dve.tensor_tensor(gaT[:, 2 * g:2 * g + 2, :], gaT[:, 2 * g:2 * g + 2, :],
                                        gbT[:, 2 * g:2 * g + 2, :], ALU.add)
                step(ins, "merged_ready")

            def gated_sum(g, keep, cuts):
                for c0, c1 in cuts:
                    for t in range(TT):
                        b = group()
                        freed_wait(dve.tensor_tensor(tok[:, t, c0:c1], ps[:, b, 0:c1 - c0], gB[:, g, c0:c1], ALU.mult))
                        step(dve.scalar_tensor_tensor(out=x[:, t, c0:c1], in0=x[:, t, c0:c1], scalar=keep,
                                                      in1=tok[:, t, c0:c1], op0=ALU.mult, op1=ALU.add))

            gated_sum(0, 1.0, [(0, 512), (512, 1024)])
            step(rms(tok), "tokens_normed", wait=False)
            step(dve.scalar_tensor_tensor(out=scale_col[:, :], in0=sec(SC2), scalar=1.0, in1=colA[:, 64:72],
                                          op0=ALU.add, op1=ALU.mult))
            transposed(scale_col, sec(SH2))

            def first_max(dst, src, val, n, scratch, g):
                step(dve.tensor_reduce(val, src, AX, ALU.max))
                step(dve.tensor_tensor(dst, src, val.unsqueeze(2).to_broadcast([P, g, n]), ALU.is_equal))
                step(dve.tensor_tensor(dst, dst, rev[:, 8 - n:8].unsqueeze(1).to_broadcast([P, g, n]), ALU.mult))
                step(dve.tensor_reduce(scratch, dst, AX, ALU.max))
                step(dve.tensor_tensor(dst, dst, scratch.unsqueeze(2).to_broadcast([P, g, n]), ALU.is_equal))

            def r2(lo, n):
                return rt[:, lo:lo + 2 * n].rearrange("p (a b) -> p a b", a=2)

            b = group()
            logits = r2(0, 36)
            dve.wait_ge(got_router, 80)
            freed_wait(dve.tensor_tensor(logits, ps[:, b, 0:72].rearrange("p (a b) -> p a b", a=2),
                                         b_router[:, :].unsqueeze(1).to_broadcast([P, 2, 36]), ALU.add))
            sc2 = rt[:, 300:302]
            gmax = rt[:, 302:304]
            first_max(r2(72, 4), logits[:, :, 0:4], gmax, 4, sc2, 2)
            step(dve.tensor_tensor(r2(80, 4), logits[:, :, 0:4], gmax.unsqueeze(2).to_broadcast([P, 2, 4]), ALU.subtract))
            chosen = r2(112, 8)
            step(dve.tensor_tensor(chosen, logits[:, :, 4:12], r2(72, 4)[:, :, 0:1].to_broadcast([P, 2, 8]), ALU.mult))
            for g in range(1, NG):
                step(dve.tensor_tensor(r2(192, 8), logits[:, :, 4 + 8 * g:12 + 8 * g],
                                       r2(72, 4)[:, :, g:g + 1].to_broadcast([P, 2, 8]), ALU.mult))
                step(dve.tensor_tensor(chosen, chosen, r2(192, 8), ALU.add))
            emax = rt[:, 304:306]
            step(dve.tensor_reduce(emax, chosen, AX, ALU.max))
            step(dve.tensor_tensor(r2(128, 8), chosen, emax.unsqueeze(2).to_broadcast([P, 2, 8]), ALU.subtract),
                 "router_logits")
            dve.wait_ge(router_exp, 1)
            pg_ = rt[:, 306:308]
            step(dve.tensor_reduce(pg_, r2(96, 4), AX, ALU.add))
            step(dve.reciprocal(pg_, pg_))
            esum = rt[:, 308:310]
            step(dve.tensor_reduce(esum, r2(144, 8), AX, ALU.add))
            step(dve.reciprocal(esum, esum))
            pr = r2(144, 8)
            step(dve.tensor_tensor(pr, pr, esum.unsqueeze(2).to_broadcast([P, 2, 8]), ALU.mult))

            def top2(pr, oh1, oh2, tmp, w1, w2, sc):
                first_max(oh1, pr, w1, 8, sc, 2)
                step(dve.scalar_tensor_tensor(out=tmp, in0=oh1, scalar=-3e38, in1=pr, op0=ALU.mult, op1=ALU.add))
                first_max(oh2, tmp, w2, 8, sc, 2)

            w1, w2 = rt[:, 310:312], rt[:, 312:314]
            top2(pr, r2(160, 8), r2(176, 8), r2(192, 8), w1, w2, sc2)
            den = rt[:, 314:316]
            step(dve.tensor_tensor(den, w1, w2, ALU.add))
            step(dve.reciprocal(den, den))
            step(dve.tensor_tensor(w1, w1, den, ALU.mult))
            step(dve.tensor_tensor(w2, w2, den, ALU.mult))
            step(dve.tensor_tensor(w1, w1, pg_, ALU.mult))
            step(dve.tensor_tensor(w2, w2, pg_, ALU.mult))
            step(dve.tensor_tensor(r2(160, 8), r2(160, 8), w1.unsqueeze(2).to_broadcast([P, 2, 8]), ALU.mult))
            step(dve.tensor_tensor(r2(176, 8), r2(176, 8), w2.unsqueeze(2).to_broadcast([P, 2, 8]), ALU.mult))
            step(dve.tensor_tensor(r2(160, 8), r2(160, 8), r2(176, 8), ALU.add))
            for g in range(NG):
                step(dve.tensor_tensor(combine[:, :, 8 * g:8 * g + 8], r2(160, 8),
                                       r2(72, 4)[:, :, g:g + 1].to_broadcast([P, 2, 8]), ALU.mult))
            step(dve.memset(tok[:, :, :], 0.0), "mix_ready")
            ub, eb = [0], [0]

            def unit(u, j, e, last, weight, seq, first=False):
                dve.wait_ge(silu_done, u + 1)
                dve.wait_ge(up_full, u + 1)
                if not first:
                    dve.wait_ge(ring_free, seq - 1)
                dve.tensor_tensor(hid[:, j % 2, :], silu_g[:, j % 2, :], ps[:, 5 + 2 * (j % 2), :], ALU.mult)\
                   .then_inc(hid_ready, 1)
                if last:
                    dve.wait_ge(ring_free, seq + 1)
                    for t in range(TT):
                        for half in range(2):
                            dst = tok[:, t, half * CH:(half + 1) * CH]
                            if weight is None:
                                ins = dve.tensor_copy(dst, ps[:, 2 * t + half, :])
                            else:
                                ins = dve.scalar_tensor_tensor(out=dst, in0=ps[:, 2 * t + half, :], scalar=weight(t),
                                                               in1=dst, op0=ALU.mult, op1=ALU.add)
                    ins.then_inc(y_free, 1)
                    dve.wait_ge(y_free, e + 1)

            def experts(n, body_e, units, seq):
                body = body_e * units
                with dve.Fori(0, n) as i:
                    for j in range(body):
                        e = i * body_e + j // units
                        unit(i * body + (ub[0] + j), j, e + eb[0], j % units == units - 1,
                             lambda t: combine[:, t, bass.ds(e, 1)], i * body + (seq + j), first=ub[0] + j < 2)
                ub[0] += n * body
                eb[0] += n * body_e

            experts(NE1 // 2, 2, U1, MOE1_SEQ)

            def gated_ffn(keep):
                for t in range(TT):
                    step(dve.tensor_tensor(tok[:, t, :], tok[:, t, :], gB[:, 1, :], ALU.mult))
                    step(dve.scalar_tensor_tensor(out=x[:, t, :], in0=x[:, t, :], scalar=keep, in1=tok[:, t, :],
                                                  op0=ALU.mult, op1=ALU.add))

            gated_ffn(1.0)
            rms(x)
            step(dve.memset(stat[:, 126:127], 0.0))
            rows_got += 16
            dve.wait_ge(got_rows, rows_got)
            for t in range(TT):
                step(dve.tensor_tensor(x[:, t, :], x[:, t, :], rowB[:, 0, :], ALU.mult))
            step(dve.memset(stat[:, 121:122], 0.0), "rows_used")
            dve.wait_ge(v_free, nv[0])
            for layer in range(2):
                cs_broadcast(1) if layer == 0 else None
                rows_got += 32
                dve.wait_ge(got_rows, rows_got)
                ada(colB[:, layer * 48:layer * 48 + 48], 1.0, False, ADA2_SEQ[layer])
                step(dve.tensor_scalar(scale_col[:, :], sec(SC1), 1.0, None, ALU.add), "tokens_normed")
                transposed(scale_col, sec(SH1))
                for g in range(2):
                    b = group()
                    freed(dve.tensor_copy(cbT[:, 2 * g:2 * g + 2, :], bank2(b)))
                for g in range(2):
                    b = group()
                    freed_wait(dve.tensor_copy(ccT[:, 2 * g:2 * g + 2, :], bank2(b)))
                step(dve.memset(zT[:, :, 0:2], 0.0))
                for g in range(2):
                    b = group()
                    freed_wait(dve.tensor_tensor(zT[:, 2 * g:2 * g + 2, 2:T + 2], ccT[:, 2 * g:2 * g + 2, :], bank2(b), ALU.mult))
                for dst in (q2T, k2T, k_tok):
                    b = group()
                    freed_wait(dve.tensor_copy(dst, bank2(b)))
                for t in range(TT):
                    b = group()
                    freed_wait(dve.tensor_copy(v2[:, t, :], ps[:, b, :]))
                b = group()
                freed_wait(dve.tensor_copy(glT, ps[0:16, b, 0:T]))
                step(dve.memset(stat[:, 124:125], 0.0), "glow_ready", wait=False)
                for c in range(4):
                    for tap in range(3):
                        w = colA[:, 80 + layer * 12 + tap * 4 + c:81 + layer * 12 + tap * 4 + c]
                        src = zT[:, c, tap:tap + T]
                        if tap == 0:
                            step(dve.tensor_scalar(conv[:, c, :], src, w, None, ALU.mult))
                        else:
                            step(dve.scalar_tensor_tensor(out=conv[:, c, :], in0=src, scalar=w, in1=conv[:, c, :],
                                                          op0=ALU.mult, op1=ALU.add))
                step(dve.tensor_tensor(cbT, cbT, conv, ALU.mult))
                b = group()
                dve.wait_ge(got_layer, 48 * (layer + 1))
                freed_wait(dve.tensor_tensor(gk, bank2(b), gkbB[:, :].unsqueeze(1).to_broadcast([P, 2, T]), ALU.add))
                step(dve.tensor_scalar(gkt, gk, -1.0, None, ALU.mult))
                step(dve.tensor_tensor(gku, gk, gkt, ALU.min), "gk_abs")
                dve.wait_ge(gk_e, layer + 1)
                step(dve.tensor_scalar(gku, gku, 1.0, None, ALU.add), "gk_exp1")
                dve.wait_ge(gk_l, layer + 1)
                step(dve.scalar_tensor_tensor(out=gk, in0=gk, scalar=0.0, in1=gku, op0=ALU.min, op1=ALU.subtract))
                step(dve.tensor_scalar(gk, gk, 1.0 / GK_DIV, GK_MIN, ALU.mult, ALU.max), "gk_ready")
                dve.wait_ge(a_free, 12 + 4 * (layer + 1))
                step(dve.scalar_tensor_tensor(out=q2T, in0=q2T, scalar=DK ** -0.5, in1=ebT, op0=ALU.mult, op1=ALU.mult),
                     wait=False)
                step(dve.tensor_tensor(k2T, k2T, enbT, ALU.mult), wait=False)
                step(dve.tensor_tensor(k_tok, k_tok, er, ALU.mult), "gla_in")
                for par in range(2):
                    b = group()
                    freed_wait(dve.tensor_tensor(scT[:, par, :, :], bank4(b),
                                                 chunk_triu[:, :].unsqueeze(1).to_broadcast([P, 4, P]), ALU.mult))
                step(dve.memset(stat[:, 125:126], 0.0), "gla_scores", wait=False)
                for c in range(3):
                    b = group()
                    if c == 0:
                        freed_wait(dve.tensor_copy(state[:, 0, :, :], ps[:, b, 0:2 * DV].rearrange("p (a b) -> p a b", a=2)))
                    else:
                        for f in range(2):
                            ins = dve.scalar_tensor_tensor(out=state[:, c, f, :], in0=state[:, c - 1, f, :],
                                                           scalar=ebT[:, f, c * CK + CK - 1:c * CK + CK],
                                                           in1=ps[:, b, f * DV:(f + 1) * DV], op0=ALU.mult, op1=ALU.add)
                        freed_wait(ins)
                step(dve.memset(stat[:, 126:127], 0.0), "states_ready", wait=False)
                dve.wait_ge(a_free, 12 + 4 * (layer + 1))
                for par in range(2):
                    b = group()
                    freed_wait(dve.tensor_copy(
                        o_tok.rearrange("p t (f a v) -> p t f a v", a=2, v=DV)[:, :, :, par, :],
                        ps[:, b, :].rearrange("p (t f v) -> p t f v", t=2, f=2)))
                for t in range(TT):
                    o4 = o_tok[:, t, :].rearrange("p (a b) -> p a b", a=4)
                    t4 = tok[:, t, 0:512].rearrange("p (a b) -> p a b", a=4)
                    step(dve.tensor_tensor(t4, o4, o4, ALU.mult))
                    step(dve.tensor_reduce(stat[:, 0:4], t4, AX, ALU.add))
                    rstd(stat[:, 4:8], stat[:, 0:4], 1.0 / DV, RMS_EPS)
                    step(dve.tensor_tensor(o4, o4, stat[:, 4:8].unsqueeze(2).to_broadcast([P, 4, DV]), ALU.mult))
                    step(dve.tensor_tensor(o4, o4, glnB[:, :].unsqueeze(1).to_broadcast([P, 4, DV]), ALU.mult))
                    step(dve.tensor_tensor(o_tok[:, t, :], o_tok[:, t, :], sg_tok[:, t, :], ALU.mult), "o_normed")
                step(dve.memset(stat[:, 121:122], 0.0), "layer_used")
                for t in range(TT):
                    b = group()
                    freed_wait(dve.tensor_copy(ygT[:, :, t * P:(t + 1) * P], bank4(b)))
                step(dve.memset(stat[:, 120:121], 0.0), "ya_ready", wait=False)
                gated_sum(0, ALPHA, W_OUT_CUTS[layer])

                def norm_x():
                    nonlocal rows_got
                    rows_got += 32
                    dve.wait_ge(got_rows, rows_got)
                    layer_norm(D, x, rowB[:, 0, :], rowB[:, 1, :], LN_EPS)

                norm_x()
                step(dve.memset(stat[:, 121:122], 0.0), "rows_used")
                step(dve.tensor_scalar(scale_col[:, :], sec(SC2), 1.0, None, ALU.add), "tokens_normed")
                transposed(scale_col, sec(SH2))
                if layer == 0:
                    step(dve.memset(stat[:, 124:125], 0.0), "mix_ready")
                    for j in range(U2):
                        unit(ub[0] + j, j, eb[0], j == U2 - 1, None, FFN_SEQ + j)
                    ub[0] += U2
                    eb[0] += 1
                else:
                    b = group()
                    freed_wait(dve.tensor_copy(r2(0, 8), ps[:, b, 0:16].rearrange("p (a b) -> p a b", a=2)))
                    m1, m2 = rt[:, 310:312], rt[:, 312:314]
                    top2(r2(0, 8), r2(160, 8), r2(176, 8), r2(192, 8), m1, m2, sc2)
                    step(dve.tensor_tensor(rt[:, 16:18], m2, m1, ALU.subtract), wait=False)
                    step(dve.memset(rt[:, 18:32], 0.0), "router_logits")
                    dve.wait_ge(router_exp, 2)
                    e2 = rt[:, 32:34]
                    step(dve.tensor_scalar(w1, e2, 1.0, None, ALU.add))
                    step(dve.reciprocal(w1, w1))
                    step(dve.tensor_tensor(w2, e2, w1, ALU.mult))
                    step(dve.tensor_tensor(r2(160, 8), r2(160, 8), w1.unsqueeze(2).to_broadcast([P, 2, 8]), ALU.mult))
                    step(dve.tensor_tensor(r2(176, 8), r2(176, 8), w2.unsqueeze(2).to_broadcast([P, 2, 8]), ALU.mult))
                    step(dve.tensor_tensor(combine[:, :, 0:8], r2(160, 8), r2(176, 8), ALU.add))
                    step(dve.memset(tok[:, :, :], 0.0), "mix_ready")
                    experts(NE2 // 4, 4, U2, MOE2_SEQ)
                gated_ffn(ALPHA)
                norm_x()
                if layer == 0:
                    step(dve.memset(stat[:, 121:122], 0.0), "rows_used")
                else:
                    step(dve.memset(stat[:, 121:122], 0.0), "x_ready")

        @block.tensor
        def _(pe):
            r = Ring()
            nv, na = [0], [0]
            owed = [False]

            def mm(*args, **kw):
                ins = pe.matmul(*args, **kw)
                if owed[0]:
                    ins.then_inc(ring_free, 1)
                    owed[0] = False
                    return None
                return ins

            def tr(*args):
                ins = pe.transpose(*args)
                if owed[0]:
                    ins.then_inc(ring_free, 1)
                    owed[0] = False
                    return None
                return ins

            def free():
                assert not owed[0]
                owed[0] = True

            def gv_():
                if nv[0] >= 4:
                    pe.wait_ge(v_free, nv[0] - 3)
                nv[0] += 1
                return (nv[0] - 1) % 4

            def ga_():
                if na[0] >= 4:
                    pe.wait_ge(a_free, na[0] - 3)
                na[0] += 1
                return 4 + (na[0] - 1) % 4

            def take(dmas=1):
                s, full, _ = r.take(dmas)
                pe.wait_ge(ring_full[s], full)
                return s

            def transposes(src, n, rows_, bank, rid=P):
                for j in range(n):
                    last = tr(ps[0:P, bank, j * rows_:(j + 1) * rows_], src(j), ident[0:rid, 0:rid])
                return last

            pe.wait_ge(consts_ready, 1)
            pe.wait_ge(got_vec, 112)
            pe.transpose(ps[:, gv_(), 0:104], vecA[:, :], ident[0:104, 0:104]).then_inc(v_full, 1)
            pe.transpose(ps[:, gv_(), 0:96], vecB[:, :], ident[0:96, 0:96]).then_inc(v_full, 1)
            pe.wait_ge(got_spatial, 32)
            for t in range(2):
                transposes(lambda j: prob[:, 0, (2 * t + j) * P:(2 * t + j + 1) * P], 2, P, gv_()).then_inc(v_full, 1)

            csn = [0]

            def ada(which):
                base, vb = r.seq, nv[0]
                assert base % SLOTS == 0 and not owed[0]
                loads = list(r.loads)
                with pe.Fori(0, 2) as h:
                    for c in range(4):
                        pe.wait_ge(ring_full[c], h * 16 + (loads[c] + 16))
                        bank = (vb + c) % 4
                        pe.wait_ge(v_free, h * 4 + (vb + c - 3))
                        for f in range(4):
                            for k in range(KD):
                                last = mm(ps[:, bank, f:f + 1], slot(c, KD, CH)[:, k, f * P:(f + 1) * P],
                                                 csT[:, which, k:k + 1], start=(k == 0), stop=(k == KD - 1))
                        last.then_inc(ring_free, 1)
                nv[0] += 8
                for _ in range(8):
                    r.take(1)
                for c in range(4):
                    s = take()
                    bank = gv_()
                    for k in range(KD):
                        last = mm(ps[:, bank, :], csB[:, k, :], slot(s, KD, CH)[:, k, :],
                                         start=(k == 0), stop=(k == KD - 1))
                    last.then_inc(v_full, 1)
                    free()

            def token_transposes(src):
                for t in range(TT):
                    for half in range(2):
                        transposes(lambda j: src[:, t, (4 * half + j) * P:(4 * half + j + 1) * P], 4, P, gv_())\
                            .then_inc(v_full, 1)

            def feature_major(w, rhs, tiles, bank, cols=lambda f: f * P, kt=KD, m=P):
                for i, f in enumerate(tiles):
                    for k in range(kt):
                        last = mm(ps[0:m, bank, i * T:(i + 1) * T], w[:, k, cols(f):cols(f) + m], rhs(k),
                                         start=(k == 0), stop=(k == kt - 1))
                return last

            def token_major(lhs, w, t, c0, c1, bank, at=0, kt=KD):
                for k in range(kt):
                    last = mm(ps[:, bank, at:at + c1 - c0], lhs(k, t), w[:, k, c0:c1],
                                     start=(k == 0), stop=(k == kt - 1))
                return last

            def h_rhs(k):
                return hT[:, k, :]

            def h_lhs(k, t):
                return hT[:, k, t * P:(t + 1) * P]

            pe.wait_ge(silu_c, 1)
            pe.wait_ge(H["cs_broadcast"], 1)
            ada(0)
            pe.wait_ge(H["tokens_normed"], 1)
            token_transposes(tok)
            pe.wait_ge(H["hT_ready"], 1)
            s = take(10)
            w = slot(s, KD, 768)
            for g in range(2):
                feature_major(w, h_rhs, (2 * g, 2 * g + 1), gv_()).then_inc(v_full, 1)
            feature_major(w, h_rhs, (4,), gv_()).then_inc(v_full, 1)
            bank = gv_()
            token_major(h_lhs, w, 0, 640, 768, bank)
            token_major(h_lhs, w, 1, 640, 768, bank, at=P).then_inc(v_full, 1)
            free()
            s = take()
            for g in range(2):
                feature_major(slot(s, KD, CH), h_rhs, (2 * g, 2 * g + 1), ga_()).then_inc(a_full, 1)
            free()
            s = take()
            for t in range(TT):
                token_major(h_lhs, slot(s, KD, CH), t, 0, CH, ga_()).then_inc(a_full, 1)
            free()
            for c in range(4):
                s = take()
                for g in range(2):
                    feature_major(slot(s, KD, CH), h_rhs, (2 * g, 2 * g + 1), ga_()).then_inc(a_full, 1)
                free()
            pe.wait_ge(H["vn_ready"], 1)
            for t in range(TT):
                bank = gv_()
                for g in range(4):
                    last = mm(ps[:, bank, g * P:(g + 1) * P], gv[:, t, g * P:(g + 1) * P], wsT[:, g, :],
                                     start=True, stop=True)
                last.then_inc(v_full, 1)
            pe.wait_ge(H["qkv_ready"], 1)
            for g in range(6):
                nh = 4 if g < 2 else 2
                h0 = 4 * g if g < 2 else 2 * (g - 2)
                bank = gv_()
                for i in range(nh):
                    hd = h0 + i
                    base, j = HD * (hd // GROUP_HEADS), hd % GROUP_HEADS
                    q0, keys = (0, P) if g < 2 else (P, T)
                    last = mm(ps[:, bank, i * keys:(i + 1) * keys], qT[base:base + HD, j, q0:q0 + P],
                                     kT[base:base + HD, 0:keys], start=True, stop=True)
                last.then_inc(v_full, 1)
            for g in range(6):
                pe.wait_ge(H["probs_ready"], g + 1)
                transposes(lambda j: prob[:, g, j * P:(j + 1) * P], 4, P, gv_()).then_inc(v_full, 1)
            for blk in range(2):
                pe.wait_ge(H["pT_ready"], 2 + 4 * blk)
                bank = gv_()
                for hd in range(HEADS):
                    base, kv = HD * (hd % 2), hd // GROUP_HEADS
                    dst = ps[base:base + HD, bank, (hd // 2) * P:(hd // 2 + 1) * P]
                    if blk == 0:
                        last = mm(dst, v_tok[:, 0, kv * HD:(kv + 1) * HD],
                                         pT[:, hd // 4, (hd % 4) * P:(hd % 4 + 1) * P], start=True, stop=True)
                    else:
                        for kt in range(2):
                            at = (2 * (hd % 2) + kt) * P
                            last = mm(dst, v_tok[:, kt, kv * HD:(kv + 1) * HD],
                                             pT[:, 2 + hd // 2, at:at + P], start=(kt == 0), stop=(kt == 1))
                last.then_inc(v_full, 1)
            pe.wait_ge(H["ya_ready"], 1)
            for c in range(2):
                s = take()
                for g in range(2):
                    feature_major(slot(s, 4, CH), lambda k: yaT[:, k, :], (2 * g, 2 * g + 1), gv_(), kt=4)\
                        .then_inc(v_full, 1)
                free()
            pe.wait_ge(H["yb_ready"], 1)
            s = take()
            for g in range(4):
                feature_major(slot(s, 4, D), lambda k: guT[:, k, :], (2 * g, 2 * g + 1), gv_(), kt=4).then_inc(v_full, 1)
            free()
            pe.wait_ge(H["merged_ready"], 4)
            for c in range(2):
                s = take()
                for t in range(TT):
                    token_major(lambda k, t: gaT[:, k, t * P:(t + 1) * P], slot(s, KD, CH), t, 0, CH, gv_())\
                        .then_inc(v_full, 1)
                free()
            pe.wait_ge(H["tokens_normed"], 2)
            token_transposes(tok)
            pe.wait_ge(H["hT_ready"], 2)
            pe.wait_ge(got_router, 80)

            def router(w, n):
                bank = gv_()
                for t in range(TT):
                    last = token_major(h_lhs, w, t, 0, n, bank, at=t * n)
                last.then_inc(v_full, 1)

            router(w_router, 36)

            ub, eb = [0], [0]

            def unit_in(s, u, full, j, first=False):
                pe.wait_ge(ring_full[s], full)
                if not first:
                    pe.wait_ge(hid_ready, u - 1)
                b = 4 + 2 * (j % 2)
                feature_major(slot_gate(s), h_rhs, (0, 1), b).then_inc(gate_full, 1)
                feature_major(slot_up(s), h_rhs, (0, 1), b + 1).then_inc(up_full, 1)

            def unit_down(s, u, j, e, opens, closes, first):
                pe.wait_ge(hid_ready, u + 1)
                if opens and not first:
                    pe.wait_ge(y_free, e)
                for t in range(TT):
                    for half in range(2):
                        for f in range(2):
                            last = mm(ps[:, 2 * t + half, :], hid[:, j % 2, f * T + t * P:f * T + (t + 1) * P],
                                             slot_down(s)[:, f, half * CH:(half + 1) * CH],
                                             start=(opens and f == 0), stop=(closes and f == 1))
                last.then_inc(ring_free, 1)

            def experts(n, body_e, units):
                body = body_e * units
                at = r.loop(n, body)
                assert not owed[0]
                pe.wait_ge(v_free, nv[0])
                pe.wait_ge(a_free, na[0])
                with pe.Fori(0, n) as i:
                    def down(j):
                        k = j % units
                        unit_down(j % SLOTS, i * body + (ub[0] + j), j, i * body_e + (eb[0] + j // units),
                                  k == 0, k == units - 1, eb[0] + j // units == 0)
                    for j in range(body):
                        s, full, _ = at(i, j)
                        unit_in(s, i * body + (ub[0] + j), full, j, first=ub[0] + j < 2)
                        if j:
                            down(j - 1)
                    down(body - 1)
                ub[0] += n * body
                eb[0] += n * body_e

            pe.wait_ge(H["mix_ready"], 1)
            experts(NE1 // 2, 2, U1)
            for layer in range(2):
                pe.wait_ge(H["rows_used"], 3 + 3 * layer)
                if layer == 0:
                    pe.wait_ge(H["cs_broadcast"], 2)
                pe.wait_ge(y_free, eb[0])
                ada(1)
                pe.wait_ge(H["tokens_normed"], 3 + 2 * layer)
                token_transposes(x)
                pe.wait_ge(H["hT_ready"], 3 + 2 * layer)
                for c in range(3):
                    s = take()
                    for g in range(2):
                        feature_major(slot(s, KD, CH), h_rhs, (2 * g, 2 * g + 1), gv_()).then_inc(v_full, 1)
                    free()
                s = take()
                w = slot(s, KD, CH)
                for g in range(2):
                    feature_major(w, h_rhs, (2 * g, 2 * g + 1), gv_()).then_inc(v_full, 1)
                bank = gv_()
                token_major(h_lhs, w, 0, T, 2 * T, bank)
                token_major(h_lhs, w, 1, T, 2 * T, bank, at=T).then_inc(v_full, 1)
                free()
                s = take()
                for t in range(TT):
                    token_major(h_lhs, slot(s, KD, CH), t, 0, CH, gv_()).then_inc(v_full, 1)
                free()
                s = take()
                w = slot(s, KD, 528)
                for t in range(TT):
                    token_major(h_lhs, w, t, 0, CH, ga_()).then_inc(a_full, 1)
                feature_major(w, h_rhs, (0,), gv_(), cols=lambda f: CH, m=16).then_inc(v_full, 1)
                free()
                pe.wait_ge(H["glow_ready"], layer + 1)
                pe.wait_ge(got_layer, 48 * (layer + 1))
                bank = gv_()
                for t in range(TT):
                    last = mm(ps[:, bank, t * T:(t + 1) * T], glT[:, t * P:(t + 1) * P], gkw2[:, :],
                                     start=True, stop=True)
                last.then_inc(v_full, 1)
                pe.wait_ge(H["gk_ready"], layer + 1)
                bank = ga_()
                for f in range(2):
                    for t in range(TT):
                        last = mm(ps[:, bank, f * T + t * P:f * T + (t + 1) * P], gk[:, t, f * P:(f + 1) * P],
                                         chunk_triu[:, :], start=True, stop=True)
                last.then_inc(a_full, 1)
                bank = ga_()
                for t in range(TT):
                    last = mm(ps[:, bank, t * T:(t + 1) * T], chunk_tril[:, :], gk[:, t, :], start=True, stop=True)
                last.then_inc(a_full, 1)
                pe.wait_ge(H["gla_in"], layer + 1)
                for par in range(2):
                    base, bank = DK * par, gv_()
                    for t in range(TT):
                        for f in range(2):
                            at = (2 * t + f) * P
                            last = mm(ps[:, bank, at:at + P], k2T[base:base + DK, f, t * P:(t + 1) * P],
                                             q2T[base:base + DK, f, t * P:(t + 1) * P], start=True, stop=True)
                    last.then_inc(v_full, 1)
                for c in range(3):
                    bank, rb, t = gv_(), CK * (c % 2), c // 2
                    for hd in range(GH):
                        ob, f = DK * (hd % 2), hd // 2
                        last = mm(ps[ob:ob + DK, bank, f * DV:(f + 1) * DV],
                                         k_tok[rb:rb + CK, t, hd * DK:(hd + 1) * DK],
                                         v2[rb:rb + CK, t, hd * DV:(hd + 1) * DV], start=True, stop=True)
                    last.then_inc(v_full, 1)
                pe.wait_ge(H["gla_scores"], layer + 1)
                pe.wait_ge(H["states_ready"], layer + 1)
                for par in range(2):
                    base, bank = DK * par, gv_()
                    for t in range(TT):
                        for f in range(2):
                            at = (2 * t + f) * P
                            hd = 2 * f + par
                            last = mm(ps[:, bank, at:at + DV], scT[:, par, 2 * t + f, :],
                                      v2[:, t, hd * DV:(hd + 1) * DV], start=True, stop=False,
                                      skip_group_check=True)
                            for c in (2 * t, 2 * t + 1):
                                if c == 0:
                                    continue
                                ob = CK * (c % 2)
                                last = mm(ps[ob:ob + CK, bank, at:at + DV],
                                          q2T[base:base + DK, f, c * CK:(c + 1) * CK],
                                          state[base:base + DK, c - 1, f, :], start=False, stop=True,
                                          skip_group_check=True)
                    last.then_inc(v_full, 1)
                for t in range(TT):
                    pe.wait_ge(H["o_normed"], 2 * layer + t + 1)
                    transposes(lambda j: o_tok[:, t, j * P:(j + 1) * P], 4, P, gv_()).then_inc(v_full, 1)
                pe.wait_ge(H["ya_ready"], 2 + layer)
                for c0, c1 in W_OUT_CUTS[layer]:
                    s = take()
                    for t in range(TT):
                        token_major(lambda k, t: (cbT if k < 4 else ygT)[:, k % 4, t * P:(t + 1) * P],
                                    slot(s, KD, c1 - c0), t, 0, c1 - c0, gv_()).then_inc(v_full, 1)
                    free()
                pe.wait_ge(H["tokens_normed"], 4 + 2 * layer)
                token_transposes(x)
                pe.wait_ge(H["hT_ready"], 4 + 2 * layer)
                if layer == 0:
                    pe.wait_ge(H["mix_ready"], 2)
                    pe.wait_ge(v_free, nv[0])
                    pe.wait_ge(a_free, na[0])
                    prev = None
                    for j in range(U2):
                        s, full, _ = r.take(3)
                        unit_in(s, ub[0] + j, full, j)
                        if prev is not None:
                            unit_down(prev, ub[0] + j - 1, j - 1, eb[0], j == 1, False, False)
                        prev = s
                    unit_down(prev, ub[0] + U2 - 1, U2 - 1, eb[0], False, True, False)
                    ub[0] += U2
                    eb[0] += 1
                else:
                    router(w_router2, NE2)
                    pe.wait_ge(H["mix_ready"], 3)
                    experts(NE2 // 4, 4, U2)


_INS = ['x', 'c', 'positions', 'rel_bias', 'w_ada', 'b_ada', 'norm1_g', 'w_in', 'sinks', 'gm_ln_g', 'gm_ln_b',
        'gm_w_s', 'gm_b_s', 'p_a', 'p_b', 'w_o', 'norm2_g', 'w_router_g', 'b_router_g', 'w_router_e', 'b_router_e',
        'w_gate', 'w_up', 'w_down', 'final_g', 'c_2', 'ada_w_2', 'ada_b_2', 'w_in_2', 'conv_w_2', 'gk_w2_2',
        'gk_b_2', 'gla_norm_w_2', 'w_out_2', 'ln1_g_2', 'ln1_b_2', 'ln2_g_2', 'ln2_b_2', 'ffn_w_gate_2',
        'ffn_w_up_2', 'ffn_w_down_2', 'router_w_2', 'moe_w_gate_2', 'moe_w_up_2', 'moe_w_down_2']


def kernel(**inputs):
    import numpy as _np
    import concourse.bacc as _bacc
    from concourse import mybir as _mybir
    from concourse.bass_utils import run_bass_kernel_spmd as _run

    nc = _bacc.Bacc("TRN2", target_bir_lowering=False, num_devices=1)
    arrays, aps = {}, {}
    for name in _INS:
        v = _np.ascontiguousarray(inputs[name])
        arrays[f"in_{name}_dram"] = v
        aps[name] = nc.dram_tensor(f"in_{name}_dram", v.shape, _mybir.dt.from_np(v.dtype), kind="ExternalInput").ap()
    out = nc.dram_tensor("out_0_dram", (1, T, D), F32, kind="ExternalOutput").ap()
    build(nc, aps, out)
    r = _run(nc, [arrays], core_ids=[0])
    return r.results[0]["out_0_dram"]
```

```python
from contextlib import ExitStack
import math

import numpy as np
import concourse.bass as bass
from concourse import mybir

F32 = mybir.dt.float32
I32 = mybir.dt.int32
ALU = mybir.AluOpType
ACT = mybir.ActivationFunctionType
AX = mybir.AxisListType.X

P = 128
D = 1024
KD = D // P
T = 256
TT = T // P
SLOTS = 4
FU = 256
SLOT = 3 * FU * KD
CH = 512

HEADS, HD, GROUP_HEADS = 8, 64, 4
POOL_HEADS = (6, 7)
ATTN_SCALE = HD ** -0.5
BUCKETS, MAX_EXACT, MAX_DISTANCE = 32, 16, 128
NEG = -1e30
RMS_EPS = 1e-6
LN_EPS = 1e-5

NG, EG = 4, 8
NE1 = NG * EG
F1 = 512
U1 = F1 // FU
NE2 = 8
F2 = 2816
U2 = F2 // FU

SL = 128
AW = 6 * D * 2 // (NE1 // 2)
CAP1, CAP2 = 64, 128
EPG1, EPG2 = SL // CAP1, SL // CAP2

GH, DK, DV, CK = 4, 64, 128, 64
GK_DIV, GK_MIN = 16.0, -1.0
ALPHA = 4.0 ** 0.25

SH1, SC1, G1, SH2, SC2, G2 = range(6)
SQ, SK, SV, SGU, SGV, SGA, SGB = 0, 512, 640, 768, 1280, 1792, 2816


def bucket_starts():
    n = np.arange(1, 4 * MAX_DISTANCE)
    large = MAX_EXACT + (np.log(n.astype(np.float32) / np.float32(MAX_EXACT))
                         / np.float32(math.log(MAX_DISTANCE / MAX_EXACT))
                         * np.float32(BUCKETS - MAX_EXACT)).astype(np.int32)
    bucket = np.where(n < MAX_EXACT, n, np.minimum(large, BUCKETS - 1))
    return [float(n[np.argmax(bucket >= b)]) for b in range(1, BUCKETS)]


class Count:

    def __init__(self, sem):
        self.sem, self.n = sem, 0


class Ring:

    def __init__(self):
        self.seq, self.loads = 0, [0] * SLOTS

    def take(self, dmas):
        i, s = self.seq, self.seq % SLOTS
        self.seq += 1
        self.loads[s] += 16 * dmas
        return s, self.loads[s], (i - SLOTS + 1 if i >= SLOTS else None)

    def loop(self, n, body):
        base, loads = self.seq, list(self.loads)
        per = 3 * 16 * (body // SLOTS)
        self.seq += n * body
        self.loads = [v + per * n for v in self.loads]

        def at(r, j):
            s = j % SLOTS
            return s, r * per + (loads[s] + 48 * (j // SLOTS + 1)), r * body + (base + j - SLOTS + 1)
        return at


def build(nc, a, out):
    with ExitStack() as ctx:
        def sb(name, shape, dt=F32):
            return ctx.enter_context(nc.sbuf_tensor(name, shape, dt))

        def sem(name):
            return ctx.enter_context(nc.semaphore(name))

        ring = sb("ring", [P, SLOTS, SLOT])
        x = sb("x", [P, TT, D])
        hT = sb("hT", [P, KD, T])
        tok = sb("tok", [P, TT, D])
        colsB = sb("colsB", [P, KD, P])
        gB = sb("gB", [P, 2, D])
        rowB = sb("rowB", [P, 2, D])
        arena = sb("arena", [P, 13824])
        ident = sb("ident", [P, P])
        triu = sb("triu", [P, P])
        chunk_triu = sb("chunk_triu", [P, P])
        chunk_tril = sb("chunk_tril", [P, P])
        colA = sb("colA", [P, 104])
        colB = sb("colB", [P, 96])
        csT = sb("csT", [P, 2, KD])
        modT = sb("modT", [P, 3, 48])
        scale_col = sb("scale_col", [P, KD])
        w_router = sb("w_router", [P, KD, 36])
        b_router = sb("b_router", [P, 36])
        w_router2 = sb("w_router2", [P, KD, NE2])
        poscol = sb("poscol", [P, TT], I32)
        relD = sb("relD", [P, BUCKETS * HEADS])
        starts = sb("starts", [P, BUCKETS])
        sinkB = sb("sinkB", [P, HEADS])
        stat = sb("stat", [P, 128])
        newton = sb("newton", [P, 12])
        rt = sb("rt", [P, 320])
        rev = sb("rev", [P, 8])
        combine = sb("combine", [P, TT, NE1 + EPG1])
        slot_of = sb("slot_of", [P, TT, NE1 + EPG1])
        chosen_by = sb("chosen_by", [P, TT, NE1])
        fits = sb("fits", [P, 2], I32)
        iota = sb("iota", [P, SL])
        ones = sb("ones", [P, P])
        strict = sb("strict", [P, P])
        gkw2 = sb("gkw2", [16, T])
        gkbB = sb("gkbB", [P, T])
        glnB = sb("glnB", [P, DV])

        def view(start, *shape):
            n = int(np.prod(shape))
            v = arena[:, start:start + n]
            if len(shape) == 2:
                v = v.rearrange("p (a b) -> p a b", a=shape[0])
            if len(shape) == 3:
                v = v.rearrange("p (a b c) -> p a b c", a=shape[0], b=shape[1])
            return v

        bias = view(0, HEADS, 384)
        pT = view(0, 6, CH)
        prob = view(3072, 6, CH)
        qT = view(6144, 4, T)
        yaT = view(6144, 4, T)
        kT = view(7168, T)
        v_tok = view(7424, TT, P)
        gv = view(7680, TT, 512)
        guT = view(8704, 4, T)
        gaT = view(9728, KD, T)
        gbT = view(11776, KD, T)
        dist = view(3584, 384)
        mask_v = view(3968, 384)
        pool_add = (view(4352, 384), view(4736, 384))
        ada_sum = (view(7680, CH), view(8192, CH))
        posf = view(10880, 4, T)
        posrow = view(11904, T).bitcast(I32)
        relB = view(12160, BUCKETS * HEADS)
        wsT = view(5120, 4, P)
        bsB = view(5632, 4, P)
        vecA = arena[0:104, 13312:13440]
        vecB = arena[0:96, 13440:13568]
        cbT = view(0, 4, T)
        ccT = view(1024, 4, T)
        ygT = view(1024, 4, T)
        zT = view(2048, 4, T + 2)
        q2T = view(3080, 2, T)
        k2T = view(3592, 2, T)
        k_tok = view(4104, TT, T)
        v2 = view(4616, TT, 512)
        sg_tok = view(5640, TT, 512)
        gk = view(6664, TT, T)
        gkt = view(7176, TT, T)
        gku = view(7688, TT, T)
        ebT = view(8200, 2, T)
        enbT = view(8712, 2, T)
        er = view(9224, TT, T)
        scT = view(9736, 2, 4, P)
        state = view(10760, 3, 2, DV)
        o_tok = view(11528, TT, 512)
        conv = view(11528, 4, T)
        glT = arena[0:16, 12552:12552 + T]
        silu_g = view(0, 2, 2 * T)
        hid = view(1024, 2, 2 * T)

        h_tok = view(2048, TT, D)
        xT = view(4096, KD, SL)
        y_slot = view(5120, D)
        pick = view(6144, TT, SL)
        pickw = view(6400, TT, SL)
        pickT = view(6656, TT, P)
        ada_w = view(6912, KD, AW)
        ada_part = view(13056, AW)

        ps = ctx.enter_context(nc.psum_tensor("ps", [P, 8, CH], F32))

        ring_full = [sem(f"ring_full{i}") for i in range(SLOTS)]
        ring_free = sem("ring_free")
        v_full, v_free, a_full, a_free = sem("v_full"), sem("v_free"), sem("a_full"), sem("a_free")
        PH = [{n: sem(f"{n}_{ph}") for n in ("gate_full", "up_full", "silu_done", "hid_ready", "y_free", "unit_full",
                                             "side_full", "side_free", "pick_ready")}
              for ph in ("moe1", "ffn", "moe2")]
        bias_done, ada_full, ada_step = sem("bias_done"), sem("ada_full"), sem("ada_step")
        got_x, got_vec, got_pos, got_spatial, got_router, got_rows = (
            sem(s) for s in ("got_x", "got_vec", "got_pos", "got_spatial", "got_router", "got_rows"))
        got_layer = sem("got_layer")
        stored = sem("stored")
        consts_step, consts_ready = sem("consts_step"), sem("consts_ready")
        dist_ready, bias_pool, pool_step = sem("dist_ready"), sem("bias_pool"), sem("pool_step")
        act_step = sem("act_step")
        names = ("cols_ready", "gate_cols", "tokens_normed", "hT_ready", "qkv_ready", "vn_ready", "scores_ready",
                 "probs_ready", "pT_ready", "ya_ready", "yb_ready", "merged_ready", "rows_used", "hT2_used",
                 "router_logits", "glow_ready", "gk_abs", "gk_exp1", "gk_ready", "gla_in", "gla_scores",
                 "states_ready", "o_normed", "mix_ready", "sink_ready", "dve_step", "layer_used", "x_ready", "ada_mac", "chosen_ready", "fits_ready")
        S = {s: Count(sem(s)) for s in names}
        H = {s: c.sem for s, c in S.items()}
        silu_c, gelu_u, gelu_v, sig_ab, exps_done, sink_exp, gk_e, gk_l, gla_exp, silu_gate, router_exp = (
            sem(s) for s in ("silu_c", "gelu_u", "gelu_v", "sig_ab", "exps_done", "sink_exp", "gk_e", "gk_l",
                             "gla_exp", "silu_gate", "router_exp"))

        block = ctx.enter_context(nc.Block())

        def chunk_k(w, c0, c1):
            return w.rearrange("(k p) n -> p k n", p=P)[:, :, c0:c1]

        def slot(s, kt, cols):
            return ring[:, s, 0:kt * cols].rearrange("p (k n) -> p k n", k=kt)

        def slot_gate(s):
            return ring[:, s, 0:KD * FU].rearrange("p (k n) -> p k n", k=KD)

        def slot_up(s):
            return ring[:, s, KD * FU:2 * KD * FU].rearrange("p (k n) -> p k n", k=KD)

        def slot_down(s):
            return ring[:, s, 2 * KD * FU:3 * KD * FU].rearrange("p (k n) -> p k n", k=2)

        MOE1_SEQ = 12 + 7 + 5
        FFN_SEQ = MOE1_SEQ + NE1 * U1 + 9
        MOE2_SEQ = FFN_SEQ + U2 + 8
        C_IN2 = [(0, 512), (512, 1024), (1024, 1536), (1536, 2048), (2048, 2560), (2560, 3088)]
        W_OUT_CUTS = [[(0, 512), (512, 768), (768, 1024)], [(0, 512), (512, 1024)]]

        @block.sync
        def _(sp):
            r = Ring()

            def load(parts):
                s, _, free = r.take(len(parts))
                if free is not None:
                    sp.wait_ge(ring_free, free)
                at = 0
                for src in parts:
                    kt, n = src.shape[1], src.shape[2]
                    sp.dma_start(ring[:, s, at:at + kt * n].rearrange("p (k n) -> p k n", k=kt), src)\
                      .then_inc(ring_full[s], 16)
                    at += kt * n

            def load_ada(w):
                wk = w.rearrange("(k p) n -> p k n", p=P)
                for c in range(4):
                    load([wk[:, :, c * CH:(c + 1) * CH]])
                with sp.Fori(0, 2) as h:
                    for c in range(4):
                        sp.wait_ge(ring_free, h * SLOTS + (c + 1))
                        sp.dma_start(slot(c, KD, CH), wk[:, :, bass.ds(h * (4 * CH) + (4 + c) * CH, CH)])\
                          .then_inc(ring_full[c], 16)
                for _ in range(8):
                    r.take(1)

            def load_units(gate, up, down, c0):
                return [chunk_k(gate, c0, c0 + FU), chunk_k(up, c0, c0 + FU),
                        down[c0:c0 + FU, :].rearrange("(k p) n -> p k n", p=P)]

            def load_experts(gate, up, down, ne, body_e, units, ada=None):
                body = body_e * units
                at = r.loop(ne // body_e, body)
                with sp.Fori(0, ne // body_e) as i:
                    for j in range(body):
                        if ada is not None and j == 1:
                            sp.wait_ge(ada_step, i * KD + 1)
                            rounds = 6 * D // AW
                            src = ada[bass.ds(i // rounds, 1), :, bass.ds((i % rounds) * AW, AW)]
                            sp.dma_start(ada_w, src.rearrange("o (k p) n -> p (o k) n", p=P)).then_inc(ada_full, 16)
                        s, _, free = at(i, j)
                        e, c0 = i * body_e + j // units, (j % units) * FU
                        sp.wait_ge(ring_free, free)
                        g = gate[bass.ds(e, 1), :, c0:c0 + FU].rearrange("o (k p) n -> p (o k) n", p=P)
                        u = up[bass.ds(e, 1), :, c0:c0 + FU].rearrange("o (k p) n -> p (o k) n", p=P)
                        d = down[bass.ds(e, 1), c0:c0 + FU, :].rearrange("o (k p) n -> p (o k) n", p=P)
                        sp.dma_start(slot_gate(s), g).then_inc(ring_full[s], 16)
                        sp.dma_start(slot_up(s), u).then_inc(ring_full[s], 16)
                        sp.dma_start(slot_down(s), d).then_inc(ring_full[s], 16)

            load_ada(a["w_ada"][0])
            w = a["w_in"][0]
            s, _, free = r.take(10)
            sp.wait_ge(ring_free, free)
            for half in range(2):
                q_src = w[:, half * 256:half * 256 + 256].rearrange("(k p) (j d) -> p j k d", p=P, d=HD)
                for j in range(4):
                    sp.dma_start(slot(s, KD, 768)[:, :, j * P + half * HD:j * P + half * HD + HD], q_src[:, j])\
                      .then_inc(ring_full[s], 16)
            sp.dma_start(slot(s, KD, 768)[:, :, 512:640], chunk_k(w, SK, SV)).then_inc(ring_full[s], 16)
            sp.dma_start(slot(s, KD, 768)[:, :, 640:768], chunk_k(w, SV, SGU)).then_inc(ring_full[s], 16)
            for c in range(6):
                load([chunk_k(w, SGU + c * CH, SGU + (c + 1) * CH)])
            for c in range(2):
                load([chunk_k(a["p_a"][0], c * CH, (c + 1) * CH)])
            load([chunk_k(a["p_b"][0], 0, D)])
            for c in range(2):
                load([chunk_k(a["w_o"][0], c * CH, (c + 1) * CH)])
            load_experts(a["w_gate"][0], a["w_up"][0], a["w_down"][0], NE1, 2, U1, a["ada_w_2"])
            for layer in range(2):
                w = a["w_in_2"][layer]
                for c0, c1 in C_IN2:
                    load([chunk_k(w, c0, c1)])
                for c0, c1 in W_OUT_CUTS[layer]:
                    load([chunk_k(a["w_out_2"][layer], c0, c1)])
                if layer == 0:
                    for u in range(U2):
                        load(load_units(a["ffn_w_gate_2"][0], a["ffn_w_up_2"][0], a["ffn_w_down_2"][0], u * FU))
            load_experts(a["moe_w_gate_2"][0], a["moe_w_up_2"][0], a["moe_w_down_2"][0], NE2, 4, U2)
            sp.wait_ge(H["x_ready"], 1)
            sp.dma_start(out[0].rearrange("(t p) d -> p t d", p=P), x[:, :, :]).then_inc(stored, 16)
            sp.wait_ge(stored, 16)

        @block.gpsimd
        def _(pool):
            n = [0]

            def const(ins, ready=False):
                n[0] += 1
                ins.then_inc(consts_step, 1)
                pool.wait_ge(consts_step, n[0])

            def pair(first, second):
                for i, v in enumerate((first, second)):
                    if v is not None:
                        pool.dma_start(rowB[:, i, :], v.partition_broadcast(P)).then_inc(got_rows, 16)

            pool.dma_start(rowB[:, 0, 0:512], a["gm_ln_g"][0].partition_broadcast(P)).then_inc(got_rows, 16)
            pool.dma_start(rowB[:, 0, 512:1024], a["gm_ln_b"][0].partition_broadcast(P)).then_inc(got_rows, 16)
            const(pool.memset(ident[:, :], 0.0))
            const(pool.affine_select(out=ident[:, :], in_=ident[:, :], compare_op=ALU.not_equal, fill=1.0, base=0,
                                     pattern=[[-1, P]], channel_multiplier=1))
            for m in (triu, chunk_triu):
                const(pool.memset(m[:, :], 1.0))
                const(pool.affine_select(out=m[:, :], in_=m[:, :], compare_op=ALU.is_ge, fill=0.0, base=0,
                                         pattern=[[1, P]], channel_multiplier=-1))
            const(pool.memset(chunk_triu[0:CK, CK:P], 0.0))
            const(pool.memset(chunk_tril[:, :], 1.0))
            const(pool.affine_select(out=chunk_tril[:, :], in_=chunk_tril[:, :], compare_op=ALU.is_ge, fill=0.0,
                                     base=-1, pattern=[[-1, P]], channel_multiplier=1))
            const(pool.memset(chunk_tril[CK:P, 0:CK], 0.0))
            const(pool.memset(ones[:, :], 1.0))
            const(pool.iota(iota[:, :], [[1, SL]], base=0, channel_multiplier=0, allow_small_or_imprecise_dtypes=True))
            const(pool.memset(strict[:, :], 1.0))
            const(pool.affine_select(out=strict[:, :], in_=strict[:, :], compare_op=ALU.is_ge, fill=0.0, base=-1,
                                     pattern=[[1, P]], channel_multiplier=-1))
            for i in range(8):
                const(pool.memset(rev[:, i:i + 1], float(8 - i)))
            const(pool.memset(starts[:, 0:1], -3e38))
            for b, s in enumerate(bucket_starts()):
                const(pool.memset(starts[:, b + 1:b + 2], s))
            const(pool.memset(bias[:, 6:8, :], 0.0))
            pool.memset(stat[:, 127:128], 1.0).then_inc(consts_ready, 1)
            pool.wait_ge(dist_ready, 1)
            k = 0
            for b in range(BUCKETS):
                for i, h in enumerate(POOL_HEADS):
                    ins = pool.tensor_scalar(pool_add[i], dist, starts[:, b:b + 1],
                                             relD[:, b * HEADS + h:b * HEADS + h + 1], ALU.is_ge, ALU.mult)
                ins.then_inc(pool_step, 1)
                k += 1
                pool.wait_ge(pool_step, k)
                for i, h in enumerate(POOL_HEADS):
                    ins = pool.tensor_tensor(bias[:, h, :], bias[:, h, :], pool_add[i], ALU.add)
                ins.then_inc(pool_step, 1)
                k += 1
                pool.wait_ge(pool_step, k)
            for h in POOL_HEADS:
                for part in range(3):
                    lo = part * P
                    sign, base = (-1, 0) if part != 1 else (1, -1)
                    ins = pool.affine_select(out=bias[:, h, lo:lo + P], in_=bias[:, h, lo:lo + P],
                                             compare_op=ALU.is_ge, fill=NEG, base=base,
                                             pattern=[[sign, P]], channel_multiplier=-sign)
            ins.then_inc(bias_pool, 1)
            pool.wait_ge(bias_done, 1)
            for h in range(6):
                for part in range(3):
                    lo = part * P
                    sign, base = (-1, 0) if part != 1 else (1, -1)
                    ins = pool.affine_select(out=bias[:, h, lo:lo + P], in_=bias[:, h, lo:lo + P],
                                             compare_op=ALU.is_ge, fill=NEG, base=base,
                                             pattern=[[sign, P]], channel_multiplier=-sign)
            ins.then_inc(bias_pool, 1)
            pool.wait_ge(H["rows_used"], 1)
            pool.dma_start(rowB[:, 0, :], a["final_g"].partition_broadcast(P)).then_inc(got_rows, 16)
            used = 2
            for layer in range(2):
                for one, two in ((a["ln1_g_2"][layer], a["ln1_b_2"][layer]),
                                 (a["ln2_g_2"][layer], a["ln2_b_2"][layer])):
                    pool.wait_ge(H["rows_used"], used)
                    pair(one, two)
                    used += 1

        @block.scalar
        def _(act):
            def load(dst, src, s):
                act.dma_start(dst, src, allow_slow_non_contiguous=True).then_inc(s, 16)

            load(vecA[0:48, :], a["b_ada"][0].rearrange("(r p) -> r p", p=P), got_vec)
            load(vecA[48:56, :], a["c"][0].rearrange("(r p) -> r p", p=P), got_vec)
            load(vecA[56:64, :], a["norm1_g"][0].rearrange("(r p) -> r p", p=P), got_vec)
            load(vecA[64:72, :], a["norm2_g"][0].rearrange("(r p) -> r p", p=P), got_vec)
            load(vecA[72:80, :], a["c_2"][0].rearrange("(r p) -> r p", p=P), got_vec)
            load(vecA[80:104, :], a["conv_w_2"].rearrange("l j (r p) -> (l j r) p", p=P), got_vec)
            load(vecB, a["ada_b_2"].rearrange("l (r p) -> (l r) p", p=P), got_vec)
            load(x[:, :, :], a["x"][0].rearrange("(t p) d -> p t d", p=P), got_x)
            load(posrow, a["positions"][0].partition_broadcast(P), got_pos)
            load(poscol[:, :], a["positions"][0].rearrange("(t p) -> p t", p=P), got_pos)
            load(relB, a["rel_bias"].rearrange("b h -> (b h)").partition_broadcast(P), got_pos)
            load(sinkB[:, :], a["sinks"][0].partition_broadcast(P), got_pos)
            ws = prob[:, 0, :].rearrange("p (g s) -> p g s", g=4)
            load(ws, a["gm_w_s"][0].rearrange("g t s -> t g s"), got_spatial)
            load(bsB[:, :, :], a["gm_b_s"][0].rearrange("g t -> (g t)").partition_broadcast(P)
                 .rearrange("p (g t) -> p g t", g=4), got_spatial)
            load(w_router[:, :, 0:4], a["w_router_g"][0].rearrange("(k p) n -> p k n", p=P), got_router)
            load(w_router[:, :, 4:36], a["w_router_e"][0].rearrange("(k p) n -> p k n", p=P), got_router)
            load(w_router2[:, :, :], a["router_w_2"][0].rearrange("(k p) n -> p k n", p=P), got_router)
            load(b_router[:, 0:4], a["b_router_g"][0].partition_broadcast(P), got_router)
            load(b_router[:, 4:36], a["b_router_e"][0].partition_broadcast(P), got_router)

            def load_layer(layer):
                load(gkw2[:, :], a["gk_w2_2"][layer], got_layer)
                load(gkbB[:, :], a["gk_b_2"][layer].partition_broadcast(P), got_layer)
                load(glnB[:, :], a["gla_norm_w_2"][layer].partition_broadcast(P), got_layer)

            load_layer(0)
            na = [0]

            def group():
                act.wait_ge(a_full, na[0] + 1)
                na[0] += 1
                return 4 + (na[0] - 1) % 4

            act.wait_ge(H["cols_ready"], 1)
            act.activation(csT[:, 0, :], colA[:, 48:56], ACT.Silu)
            act.activation(csT[:, 1, :], colA[:, 72:80], ACT.Silu).then_inc(silu_c, 1)
            for g in range(2):
                bank = group()
                act.activation(guT[:, 2 * g:2 * g + 2, :], ps[:, bank, :].rearrange("p (a b) -> p a b", a=2),
                               ACT.Gelu_apprx_tanh).then_inc(a_free, 1)
            for t in range(TT):
                bank = group()
                act.activation(gv[:, t, :], ps[:, bank, :], ACT.Gelu_apprx_tanh).then_inc(a_free, 1)
            for g in range(4):
                bank = group()
                act.activation(gaT[:, 2 * g:2 * g + 2, :], ps[:, bank, :].rearrange("p (a b) -> p a b", a=2),
                               ACT.Sigmoid).then_inc(a_free, 1)
            for g in range(4):
                bank = group()
                act.activation(gbT[:, 2 * g:2 * g + 2, :], ps[:, bank, :].rearrange("p (a b) -> p a b", a=2),
                               ACT.Sigmoid).then_inc(a_free, 1)
            for g in range(6):
                act.wait_ge(H["scores_ready"], g + 1)
                nh = 4 if g < 2 else 2
                st = 4 * g if g < 2 else 8 + 2 * (g - 2)
                for i in range(nh):
                    w = CH // nh
                    ins = act.activation(prob[:, g, i * w:(i + 1) * w], prob[:, g, i * w:(i + 1) * w], ACT.Exp,
                                         bias=stat[:, 16 + st + i:17 + st + i], accum_out=stat[:, 32 + st + i:33 + st + i])
                ins.then_inc(exps_done, 1)
            act.wait_ge(H["sink_ready"], 1)
            act.activation(stat[:, 64:80], stat[:, 48:64], ACT.Exp).then_inc(sink_exp, 1)

            def experts(layer, q, n, body, cap):
                act.wait_ge(H["fits_ready"], layer + 1)
                flag = act.value_load(fits[0:1, layer:layer + 1], min_val=0, max_val=1)
                with act.If(flag == 1):
                    with act.Fori(0, n) as i:
                        for j in range(body):
                            act.wait_ge(q["unit_full"], i * body + (j + 1))
                            if j >= 2:
                                act.wait_ge(q["hid_ready"], i * body + (j - 1))
                            act.activation(silu_g[:, j % 2, 0:2 * cap], ps[:, 6 + j % 2, 0:2 * cap], ACT.Silu)\
                               .then_inc(q["silu_done"], 1)
                with act.Else():
                    with act.Fori(0, n) as i:
                        for j in range(body):
                            act.wait_ge(q["gate_full"], i * body + (j + 1))
                            if j >= 2:
                                act.wait_ge(q["hid_ready"], i * body + (j - 1))
                            act.activation(silu_g[:, j % 2, :], ps[:, 4 + 2 * (j % 2), :], ACT.Silu)\
                               .then_inc(q["silu_done"], 1)

            act.wait_ge(H["router_logits"], 1)
            act.activation(rt[:, 96:104], rt[:, 80:88], ACT.Exp)
            act.activation(rt[:, 144:160], rt[:, 128:144], ACT.Exp).then_inc(router_exp, 1)
            act.wait_ge(H["mix_ready"], 1)
            experts(0, PH[0], NE1 // 2, 2 * U1, CAP1)
            for layer in range(2):
                for t in range(TT):
                    bank = group()
                    act.activation(sg_tok[:, t, :], ps[:, bank, :], ACT.Silu).then_inc(a_free, 1)
                act.wait_ge(H["gk_abs"], layer + 1)
                act.activation(gku, gku, ACT.Exp).then_inc(gk_e, 1)
                act.wait_ge(H["gk_exp1"], layer + 1)
                act.activation(gku, gku, ACT.Ln).then_inc(gk_l, 1)
                bank = group()
                act.activation(ebT, ps[:, bank, :].rearrange("p (a b) -> p a b", a=2), ACT.Exp).then_inc(act_step, 1)
                act.wait_ge(act_step, layer + 1)
                act.activation(enbT, ps[:, bank, :].rearrange("p (a b) -> p a b", a=2), ACT.Exp, scale=-1.0)\
                   .then_inc(a_free, 1)
                bank = group()
                act.activation(er, ps[:, bank, :].rearrange("p (a b) -> p a b", a=2), ACT.Exp).then_inc(a_free, 1)
                if layer == 0:
                    act.wait_ge(H["layer_used"], 1)
                    load_layer(1)
                    act.wait_ge(H["mix_ready"], 2)
                    for j in range(U2):
                        act.wait_ge(PH[1]["gate_full"], j + 1)
                        if j >= 2:
                            act.wait_ge(PH[1]["hid_ready"], j - 1)
                        act.activation(silu_g[:, j % 2, :], ps[:, 4 + 2 * (j % 2), :], ACT.Silu)\
                           .then_inc(PH[1]["silu_done"], 1)
                else:
                    act.wait_ge(H["router_logits"], 2)
                    act.activation(rt[:, 32:48], rt[:, 16:32], ACT.Exp).then_inc(router_exp, 1)
                    act.wait_ge(H["mix_ready"], 3)
                    experts(1, PH[2], NE2 // 4, 4 * U2, CAP2)

        @block.vector
        def _(dve):
            nv, nf = [0], [0]

            def step(ins, name="dve_step", wait=True):
                c = S[name]
                c.n += 1
                ins.then_inc(c.sem, 1)
                if wait:
                    dve.wait_ge(c.sem, c.n)
                return ins

            def group():
                nf[0] += 1
                dve.wait_ge(v_full, nf[0])
                nv[0] += 1
                return (nv[0] - 1) % 4

            def freed(ins):
                ins.then_inc(v_free, 1)

            def freed_wait(ins):
                ins.then_inc(v_free, 1)
                dve.wait_ge(v_free, nv[0])

            def bank2(b):
                return ps[:, b, :].rearrange("p (a b) -> p a b", a=2)

            def bank4(b):
                return ps[:, b, :].rearrange("p (a b) -> p a b", a=4)

            ones_wait = 1
            dve.wait_ge(consts_ready, 1)
            dve.wait_ge(got_pos, 64)
            posi = posf[:, 0:2, :].bitcast(I32)
            hi_r, lo_r = posi[:, 0, :], posi[:, 1, :]
            step(dve.tensor_scalar(hi_r, posrow, 16, None, ALU.arith_shift_right))
            step(dve.tensor_scalar(lo_r, posrow, 65535, None, ALU.bitwise_and))
            ci = stat[:, 0:4].bitcast(I32)
            step(dve.tensor_scalar(ci[:, 0:2], poscol[:, :], 16, None, ALU.arith_shift_right))
            step(dve.tensor_scalar(ci[:, 2:4], poscol[:, :], 65535, None, ALU.bitwise_and))
            step(dve.tensor_copy(stat[:, 4:8], ci))
            step(dve.tensor_copy(posf[:, 2, :], hi_r))
            step(dve.tensor_copy(posf[:, 3, :], lo_r))
            for t, (lo, w) in enumerate(((0, P), (P, T))):
                step(dve.tensor_scalar(dist[:, lo:lo + w], posf[:, 2, 0:w], stat[:, 4 + t:5 + t], -65536.0,
                                       ALU.subtract, ALU.mult))
                step(dve.tensor_scalar(mask_v[:, lo:lo + w], posf[:, 3, 0:w], stat[:, 6 + t:7 + t], -1.0,
                                       ALU.subtract, ALU.mult))
            step(dve.tensor_copy(relD[:, 0:HEADS], relB[:, 0:HEADS]), wait=False)
            step(dve.tensor_tensor(relD[:, HEADS:], relB[:, HEADS:], relB[:, 0:(BUCKETS - 1) * HEADS], ALU.subtract))
            dve.tensor_tensor(dist, dist, mask_v, ALU.add).then_inc(dist_ready, 1)
            dve.wait_ge(dist_ready, 1)
            step(dve.memset(bias[:, 0:6, :], 0.0))
            b = group()
            freed(dve.tensor_copy(colA[:, :], ps[:, b, 0:104]))
            b = group()
            freed_wait(dve.tensor_copy(colB[:, :], ps[:, b, 0:96]))
            step(dve.tensor_copy(stat[:, 120:121], colA[:, 0:1]), "cols_ready")
            for t in range(2):
                b = group()
                freed_wait(dve.tensor_tensor(wsT[:, 2 * t:2 * t + 2, :], ps[:, b, 0:256].rearrange("p (a b) -> p a b", a=2),
                                             triu[:, :].unsqueeze(1).to_broadcast([P, 2, P]), ALU.mult))

            dve.wait_ge(silu_c, 1)

            def ada_cols(h, c):
                dve.wait_ge(ring_free, h * 4 + (c + 1))
                dve.tensor_tensor(modT[:, 0, bass.ds(h * 16 + 4 * c, 4)], ps[:, (nv[0] + c) % 4, 0:4],
                                  colA[:, bass.ds(h * 16 + 4 * c, 4)], ALU.add).then_inc(v_free, 1)

            with dve.Fori(0, 3) as h:
                for c in range(4):
                    dve.wait_ge(ring_full[c], h * 16 + 16)
                    w = slot(c, KD, CH)
                    for k in range(KD):
                        if k == 0:
                            ins = dve.tensor_scalar(ada_sum[c % 2], w[:, 0, :], csT[:, 0, 0:1], None, ALU.mult)
                        else:
                            ins = dve.scalar_tensor_tensor(out=ada_sum[c % 2], in0=w[:, k, :],
                                                           scalar=csT[:, 0, k:k + 1], in1=ada_sum[c % 2],
                                                           op0=ALU.mult, op1=ALU.add)
                        ins.then_inc(H["ada_mac"], 1)
                        dve.wait_ge(H["ada_mac"], h * (4 * KD) + (c * KD + k + 1))
                    if c:
                        ada_cols(h, c - 1)
                ada_cols(h, 3)
            nv[0] += 12
            dve.wait_ge(v_free, nv[0])

            def gates(m, one):
                for g, s in enumerate((G1, G2)):
                    step(dve.tensor_copy(colsB[:, :, :], sec(s, m).unsqueeze(2).to_broadcast([P, KD, P])),
                         "gate_cols", wait=False)
                    for half in range(2):
                        b = group()
                        freed_wait(dve.tensor_scalar(gB[:, g, half * CH:(half + 1) * CH], ps[:, b, :], one, None, ALU.add))

            def relative_bias(lo, hi):
                base = S["dve_step"].n
                with dve.Fori(0, hi - lo) as r_:
                    n = 0
                    for i in range(4):
                        bk = r_ * 4 + (4 * lo + i)
                        dve.tensor_scalar(mask_v, dist, starts[:, bass.ds(bk, 1)], None, ALU.is_ge)\
                           .then_inc(H["dve_step"], 1)
                        n += 1
                        dve.wait_ge(H["dve_step"], r_ * 8 + (base + n))
                        for hd in range(6):
                            ins = dve.scalar_tensor_tensor(
                                out=bias[:, hd, :], in0=mask_v, scalar=relD[:, bass.ds(bk * HEADS + hd, 1)],
                                in1=bias[:, hd, :], op0=ALU.mult, op1=ALU.add)
                        ins.then_inc(H["dve_step"], 1)
                        n += 1
                        dve.wait_ge(H["dve_step"], r_ * 8 + (base + n))
                S["dve_step"].n += 8 * (hi - lo)

            rows_got = 0

            def rstd(dst, src, mul, eps):
                n = src.shape[1]
                v, bits, t = (newton[:, 4 * i:4 * i + n] for i in range(3))
                step(dve.tensor_scalar(v, src, mul, eps, ALU.mult, ALU.add))
                step(dve.tensor_scalar(bits.bitcast(I32), v.bitcast(I32), 1, None, ALU.arith_shift_right))
                step(dve.tensor_scalar(dst.bitcast(I32), bits.bitcast(I32), -1.0, float(0x5f3759df),
                                       ALU.mult, ALU.add))
                for _ in range(4):
                    step(dve.tensor_tensor(t, dst, dst, ALU.mult))
                    step(dve.scalar_tensor_tensor(out=t, in0=t, scalar=-0.5, in1=v, op0=ALU.mult, op1=ALU.mult))
                    step(dve.scalar_tensor_tensor(out=dst, in0=t, scalar=1.5, in1=dst, op0=ALU.add, op1=ALU.mult))

            def rms(dst):
                for t in range(TT):
                    step(dve.tensor_tensor_reduce(out=tok[:, t, :], in0=x[:, t, :], in1=x[:, t, :], scale=1.0,
                                                  scalar=0.0, op0=ALU.mult, op1=ALU.add, accum_out=stat[:, 80 + t:81 + t]))
                rstd(stat[:, 82:84], stat[:, 80:82], 1.0 / D, RMS_EPS)
                for t in range(TT):
                    ins = dve.tensor_scalar(dst[:, t, :], x[:, t, :], stat[:, 82 + t:83 + t], None, ALU.mult)
                return ins

            def transposed(scale, shift):
                for t in range(TT):
                    for half in range(2):
                        b = group()
                        for j in range(4):
                            k = 4 * half + j
                            ins = dve.tensor_scalar(hT[:, k, t * P:(t + 1) * P], ps[:, b, j * P:(j + 1) * P],
                                                    scale[:, k:k + 1], shift[:, k:k + 1], ALU.mult, ALU.add)
                        freed(ins)
                dve.wait_ge(v_free, nv[0])
                step(dve.memset(stat[:, 122:123], 0.0), "hT_ready", wait=False)

            def sec(s, m=0):
                return modT[:, m, s * KD:(s + 1) * KD]

            dve.wait_ge(got_x, 16)
            step(rms(tok), "tokens_normed", wait=False)
            step(dve.scalar_tensor_tensor(out=scale_col[:, :], in0=sec(SC1), scalar=1.0, in1=colA[:, 56:64],
                                          op0=ALU.add, op1=ALU.mult))
            transposed(scale_col, sec(SH1))
            gates(0, 0.0)
            for g in range(2):
                b = group()
                freed(dve.tensor_copy(qT[:, 2 * g:2 * g + 2, :], bank2(b)))
            b = group()
            freed(dve.tensor_copy(kT, ps[:, b, 0:T]))
            b = group()
            freed(dve.tensor_copy(v_tok, ps[:, b, 0:T].rearrange("p (a b) -> p a b", a=2)))
            dve.wait_ge(v_free, nv[0])
            step(dve.memset(stat[:, 123:124], 0.0), "qkv_ready", wait=False)

            def layer_norm(w, v, g, b, eps):
                m = w // 512
                for t in range(TT):
                    for i in range(m):
                        at = 84 + 12 * t + 6 * i
                        ins = dve.bn_stats(stat[:, at:at + 6], v[:, t, i * 512:(i + 1) * 512])
                step(ins)
                for t in range(TT):
                    ins = dve.bn_aggr(stat[:, 108 + 2 * t:110 + 2 * t], stat[:, 84 + 12 * t:84 + 12 * t + 6 * m]
                                      .rearrange("p (a b) -> p a b", b=6))
                step(ins)
                step(dve.tensor_copy(stat[:, 80:82], stat[:, 108:112].rearrange("p (a b) -> p a b", b=2)[:, :, 1]))
                rstd(stat[:, 82:84], stat[:, 80:82], 1.0, eps)
                for t in range(TT):
                    step(dve.tensor_scalar(v[:, t, :], v[:, t, :], stat[:, 108 + 2 * t:109 + 2 * t],
                                           stat[:, 82 + t:83 + t], ALU.subtract, ALU.mult))
                    step(dve.tensor_tensor(v[:, t, :], v[:, t, :], g, ALU.mult))
                    step(dve.tensor_tensor(v[:, t, :], v[:, t, :], b, ALU.add))

            relative_bias(0, 2)
            dve.wait_ge(a_free, 4)
            rows_got += 32
            dve.wait_ge(got_rows, rows_got)
            layer_norm(512, gv, rowB[:, 0, 0:512], rowB[:, 0, 512:1024], RMS_EPS)
            step(dve.memset(stat[:, 124:125], 0.0), "vn_ready")
            step(dve.memset(stat[:, 121:122], 0.0), "rows_used")
            relative_bias(2, 8)
            dve.memset(stat[:, 121:122], 0.0).then_inc(bias_done, 1)
            dve.wait_ge(got_spatial, 32)
            for t in range(TT):
                b = group()
                step(dve.tensor_tensor(tok[:, t, 0:512].rearrange("p (a b) -> p a b", a=4), bank4(b), bsB[:, :, :], ALU.add))
                freed(dve.tensor_tensor(guT[:, :, t * P:(t + 1) * P], guT[:, :, t * P:(t + 1) * P],
                                        tok[:, t, 0:512].rearrange("p (a b) -> p a b", a=4), ALU.mult))
            dve.wait_ge(v_free, nv[0])
            step(dve.memset(stat[:, 125:126], 0.0), "yb_ready", wait=False)
            dve.wait_ge(bias_pool, 2)
            for g in range(6):
                nh = 4 if g < 2 else 2
                w = CH // nh
                h0 = 4 * g if g < 2 else 2 * (g - 2)
                st = h0 if g < 2 else 8 + h0
                bv = bias[:, h0:h0 + nh, 0:P] if g < 2 else bias[:, h0:h0 + nh, P:384]
                b = group()
                pg = prob[:, g, :].rearrange("p (a b) -> p a b", a=nh)
                freed_wait(dve.scalar_tensor_tensor(out=pg, in0=ps[:, b, :].rearrange("p (a b) -> p a b", a=nh),
                                                    scalar=ATTN_SCALE, in1=bv, op0=ALU.mult, op1=ALU.add))
                step(dve.tensor_reduce(stat[:, st:st + nh], pg, AX, ALU.max))
                step(dve.tensor_tensor(stat[:, st:st + nh], stat[:, st:st + nh], sinkB[:, h0:h0 + nh], ALU.max))
                step(dve.tensor_scalar(stat[:, 16 + st:16 + st + nh], stat[:, st:st + nh], -1.0, None, ALU.mult),
                     "scores_ready")
            for blk in range(2):
                ins = dve.tensor_tensor(stat[:, 48 + 8 * blk:56 + 8 * blk], sinkB[:, :],
                                        stat[:, 16 + 8 * blk:24 + 8 * blk], ALU.add)
            step(ins, "sink_ready")
            dve.wait_ge(sink_exp, 1)
            step(dve.tensor_tensor(stat[:, 32:48], stat[:, 32:48], stat[:, 64:80], ALU.add))
            step(dve.reciprocal(stat[:, 32:48], stat[:, 32:48]))
            for g in range(6):
                nh = 4 if g < 2 else 2
                st = 4 * g if g < 2 else 8 + 2 * (g - 2)
                pg = prob[:, g, :].rearrange("p (a b) -> p a b", a=nh)
                step(dve.tensor_tensor(pg, pg, stat[:, 32 + st:32 + st + nh].unsqueeze(2)
                                       .to_broadcast([P, nh, CH // nh]), ALU.mult), "probs_ready", wait=False)
            for g in range(6):
                b = group()
                freed_wait(dve.tensor_copy(pT[:, g, :], ps[:, b, :]))
                step(dve.memset(stat[:, 126:127], 0.0), "pT_ready", wait=False)
            for blk in range(2):
                b = group()
                freed(dve.tensor_copy(yaT[:, :, blk * P:(blk + 1) * P], bank4(b)))
            dve.wait_ge(v_free, nv[0])
            step(dve.memset(stat[:, 120:121], 0.0), "ya_ready", wait=False)
            dve.wait_ge(a_free, 12)
            for g in range(4):
                b = group()
                freed_wait(dve.tensor_tensor(gaT[:, 2 * g:2 * g + 2, :], gaT[:, 2 * g:2 * g + 2, :], bank2(b), ALU.mult))
            for g in range(4):
                b = group()
                freed_wait(dve.tensor_tensor(gbT[:, 2 * g:2 * g + 2, :], gbT[:, 2 * g:2 * g + 2, :], bank2(b), ALU.mult))
                ins = dve.tensor_tensor(gaT[:, 2 * g:2 * g + 2, :], gaT[:, 2 * g:2 * g + 2, :],
                                        gbT[:, 2 * g:2 * g + 2, :], ALU.add)
                step(ins, "merged_ready")

            def gated_sum(g, keep, cuts):
                for c0, c1 in cuts:
                    for t in range(TT):
                        b = group()
                        freed_wait(dve.tensor_tensor(tok[:, t, c0:c1], ps[:, b, 0:c1 - c0], gB[:, g, c0:c1], ALU.mult))
                        step(dve.scalar_tensor_tensor(out=x[:, t, c0:c1], in0=x[:, t, c0:c1], scalar=keep,
                                                      in1=tok[:, t, c0:c1], op0=ALU.mult, op1=ALU.add))

            gated_sum(0, 1.0, [(0, 512), (512, 1024)])
            step(rms(tok), "tokens_normed", wait=False)
            step(dve.scalar_tensor_tensor(out=scale_col[:, :], in0=sec(SC2), scalar=1.0, in1=colA[:, 64:72],
                                          op0=ALU.add, op1=ALU.mult))
            transposed(scale_col, sec(SH2))

            def first_max(dst, src, val, n, scratch, g):
                step(dve.tensor_reduce(val, src, AX, ALU.max))
                step(dve.tensor_tensor(dst, src, val.unsqueeze(2).to_broadcast([P, g, n]), ALU.is_equal))
                step(dve.tensor_tensor(dst, dst, rev[:, 8 - n:8].unsqueeze(1).to_broadcast([P, g, n]), ALU.mult))
                step(dve.tensor_reduce(scratch, dst, AX, ALU.max))
                step(dve.tensor_tensor(dst, dst, scratch.unsqueeze(2).to_broadcast([P, g, n]), ALU.is_equal))

            def r2(lo, n):
                return rt[:, lo:lo + 2 * n].rearrange("p (a b) -> p a b", a=2)

            b = group()
            logits = r2(0, 36)
            dve.wait_ge(got_router, 80)
            freed_wait(dve.tensor_tensor(logits, ps[:, b, 0:72].rearrange("p (a b) -> p a b", a=2),
                                         b_router[:, :].unsqueeze(1).to_broadcast([P, 2, 36]), ALU.add))
            sc2 = rt[:, 300:302]
            gmax = rt[:, 302:304]
            first_max(r2(72, 4), logits[:, :, 0:4], gmax, 4, sc2, 2)
            step(dve.tensor_tensor(r2(80, 4), logits[:, :, 0:4], gmax.unsqueeze(2).to_broadcast([P, 2, 4]), ALU.subtract))
            chosen = r2(112, 8)
            step(dve.tensor_tensor(chosen, logits[:, :, 4:12], r2(72, 4)[:, :, 0:1].to_broadcast([P, 2, 8]), ALU.mult))
            for g in range(1, NG):
                step(dve.tensor_tensor(r2(192, 8), logits[:, :, 4 + 8 * g:12 + 8 * g],
                                       r2(72, 4)[:, :, g:g + 1].to_broadcast([P, 2, 8]), ALU.mult))
                step(dve.tensor_tensor(chosen, chosen, r2(192, 8), ALU.add))
            emax = rt[:, 304:306]
            step(dve.tensor_reduce(emax, chosen, AX, ALU.max))
            step(dve.tensor_tensor(r2(128, 8), chosen, emax.unsqueeze(2).to_broadcast([P, 2, 8]), ALU.subtract),
                 "router_logits")
            dve.wait_ge(router_exp, 1)
            pg_ = rt[:, 306:308]
            step(dve.tensor_reduce(pg_, r2(96, 4), AX, ALU.add))
            step(dve.reciprocal(pg_, pg_))
            esum = rt[:, 308:310]
            step(dve.tensor_reduce(esum, r2(144, 8), AX, ALU.add))
            step(dve.reciprocal(esum, esum))
            pr = r2(144, 8)
            step(dve.tensor_tensor(pr, pr, esum.unsqueeze(2).to_broadcast([P, 2, 8]), ALU.mult))

            def top2(pr, oh1, oh2, tmp, w1, w2, sc):
                first_max(oh1, pr, w1, 8, sc, 2)
                step(dve.scalar_tensor_tensor(out=tmp, in0=oh1, scalar=-3e38, in1=pr, op0=ALU.mult, op1=ALU.add))
                first_max(oh2, tmp, w2, 8, sc, 2)

            w1, w2 = rt[:, 310:312], rt[:, 312:314]
            top2(pr, r2(160, 8), r2(176, 8), r2(192, 8), w1, w2, sc2)
            den = rt[:, 314:316]
            step(dve.tensor_tensor(den, w1, w2, ALU.add))
            step(dve.reciprocal(den, den))
            step(dve.tensor_tensor(w1, w1, den, ALU.mult))
            step(dve.tensor_tensor(w2, w2, den, ALU.mult))
            step(dve.tensor_tensor(w1, w1, pg_, ALU.mult))
            step(dve.tensor_tensor(w2, w2, pg_, ALU.mult))
            step(dve.tensor_tensor(r2(160, 8), r2(160, 8), w1.unsqueeze(2).to_broadcast([P, 2, 8]), ALU.mult))
            step(dve.tensor_tensor(r2(176, 8), r2(176, 8), w2.unsqueeze(2).to_broadcast([P, 2, 8]), ALU.mult))
            step(dve.tensor_tensor(r2(160, 8), r2(160, 8), r2(176, 8), ALU.add))
            for g in range(NG):
                step(dve.tensor_tensor(combine[:, :, 8 * g:8 * g + 8], r2(160, 8),
                                       r2(72, 4)[:, :, g:g + 1].to_broadcast([P, 2, 8]), ALU.mult))
            def slots(layer, ne, cap, extra):
                for t in range(TT):
                    for half in range(2):
                        b = group()
                        freed_wait(dve.tensor_copy(h_tok[:, t, half * CH:(half + 1) * CH], ps[:, b, :]))
                step(dve.tensor_scalar(chosen_by[:, :, 0:ne], combine[:, :, 0:ne], 0.0, None, ALU.is_gt),
                     "chosen_ready")
                b = group()
                step(dve.memset(slot_of[:, :, ne:ne + extra], -1.0), wait=False)
                step(dve.memset(combine[:, :, ne:ne + extra], 0.0))
                place = slot_of[:, :, 0:ne]
                step(dve.tensor_scalar(place, ps[:, b, 0:2 * ne].rearrange("p (a b) -> p a b", a=2), 1.0, None, ALU.add))
                step(dve.tensor_tensor(place, place, chosen_by[:, :, 0:ne], ALU.mult))
                step(dve.tensor_scalar(place, place, -1.0, None, ALU.add))
                freed_wait(dve.tensor_reduce(stat[:, 112:113], ps[:, b, 2 * ne:3 * ne], AX, ALU.max))
                step(dve.tensor_scalar(fits[:, layer:layer + 1], stat[:, 112:113], float(cap), None, ALU.is_le))
                step(dve.memset(tok[:, :, :], 0.0))
                step(dve.memset(y_slot, 0.0))
                step(dve.memset(pickT, 0.0), "fits_ready")

            slots(0, NE1, CAP1, EPG1)
            step(dve.memset(stat[:, 120:121], 0.0), "mix_ready")
            dve.memset(ada_part[:, 0:1], 0.0).then_inc(ada_step, 1)
            dve.wait_ge(ada_step, 1)

            def ada_sums(i):
                dve.wait_ge(ada_full, i * 16 + 16)
                for k in range(KD):
                    if k == 0:
                        ins = dve.tensor_scalar(ada_part, ada_w[:, 0, :], csT[:, 1, 0:1], None, ALU.mult)
                    else:
                        ins = dve.scalar_tensor_tensor(out=ada_part, in0=ada_w[:, k, :], scalar=csT[:, 1, k:k + 1],
                                                       in1=ada_part, op0=ALU.mult, op1=ALU.add)
                    ins.then_inc(ada_step, 1)
                    dve.wait_ge(ada_step, i * KD + (k + 2))

            def ada_mod(i, bank):
                n = AW // P
                return dve.tensor_tensor(modT[:, 1:3, :].rearrange("p m c -> p (m c)")[:, bass.ds(i * n, n)],
                                         ps[:, bank, 0:n], colB[:, bass.ds(i * n, n)], ALU.add)

            def unit(q, u, j, e, last, weight, seq, first):
                dve.wait_ge(q["silu_done"], u + 1)
                dve.wait_ge(q["up_full"], u + 1)
                if not first:
                    dve.wait_ge(ring_free, seq - 1)
                dve.tensor_tensor(hid[:, j % 2, :], silu_g[:, j % 2, :], ps[:, 5 + 2 * (j % 2), :], ALU.mult)\
                   .then_inc(q["hid_ready"], 1)
                if last:
                    dve.wait_ge(ring_free, seq + 1)
                    for t in range(TT):
                        for half in range(2):
                            dst = tok[:, t, half * CH:(half + 1) * CH]
                            if weight is None:
                                ins = dve.tensor_copy(dst, ps[:, 2 * t + half, :])
                            else:
                                ins = dve.scalar_tensor_tensor(out=dst, in0=ps[:, 2 * t + half, :], scalar=weight(t),
                                                               in1=dst, op0=ALU.mult, op1=ALU.add)
                    ins.then_inc(q["y_free"], 1)
                    dve.wait_ge(q["y_free"], e + 1)

            def experts_all(q, n, body_e, units, seq, with_ada):
                body = body_e * units
                with dve.Fori(0, n) as i:
                    for j in range(body):
                        e = i * body_e + j // units
                        unit(q, i * body + j, j, e, j % units == units - 1,
                             lambda t: combine[:, t, bass.ds(e, 1)], i * body + (seq + j), j < 2)
                    if with_ada:
                        ada_sums(i)
                        dve.wait_ge(q["side_full"], i + 1)
                        ada_mod(i, 0).then_inc(q["side_free"], 1)

            def experts_slots(q, n, body_e, units, seq, cap, epg, with_ada):
                body, groups = body_e * units, body_e // epg
                per = epg * units
                steps = 8 * groups

                def side(i, k):
                    dve.wait_ge(q["side_full"], i * steps + (k + 1))

                def side_free(ins, i, k):
                    ins.then_inc(q["side_free"], 1)
                    dve.wait_ge(q["side_free"], i * steps + (k + 1))

                def build(g):
                    for a_ in range(epg):
                        for t in range(TT):
                            place = slot_of[:, t, bass.ds(g * epg + a_, 1)]
                            weight = combine[:, t, bass.ds(g * epg + a_, 1)]
                            dve.tensor_scalar(pickw[:, t, a_ * cap:(a_ + 1) * cap], iota[:, 0:cap], place, weight,
                                              ALU.is_equal, ALU.mult)
                            ins = dve.tensor_scalar(pick[:, t, a_ * cap:(a_ + 1) * cap], iota[:, 0:cap], place, None,
                                                    ALU.is_equal)
                    ins.then_inc(q["pick_ready"], 1)

                def dispatched(i, k):
                    for c in range(2):
                        side(i, k + c)
                        side_free(dve.tensor_copy(xT[:, 4 * c:4 * c + 4, :],
                                                  ps[:, (k + c) % 4, :].rearrange("p (a b) -> p a b", a=4)), i, k + c)

                def combined(i, k):
                    for c in range(4):
                        t, half = c // 2, c % 2
                        side(i, k + c)
                        dst = tok[:, t, half * CH:(half + 1) * CH]
                        side_free(dve.tensor_tensor(dst, dst, ps[:, (k + c) % 4, :], ALU.add), i, k + c)

                build(0)
                dispatched(0, 0)
                dve.memset(stat[:, 127:128], 0.0).then_inc(q["y_free"], 1)
                with dve.Fori(0, n) as i:
                    for gi in range(groups):
                        k = 2 + 8 * gi
                        for jj in range(per):
                            j = gi * per + jj
                            dve.wait_ge(q["silu_done"], i * body + (j + 1))
                            dve.wait_ge(ring_free, i * body + (seq + j - 1))
                            dve.tensor_tensor(hid[:, j % 2, 0:2 * cap], silu_g[:, j % 2, 0:2 * cap],
                                              ps[:, 6 + j % 2, 2 * cap:4 * cap], ALU.mult).then_inc(q["hid_ready"], 1)
                            if jj == 1:
                                combined(i, k)
                                if with_ada:
                                    side(i, k + 4)
                                    side_free(dve.tensor_copy(pickT, ps[:, (k + 4) % 4, 0:TT * P]
                                                              .rearrange("p (a b) -> p a b", a=TT)), i, k + 4)
                                else:
                                    for t in range(TT):
                                        side(i, k + 4 + t)
                                        side_free(dve.tensor_copy(pickT[:, t, :], ps[:, (k + 4 + t) % 4, 0:P]),
                                                  i, k + 4 + t)
                                build(i * groups + (gi + 1))
                                if with_ada:
                                    ada_sums(i)
                        if with_ada:
                            side(i, k + 5)
                            side_free(ada_mod(i, (k + 5) % 4), i, k + 5)
                        dispatched(i, k + 6)
                        dve.wait_ge(ring_free, i * body + (seq + (gi + 1) * per))
                        for half in range(2):
                            ins = dve.tensor_copy(y_slot[:, half * CH:(half + 1) * CH], ps[:, 4 + half, :])
                        ins.then_inc(q["y_free"], 1)
                combined(n - 1, 2 + 8 * groups)

            def experts(layer, q, n, body_e, units, seq, cap, epg, with_ada):
                flag = dve.value_load(fits[0:1, layer:layer + 1], min_val=0, max_val=1)
                with dve.If(flag == 1):
                    experts_slots(q, n, body_e, units, seq, cap, epg, with_ada)
                with dve.Else():
                    experts_all(q, n, body_e, units, seq, with_ada)

            experts(0, PH[0], NE1 // 2, 2, U1, MOE1_SEQ, CAP1, EPG1, True)

            def gated_ffn(keep):
                for t in range(TT):
                    step(dve.tensor_tensor(tok[:, t, :], tok[:, t, :], gB[:, 1, :], ALU.mult))
                    step(dve.scalar_tensor_tensor(out=x[:, t, :], in0=x[:, t, :], scalar=keep, in1=tok[:, t, :],
                                                  op0=ALU.mult, op1=ALU.add))

            gated_ffn(1.0)
            rms(x)
            step(dve.memset(stat[:, 126:127], 0.0))
            rows_got += 16
            dve.wait_ge(got_rows, rows_got)
            for t in range(TT):
                step(dve.tensor_tensor(x[:, t, :], x[:, t, :], rowB[:, 0, :], ALU.mult))
            step(dve.memset(stat[:, 121:122], 0.0), "rows_used")
            dve.wait_ge(v_free, nv[0])
            for layer in range(2):
                step(dve.tensor_scalar(scale_col[:, :], sec(SC1, layer + 1), 1.0, None, ALU.add), "tokens_normed")
                transposed(scale_col, sec(SH1, layer + 1))
                gates(layer + 1, 1.0)
                for g in range(2):
                    b = group()
                    freed(dve.tensor_copy(cbT[:, 2 * g:2 * g + 2, :], bank2(b)))
                for g in range(2):
                    b = group()
                    freed_wait(dve.tensor_copy(ccT[:, 2 * g:2 * g + 2, :], bank2(b)))
                step(dve.memset(zT[:, :, 0:2], 0.0))
                for g in range(2):
                    b = group()
                    freed_wait(dve.tensor_tensor(zT[:, 2 * g:2 * g + 2, 2:T + 2], ccT[:, 2 * g:2 * g + 2, :], bank2(b), ALU.mult))
                for dst in (q2T, k2T, k_tok):
                    b = group()
                    freed_wait(dve.tensor_copy(dst, bank2(b)))
                for t in range(TT):
                    b = group()
                    freed_wait(dve.tensor_copy(v2[:, t, :], ps[:, b, :]))
                b = group()
                freed_wait(dve.tensor_copy(glT, ps[0:16, b, 0:T]))
                step(dve.memset(stat[:, 124:125], 0.0), "glow_ready", wait=False)
                for c in range(4):
                    for tap in range(3):
                        w = colA[:, 80 + layer * 12 + tap * 4 + c:81 + layer * 12 + tap * 4 + c]
                        src = zT[:, c, tap:tap + T]
                        if tap == 0:
                            step(dve.tensor_scalar(conv[:, c, :], src, w, None, ALU.mult))
                        else:
                            step(dve.scalar_tensor_tensor(out=conv[:, c, :], in0=src, scalar=w, in1=conv[:, c, :],
                                                          op0=ALU.mult, op1=ALU.add))
                step(dve.tensor_tensor(cbT, cbT, conv, ALU.mult))
                b = group()
                dve.wait_ge(got_layer, 48 * (layer + 1))
                freed_wait(dve.tensor_tensor(gk, bank2(b), gkbB[:, :].unsqueeze(1).to_broadcast([P, 2, T]), ALU.add))
                step(dve.tensor_scalar(gkt, gk, -1.0, None, ALU.mult))
                step(dve.tensor_tensor(gku, gk, gkt, ALU.min), "gk_abs")
                dve.wait_ge(gk_e, layer + 1)
                step(dve.tensor_scalar(gku, gku, 1.0, None, ALU.add), "gk_exp1")
                dve.wait_ge(gk_l, layer + 1)
                step(dve.scalar_tensor_tensor(out=gk, in0=gk, scalar=0.0, in1=gku, op0=ALU.min, op1=ALU.subtract))
                step(dve.tensor_scalar(gk, gk, 1.0 / GK_DIV, GK_MIN, ALU.mult, ALU.max), "gk_ready")
                dve.wait_ge(a_free, 12 + 4 * (layer + 1))
                step(dve.scalar_tensor_tensor(out=q2T, in0=q2T, scalar=DK ** -0.5, in1=ebT, op0=ALU.mult, op1=ALU.mult),
                     wait=False)
                step(dve.tensor_tensor(k2T, k2T, enbT, ALU.mult), wait=False)
                step(dve.tensor_tensor(k_tok, k_tok, er, ALU.mult), "gla_in")
                for par in range(2):
                    b = group()
                    freed_wait(dve.tensor_tensor(scT[:, par, :, :], bank4(b),
                                                 chunk_triu[:, :].unsqueeze(1).to_broadcast([P, 4, P]), ALU.mult))
                step(dve.memset(stat[:, 125:126], 0.0), "gla_scores", wait=False)
                for c in range(3):
                    b = group()
                    if c == 0:
                        freed_wait(dve.tensor_copy(state[:, 0, :, :], ps[:, b, 0:2 * DV].rearrange("p (a b) -> p a b", a=2)))
                    else:
                        for f in range(2):
                            ins = dve.scalar_tensor_tensor(out=state[:, c, f, :], in0=state[:, c - 1, f, :],
                                                           scalar=ebT[:, f, c * CK + CK - 1:c * CK + CK],
                                                           in1=ps[:, b, f * DV:(f + 1) * DV], op0=ALU.mult, op1=ALU.add)
                        freed_wait(ins)
                step(dve.memset(stat[:, 126:127], 0.0), "states_ready", wait=False)
                dve.wait_ge(a_free, 12 + 4 * (layer + 1))
                for par in range(2):
                    b = group()
                    freed_wait(dve.tensor_copy(
                        o_tok.rearrange("p t (f a v) -> p t f a v", a=2, v=DV)[:, :, :, par, :],
                        ps[:, b, :].rearrange("p (t f v) -> p t f v", t=2, f=2)))
                for t in range(TT):
                    o4 = o_tok[:, t, :].rearrange("p (a b) -> p a b", a=4)
                    t4 = tok[:, t, 0:512].rearrange("p (a b) -> p a b", a=4)
                    step(dve.tensor_tensor(t4, o4, o4, ALU.mult))
                    step(dve.tensor_reduce(stat[:, 0:4], t4, AX, ALU.add))
                    rstd(stat[:, 4:8], stat[:, 0:4], 1.0 / DV, RMS_EPS)
                    step(dve.tensor_tensor(o4, o4, stat[:, 4:8].unsqueeze(2).to_broadcast([P, 4, DV]), ALU.mult))
                    step(dve.tensor_tensor(o4, o4, glnB[:, :].unsqueeze(1).to_broadcast([P, 4, DV]), ALU.mult))
                    step(dve.tensor_tensor(o_tok[:, t, :], o_tok[:, t, :], sg_tok[:, t, :], ALU.mult), "o_normed")
                step(dve.memset(stat[:, 121:122], 0.0), "layer_used")
                for t in range(TT):
                    b = group()
                    freed_wait(dve.tensor_copy(ygT[:, :, t * P:(t + 1) * P], bank4(b)))
                step(dve.memset(stat[:, 120:121], 0.0), "ya_ready", wait=False)
                gated_sum(0, ALPHA, W_OUT_CUTS[layer])

                def norm_x():
                    nonlocal rows_got
                    rows_got += 32
                    dve.wait_ge(got_rows, rows_got)
                    layer_norm(D, x, rowB[:, 0, :], rowB[:, 1, :], LN_EPS)

                norm_x()
                step(dve.memset(stat[:, 121:122], 0.0), "rows_used")
                step(dve.tensor_scalar(scale_col[:, :], sec(SC2, layer + 1), 1.0, None, ALU.add), "tokens_normed")
                transposed(scale_col, sec(SH2, layer + 1))
                if layer == 0:
                    step(dve.memset(stat[:, 124:125], 0.0), "mix_ready")
                    for j in range(U2):
                        unit(PH[1], j, j, 0, j == U2 - 1, None, FFN_SEQ + j, j < 2)
                else:
                    b = group()
                    freed_wait(dve.tensor_copy(r2(0, 8), ps[:, b, 0:16].rearrange("p (a b) -> p a b", a=2)))
                    m1, m2 = rt[:, 310:312], rt[:, 312:314]
                    top2(r2(0, 8), r2(160, 8), r2(176, 8), r2(192, 8), m1, m2, sc2)
                    step(dve.tensor_tensor(rt[:, 16:18], m2, m1, ALU.subtract), wait=False)
                    step(dve.memset(rt[:, 18:32], 0.0), "router_logits")
                    dve.wait_ge(router_exp, 2)
                    e2 = rt[:, 32:34]
                    step(dve.tensor_scalar(w1, e2, 1.0, None, ALU.add))
                    step(dve.reciprocal(w1, w1))
                    step(dve.tensor_tensor(w2, e2, w1, ALU.mult))
                    step(dve.tensor_tensor(r2(160, 8), r2(160, 8), w1.unsqueeze(2).to_broadcast([P, 2, 8]), ALU.mult))
                    step(dve.tensor_tensor(r2(176, 8), r2(176, 8), w2.unsqueeze(2).to_broadcast([P, 2, 8]), ALU.mult))
                    step(dve.tensor_tensor(combine[:, :, 0:8], r2(160, 8), r2(176, 8), ALU.add))
                    slots(1, NE2, CAP2, EPG2)
                    step(dve.memset(stat[:, 120:121], 0.0), "mix_ready")
                    experts(1, PH[2], NE2 // 4, 4, U2, MOE2_SEQ, CAP2, EPG2, False)
                gated_ffn(ALPHA)
                norm_x()
                if layer == 0:
                    step(dve.memset(stat[:, 121:122], 0.0), "rows_used")
                else:
                    step(dve.memset(stat[:, 121:122], 0.0), "x_ready")

        @block.tensor
        def _(pe):
            r = Ring()
            nv, na = [0], [0]
            owed = [False]

            def mm(*args, **kw):
                ins = pe.matmul(*args, **kw)
                if owed[0]:
                    ins.then_inc(ring_free, 1)
                    owed[0] = False
                    return None
                return ins

            def tr(*args):
                ins = pe.transpose(*args)
                if owed[0]:
                    ins.then_inc(ring_free, 1)
                    owed[0] = False
                    return None
                return ins

            def free():
                assert not owed[0]
                owed[0] = True

            def gv_():
                if nv[0] >= 4:
                    pe.wait_ge(v_free, nv[0] - 3)
                nv[0] += 1
                return (nv[0] - 1) % 4

            def ga_():
                if na[0] >= 4:
                    pe.wait_ge(a_free, na[0] - 3)
                na[0] += 1
                return 4 + (na[0] - 1) % 4

            def take(dmas=1):
                s, full, _ = r.take(dmas)
                pe.wait_ge(ring_full[s], full)
                return s

            def transposes(src, n, rows_, bank, rid=P):
                for j in range(n):
                    last = tr(ps[0:P, bank, j * rows_:(j + 1) * rows_], src(j), ident[0:rid, 0:rid])
                return last

            pe.wait_ge(consts_ready, 1)
            pe.wait_ge(got_vec, 112)
            pe.transpose(ps[:, gv_(), 0:104], vecA, ident[0:104, 0:104]).then_inc(v_full, 1)
            pe.transpose(ps[:, gv_(), 0:96], vecB, ident[0:96, 0:96]).then_inc(v_full, 1)
            pe.wait_ge(got_spatial, 32)
            for t in range(2):
                transposes(lambda j: prob[:, 0, (2 * t + j) * P:(2 * t + j + 1) * P], 2, P, gv_()).then_inc(v_full, 1)

            def ada():
                vb = nv[0]
                assert r.seq == 0 and vb == 4
                with pe.Fori(0, 3) as h:
                    for c in range(4):
                        pe.wait_ge(H["ada_mac"], h * (4 * KD) + (c + 1) * KD)
                        pe.wait_ge(v_free, h * 4 + (vb + c - 3))
                        for f in range(4):
                            last = mm(ps[:, c, f:f + 1], ada_sum[c % 2][:, f * P:(f + 1) * P], ones[:, 0:1],
                                      start=True, stop=True)
                        last.then_inc(ring_free, 1)
                nv[0] += 12
                for _ in range(12):
                    r.take(1)

            def gates(m):
                for g in range(2):
                    pe.wait_ge(H["gate_cols"], 2 * m + g + 1)
                    for half in range(2):
                        bank = gv_()
                        for j in range(4):
                            last = mm(ps[:, bank, j * P:(j + 1) * P], colsB[:, 4 * half + j, :], ident[:, :],
                                      start=True, stop=True)
                        last.then_inc(v_full, 1)

            def token_transposes(src):
                for t in range(TT):
                    for half in range(2):
                        transposes(lambda j: src[:, t, (4 * half + j) * P:(4 * half + j + 1) * P], 4, P, gv_())\
                            .then_inc(v_full, 1)

            def feature_major(w, rhs, tiles, bank, cols=lambda f: f * P, kt=KD, m=P):
                for i, f in enumerate(tiles):
                    for k in range(kt):
                        last = mm(ps[0:m, bank, i * T:(i + 1) * T], w[:, k, cols(f):cols(f) + m], rhs(k),
                                         start=(k == 0), stop=(k == kt - 1))
                return last

            def token_major(lhs, w, t, c0, c1, bank, at=0, kt=KD):
                for k in range(kt):
                    last = mm(ps[:, bank, at:at + c1 - c0], lhs(k, t), w[:, k, c0:c1],
                                     start=(k == 0), stop=(k == kt - 1))
                return last

            def h_rhs(k):
                return hT[:, k, :]

            def h_lhs(k, t):
                return hT[:, k, t * P:(t + 1) * P]

            ada()
            pe.wait_ge(H["tokens_normed"], 1)
            token_transposes(tok)
            pe.wait_ge(H["hT_ready"], 1)
            gates(0)
            s = take(10)
            w = slot(s, KD, 768)
            for g in range(2):
                feature_major(w, h_rhs, (2 * g, 2 * g + 1), gv_()).then_inc(v_full, 1)
            feature_major(w, h_rhs, (4,), gv_()).then_inc(v_full, 1)
            bank = gv_()
            token_major(h_lhs, w, 0, 640, 768, bank)
            token_major(h_lhs, w, 1, 640, 768, bank, at=P).then_inc(v_full, 1)
            free()
            s = take()
            for g in range(2):
                feature_major(slot(s, KD, CH), h_rhs, (2 * g, 2 * g + 1), ga_()).then_inc(a_full, 1)
            free()
            s = take()
            for t in range(TT):
                token_major(h_lhs, slot(s, KD, CH), t, 0, CH, ga_()).then_inc(a_full, 1)
            free()
            for c in range(4):
                s = take()
                for g in range(2):
                    feature_major(slot(s, KD, CH), h_rhs, (2 * g, 2 * g + 1), ga_()).then_inc(a_full, 1)
                free()
            pe.wait_ge(H["vn_ready"], 1)
            for t in range(TT):
                bank = gv_()
                for g in range(4):
                    last = mm(ps[:, bank, g * P:(g + 1) * P], gv[:, t, g * P:(g + 1) * P], wsT[:, g, :],
                                     start=True, stop=True)
                last.then_inc(v_full, 1)
            pe.wait_ge(H["qkv_ready"], 1)
            for g in range(6):
                nh = 4 if g < 2 else 2
                h0 = 4 * g if g < 2 else 2 * (g - 2)
                bank = gv_()
                for i in range(nh):
                    hd = h0 + i
                    base, j = HD * (hd // GROUP_HEADS), hd % GROUP_HEADS
                    q0, keys = (0, P) if g < 2 else (P, T)
                    last = mm(ps[:, bank, i * keys:(i + 1) * keys], qT[base:base + HD, j, q0:q0 + P],
                                     kT[base:base + HD, 0:keys], start=True, stop=True)
                last.then_inc(v_full, 1)
            for g in range(6):
                pe.wait_ge(H["probs_ready"], g + 1)
                transposes(lambda j: prob[:, g, j * P:(j + 1) * P], 4, P, gv_()).then_inc(v_full, 1)
            for blk in range(2):
                pe.wait_ge(H["pT_ready"], 2 + 4 * blk)
                bank = gv_()
                for hd in range(HEADS):
                    base, kv = HD * (hd % 2), hd // GROUP_HEADS
                    dst = ps[base:base + HD, bank, (hd // 2) * P:(hd // 2 + 1) * P]
                    if blk == 0:
                        last = mm(dst, v_tok[:, 0, kv * HD:(kv + 1) * HD],
                                         pT[:, hd // 4, (hd % 4) * P:(hd % 4 + 1) * P], start=True, stop=True)
                    else:
                        for kt in range(2):
                            at = (2 * (hd % 2) + kt) * P
                            last = mm(dst, v_tok[:, kt, kv * HD:(kv + 1) * HD],
                                             pT[:, 2 + hd // 2, at:at + P], start=(kt == 0), stop=(kt == 1))
                last.then_inc(v_full, 1)
            pe.wait_ge(H["ya_ready"], 1)
            for c in range(2):
                s = take()
                for g in range(2):
                    feature_major(slot(s, 4, CH), lambda k: yaT[:, k, :], (2 * g, 2 * g + 1), gv_(), kt=4)\
                        .then_inc(v_full, 1)
                free()
            pe.wait_ge(H["yb_ready"], 1)
            s = take()
            for g in range(4):
                feature_major(slot(s, 4, D), lambda k: guT[:, k, :], (2 * g, 2 * g + 1), gv_(), kt=4).then_inc(v_full, 1)
            free()
            pe.wait_ge(H["merged_ready"], 4)
            for c in range(2):
                s = take()
                for t in range(TT):
                    token_major(lambda k, t: gaT[:, k, t * P:(t + 1) * P], slot(s, KD, CH), t, 0, CH, gv_())\
                        .then_inc(v_full, 1)
                free()
            pe.wait_ge(H["tokens_normed"], 2)
            token_transposes(tok)
            pe.wait_ge(H["hT_ready"], 2)
            pe.wait_ge(got_router, 80)

            def router(w, n):
                bank = gv_()
                for t in range(TT):
                    last = token_major(h_lhs, w, t, 0, n, bank, at=t * n)
                last.then_inc(v_full, 1)

            router(w_router, 36)

            def unit_in(q, s, u, full, j, first):
                pe.wait_ge(ring_full[s], full)
                if not first:
                    pe.wait_ge(q["hid_ready"], u - 1)
                b = 4 + 2 * (j % 2)
                feature_major(slot_gate(s), h_rhs, (0, 1), b).then_inc(q["gate_full"], 1)
                feature_major(slot_up(s), h_rhs, (0, 1), b + 1).then_inc(q["up_full"], 1)

            def unit_down(q, s, u, j, opens, closes):
                pe.wait_ge(q["hid_ready"], u + 1)
                for t in range(TT):
                    for half in range(2):
                        for f in range(2):
                            last = mm(ps[:, 2 * t + half, :], hid[:, j % 2, f * T + t * P:f * T + (t + 1) * P],
                                      slot_down(s)[:, f, half * CH:(half + 1) * CH],
                                      start=(opens and f == 0), stop=(closes and f == 1))
                last.then_inc(ring_free, 1)

            def ada_columns(q, i, bank):
                pe.wait_ge(ada_step, i * KD + (KD + 1))
                for f in range(AW // P):
                    last = mm(ps[:, bank, f:f + 1], ada_part[:, f * P:(f + 1) * P], ones[:, 0:1], start=True, stop=True)
                last.then_inc(q["side_full"], 1)

            def experts_all(q, at, n, body_e, units, with_ada):
                body = body_e * units
                with pe.Fori(0, n) as i:
                    def down(j):
                        k = j % units
                        unit_down(q, j % SLOTS, i * body + j, j, k == 0, k == units - 1)
                    for j in range(body):
                        s, full, _ = at(i, j)
                        unit_in(q, s, i * body + j, full, j, j < 2)
                        if j:
                            down(j - 1)
                    down(body - 1)
                    if with_ada:
                        pe.wait_ge(q["y_free"], i * body_e + body_e)
                        ada_columns(q, i, 0)
                pe.wait_ge(q["y_free"], n * body_e)
                if with_ada:
                    pe.wait_ge(q["side_free"], n)

            def experts_slots(q, at, n, body_e, units, cap, epg, with_ada):
                body, groups, per = body_e * units, body_e // epg, epg * units
                steps = 8 * groups

                def side(i, k):
                    pe.wait_ge(q["side_free"], i * steps + (k - 3))
                    return k % 4

                def dispatch(i, k, picks, first=False):
                    pe.wait_ge(q["pick_ready"], picks)
                    for c in range(2):
                        bank = c if first else side(i, k + c)
                        for kt in range(4):
                            for t in range(TT):
                                last = mm(ps[:, bank, kt * SL:(kt + 1) * SL],
                                          h_tok[:, t, (4 * c + kt) * P:(4 * c + kt + 1) * P], pick[:, t, :],
                                          start=(t == 0), stop=(t == TT - 1))
                        last.then_inc(q["side_full"], 1)

                def combine_(i, k, done, first=False):
                    pe.wait_ge(q["y_free"], done)
                    for c in range(4):
                        t, half = c // 2, c % 2
                        bank = c + 2 if first and c < 2 else side(i, k + c)
                        mm(ps[:, bank, :], pickT[:, t, :], y_slot[:, half * CH:(half + 1) * CH],
                           start=True, stop=True).then_inc(q["side_full"], 1)

                def gate_up(i, j, full):
                    s, a_ = j % SLOTS, (j % per) // units
                    pe.wait_ge(ring_full[s], full)
                    if j >= 2:
                        pe.wait_ge(q["hid_ready"], i * body + (j - 1))
                    for part, w in enumerate((slot_gate(s), slot_up(s))):
                        for f in range(2):
                            o = (2 * part + f) * cap
                            for k in range(KD):
                                last = mm(ps[:, 6 + j % 2, o:o + cap], w[:, k, f * P:(f + 1) * P],
                                          xT[:, k, a_ * cap:(a_ + 1) * cap], start=(k == 0), stop=(k == KD - 1))
                    last.then_inc(q["unit_full"], 1)

                def down(i, j):
                    a_, k = (j % per) // units, j % units
                    pe.wait_ge(q["hid_ready"], i * body + (j + 1))
                    for half in range(2):
                        for f in range(2):
                            last = mm(ps[a_ * cap:(a_ + 1) * cap, 4 + half, :], hid[:, j % 2, f * cap:(f + 1) * cap],
                                      slot_down(j % SLOTS)[:, f, half * CH:(half + 1) * CH],
                                      start=(k == 0 and f == 0), stop=(k == units - 1 and f == 1))
                    last.then_inc(ring_free, 1)

                dispatch(0, 0, 1, first=True)
                with pe.Fori(0, n) as i:
                    for gi in range(groups):
                        k = 2 + 8 * gi
                        pe.wait_ge(q["side_free"], i * steps + k)
                        for jj in range(per):
                            j = gi * per + jj
                            gate_up(i, j, at(i, j)[1])
                            if jj == 1:
                                pe.wait_ge(q["y_free"], i * groups + (gi + 1))
                            if jj:
                                down(i, j - 1)
                            if jj == 1:
                                combine_(i, k, i * groups + (gi + 1), first=gi == 0)
                                if with_ada:
                                    bank = side(i, k + 4)
                                    for t in range(TT):
                                        last = tr(ps[:, bank, t * P:(t + 1) * P], pickw[:, t, :], ident[:, :])
                                    last.then_inc(q["side_full"], 1)
                                else:
                                    for t in range(TT):
                                        tr(ps[:, side(i, k + 4 + t), 0:P], pickw[:, t, :], ident[:, :])\
                                            .then_inc(q["side_full"], 1)
                            if jj == per - 1:
                                if with_ada:
                                    ada_columns(q, i, side(i, k + 5))
                                dispatch(i, k + 6, i * groups + (gi + 2))
                        down(i, gi * per + per - 1)
                combine_(n - 1, 2 + 8 * groups, n * groups + 1)
                pe.wait_ge(q["side_free"], 2 + 8 * groups * n + 4)

            def experts(layer, q, n, body_e, units, cap, epg, with_ada):
                at = r.loop(n, body_e * units)
                assert not owed[0]
                pe.wait_ge(v_free, nv[0])
                pe.wait_ge(a_free, na[0])
                flag = pe.value_load(fits[0:1, layer:layer + 1], min_val=0, max_val=1)
                with pe.If(flag == 1):
                    experts_slots(q, at, n, body_e, units, cap, epg, with_ada)
                with pe.Else():
                    experts_all(q, at, n, body_e, units, with_ada)

            def find_slots(layer, ne):
                for t in range(TT):
                    for half in range(2):
                        bank = gv_()
                        for j in range(4):
                            last = tr(ps[:, bank, j * P:(j + 1) * P], hT[:, 4 * half + j, t * P:(t + 1) * P], ident[:, :])
                        last.then_inc(v_full, 1)
                pe.wait_ge(H["chosen_ready"], layer + 1)
                bank = gv_()
                mm(ps[:, bank, 0:ne], strict[:, :], chosen_by[:, 0, 0:ne], start=True, stop=True)
                for at, m1 in ((ne, strict), (2 * ne, ones)):
                    mm(ps[:, bank, at:at + ne], ones[:, :], chosen_by[:, 0, 0:ne], start=True, stop=False)
                    last = mm(ps[:, bank, at:at + ne], m1[:, :], chosen_by[:, 1, 0:ne], start=False, stop=True)
                last.then_inc(v_full, 1)

            find_slots(0, NE1)
            pe.wait_ge(H["mix_ready"], 1)
            experts(0, PH[0], NE1 // 2, 2, U1, CAP1, EPG1, True)
            for layer in range(2):
                pe.wait_ge(H["rows_used"], 2 + 2 * layer)
                pe.wait_ge(H["tokens_normed"], 3 + 2 * layer)
                token_transposes(x)
                pe.wait_ge(H["hT_ready"], 3 + 2 * layer)
                gates(layer + 1)
                for c in range(3):
                    s = take()
                    for g in range(2):
                        feature_major(slot(s, KD, CH), h_rhs, (2 * g, 2 * g + 1), gv_()).then_inc(v_full, 1)
                    free()
                s = take()
                w = slot(s, KD, CH)
                for g in range(2):
                    feature_major(w, h_rhs, (2 * g, 2 * g + 1), gv_()).then_inc(v_full, 1)
                bank = gv_()
                token_major(h_lhs, w, 0, T, 2 * T, bank)
                token_major(h_lhs, w, 1, T, 2 * T, bank, at=T).then_inc(v_full, 1)
                free()
                s = take()
                for t in range(TT):
                    token_major(h_lhs, slot(s, KD, CH), t, 0, CH, gv_()).then_inc(v_full, 1)
                free()
                s = take()
                w = slot(s, KD, 528)
                for t in range(TT):
                    token_major(h_lhs, w, t, 0, CH, ga_()).then_inc(a_full, 1)
                feature_major(w, h_rhs, (0,), gv_(), cols=lambda f: CH, m=16).then_inc(v_full, 1)
                free()
                pe.wait_ge(H["glow_ready"], layer + 1)
                pe.wait_ge(got_layer, 48 * (layer + 1))
                bank = gv_()
                for t in range(TT):
                    last = mm(ps[:, bank, t * T:(t + 1) * T], glT[:, t * P:(t + 1) * P], gkw2[:, :],
                                     start=True, stop=True)
                last.then_inc(v_full, 1)
                pe.wait_ge(H["gk_ready"], layer + 1)
                bank = ga_()
                for f in range(2):
                    for t in range(TT):
                        last = mm(ps[:, bank, f * T + t * P:f * T + (t + 1) * P], gk[:, t, f * P:(f + 1) * P],
                                         chunk_triu[:, :], start=True, stop=True)
                last.then_inc(a_full, 1)
                bank = ga_()
                for t in range(TT):
                    last = mm(ps[:, bank, t * T:(t + 1) * T], chunk_tril[:, :], gk[:, t, :], start=True, stop=True)
                last.then_inc(a_full, 1)
                pe.wait_ge(H["gla_in"], layer + 1)
                for par in range(2):
                    base, bank = DK * par, gv_()
                    for t in range(TT):
                        for f in range(2):
                            at = (2 * t + f) * P
                            last = mm(ps[:, bank, at:at + P], k2T[base:base + DK, f, t * P:(t + 1) * P],
                                             q2T[base:base + DK, f, t * P:(t + 1) * P], start=True, stop=True)
                    last.then_inc(v_full, 1)
                for c in range(3):
                    bank, rb, t = gv_(), CK * (c % 2), c // 2
                    for hd in range(GH):
                        ob, f = DK * (hd % 2), hd // 2
                        last = mm(ps[ob:ob + DK, bank, f * DV:(f + 1) * DV],
                                         k_tok[rb:rb + CK, t, hd * DK:(hd + 1) * DK],
                                         v2[rb:rb + CK, t, hd * DV:(hd + 1) * DV], start=True, stop=True)
                    last.then_inc(v_full, 1)
                pe.wait_ge(H["gla_scores"], layer + 1)
                pe.wait_ge(H["states_ready"], layer + 1)
                for par in range(2):
                    base, bank = DK * par, gv_()
                    for t in range(TT):
                        for f in range(2):
                            at = (2 * t + f) * P
                            hd = 2 * f + par
                            last = mm(ps[:, bank, at:at + DV], scT[:, par, 2 * t + f, :],
                                      v2[:, t, hd * DV:(hd + 1) * DV], start=True, stop=False,
                                      skip_group_check=True)
                            for c in (2 * t, 2 * t + 1):
                                if c == 0:
                                    continue
                                ob = CK * (c % 2)
                                last = mm(ps[ob:ob + CK, bank, at:at + DV],
                                          q2T[base:base + DK, f, c * CK:(c + 1) * CK],
                                          state[base:base + DK, c - 1, f, :], start=False, stop=True,
                                          skip_group_check=True)
                    last.then_inc(v_full, 1)
                for t in range(TT):
                    pe.wait_ge(H["o_normed"], 2 * layer + t + 1)
                    transposes(lambda j: o_tok[:, t, j * P:(j + 1) * P], 4, P, gv_()).then_inc(v_full, 1)
                pe.wait_ge(H["ya_ready"], 2 + layer)
                for c0, c1 in W_OUT_CUTS[layer]:
                    s = take()
                    for t in range(TT):
                        token_major(lambda k, t: (cbT if k < 4 else ygT)[:, k % 4, t * P:(t + 1) * P],
                                    slot(s, KD, c1 - c0), t, 0, c1 - c0, gv_()).then_inc(v_full, 1)
                    free()
                pe.wait_ge(H["tokens_normed"], 4 + 2 * layer)
                token_transposes(x)
                pe.wait_ge(H["hT_ready"], 4 + 2 * layer)
                if layer == 0:
                    pe.wait_ge(H["mix_ready"], 2)
                    pe.wait_ge(v_free, nv[0])
                    pe.wait_ge(a_free, na[0])
                    prev = None
                    for j in range(U2):
                        s, full, _ = r.take(3)
                        unit_in(PH[1], s, j, full, j, j < 2)
                        if prev is not None:
                            unit_down(PH[1], prev, j - 1, j - 1, j == 1, False)
                        prev = s
                    unit_down(PH[1], prev, U2 - 1, U2 - 1, False, True)
                    pe.wait_ge(PH[1]["y_free"], 1)
                else:
                    router(w_router2, NE2)
                    find_slots(1, NE2)
                    pe.wait_ge(H["mix_ready"], 3)
                    experts(1, PH[2], NE2 // 4, 4, U2, CAP2, EPG2, False)


_INS = ['x', 'c', 'positions', 'rel_bias', 'w_ada', 'b_ada', 'norm1_g', 'w_in', 'sinks', 'gm_ln_g', 'gm_ln_b',
        'gm_w_s', 'gm_b_s', 'p_a', 'p_b', 'w_o', 'norm2_g', 'w_router_g', 'b_router_g', 'w_router_e', 'b_router_e',
        'w_gate', 'w_up', 'w_down', 'final_g', 'c_2', 'ada_w_2', 'ada_b_2', 'w_in_2', 'conv_w_2', 'gk_w2_2',
        'gk_b_2', 'gla_norm_w_2', 'w_out_2', 'ln1_g_2', 'ln1_b_2', 'ln2_g_2', 'ln2_b_2', 'ffn_w_gate_2',
        'ffn_w_up_2', 'ffn_w_down_2', 'router_w_2', 'moe_w_gate_2', 'moe_w_up_2', 'moe_w_down_2']


def kernel(**inputs):
    import numpy as _np
    import concourse.bacc as _bacc
    from concourse import mybir as _mybir
    from concourse.bass_utils import run_bass_kernel_spmd as _run

    nc = _bacc.Bacc("TRN2", target_bir_lowering=False, num_devices=1)
    arrays, aps = {}, {}
    for name in _INS:
        v = _np.ascontiguousarray(inputs[name])
        arrays[f"in_{name}_dram"] = v
        aps[name] = nc.dram_tensor(f"in_{name}_dram", v.shape, _mybir.dt.from_np(v.dtype), kind="ExternalInput").ap()
    out = nc.dram_tensor("out_0_dram", (1, T, D), F32, kind="ExternalOutput").ap()
    build(nc, aps, out)
    r = _run(nc, [arrays], core_ids=[0])
    return r.results[0]["out_0_dram"]
```

```python
from contextlib import ExitStack
import math

import numpy as np
import concourse.bass as bass
from concourse import mybir

F32 = mybir.dt.float32
I32 = mybir.dt.int32
ALU = mybir.AluOpType
ACT = mybir.ActivationFunctionType
AX = mybir.AxisListType.X

P = 128
D = 1024
KD = D // P
T = 256
TT = T // P
SLOTS = 4
FU = 256
SLOT = 3 * FU * KD
CH = 512

HEADS, HD, GROUP_HEADS = 8, 64, 4
POOL_HEADS = (6, 7)
ATTN_SCALE = HD ** -0.5
BUCKETS, MAX_EXACT, MAX_DISTANCE = 32, 16, 128
NEG = -1e30
RMS_EPS = 1e-6
LN_EPS = 1e-5

NG, EG = 4, 8
NE1 = NG * EG
F1 = 512
U1 = F1 // FU
NE2 = 8
F2 = 2816
U2 = F2 // FU

SL = 128
AW = 6 * D * 2 // (NE1 // 2)
CAP1, CAP2 = 64, 128
EPG1, EPG2 = SL // CAP1, SL // CAP2

GH, DK, DV, CK = 4, 64, 128, 64
GK_DIV, GK_MIN = 16.0, -1.0
ALPHA = 4.0 ** 0.25

SH1, SC1, G1, SH2, SC2, G2 = range(6)
SQ, SK, SV, SGU, SGV, SGA, SGB = 0, 512, 640, 768, 1280, 1792, 2816


def bucket_starts():
    n = np.arange(1, 4 * MAX_DISTANCE)
    large = MAX_EXACT + (np.log(n.astype(np.float32) / np.float32(MAX_EXACT))
                         / np.float32(math.log(MAX_DISTANCE / MAX_EXACT))
                         * np.float32(BUCKETS - MAX_EXACT)).astype(np.int32)
    bucket = np.where(n < MAX_EXACT, n, np.minimum(large, BUCKETS - 1))
    return [float(n[np.argmax(bucket >= b)]) for b in range(1, BUCKETS)]


class Count:

    def __init__(self, sem):
        self.sem, self.n = sem, 0


class Ring:

    def __init__(self):
        self.seq, self.loads = 0, [0] * SLOTS

    def take(self, dmas):
        i, s = self.seq, self.seq % SLOTS
        self.seq += 1
        self.loads[s] += 16 * dmas
        return s, self.loads[s], (i - SLOTS + 1 if i >= SLOTS else None)

    def loop(self, n, body):
        base, loads = self.seq, list(self.loads)
        per = 3 * 16 * (body // SLOTS)
        self.seq += n * body
        self.loads = [v + per * n for v in self.loads]

        def at(r, j):
            s = j % SLOTS
            return s, r * per + (loads[s] + 48 * (j // SLOTS + 1)), r * body + (base + j - SLOTS + 1)
        return at


def build(nc, a, out):
    with ExitStack() as ctx:
        def sb(name, shape, dt=F32):
            return ctx.enter_context(nc.sbuf_tensor(name, shape, dt))

        def sem(name):
            return ctx.enter_context(nc.semaphore(name))

        ring = sb("ring", [P, SLOTS, SLOT])
        x = sb("x", [P, TT, D])
        hT = sb("hT", [P, KD, T])
        tok = sb("tok", [P, TT, D])
        colsB = sb("colsB", [P, KD, P])
        gB = sb("gB", [P, 2, D])
        rowB = sb("rowB", [P, 2, D])
        arena = sb("arena", [P, 13824])
        ident = sb("ident", [P, P])
        triu = sb("triu", [P, P])
        chunk_triu = sb("chunk_triu", [P, P])
        chunk_tril = sb("chunk_tril", [P, P])
        colA = sb("colA", [P, 104])
        colB = sb("colB", [P, 96])
        csT = sb("csT", [P, 2, KD])
        modT = sb("modT", [P, 3, 48])
        scale_col = sb("scale_col", [P, KD])
        shift_col = sb("shift_col", [P, KD])
        colC = sb("colC", [P, 5, KD])
        w_router = sb("w_router", [P, KD, 36])
        b_router = sb("b_router", [P, 36])
        w_router2 = sb("w_router2", [P, KD, NE2])
        poscol = sb("poscol", [P, TT], I32)
        relD = sb("relD", [P, BUCKETS * HEADS])
        starts = sb("starts", [P, BUCKETS + 1])
        sinkB = sb("sinkB", [P, HEADS])
        stat = sb("stat", [P, 128])
        newton = sb("newton", [P, 24])
        rt = sb("rt", [P, 320])
        vecC = rt[0:5 * KD, 0:P]
        rev = sb("rev", [P, 8])
        combine = sb("combine", [P, TT, NE1 + EPG1])
        slot_of = sb("slot_of", [P, TT, NE1 + EPG1])
        chosen_by = sb("chosen_by", [P, TT, NE1])
        fits = sb("fits", [P, 2], I32)
        iota = sb("iota", [P, SL])
        ones = sb("ones", [P, P])
        strict = sb("strict", [P, P])
        gkw2 = sb("gkw2", [16, T])
        gkbB = sb("gkbB", [P, T])
        glnB = sb("glnB", [P, DV])

        def view(start, *shape):
            n = int(np.prod(shape))
            v = arena[:, start:start + n]
            if len(shape) == 2:
                v = v.rearrange("p (a b) -> p a b", a=shape[0])
            if len(shape) == 3:
                v = v.rearrange("p (a b c) -> p a b c", a=shape[0], b=shape[1])
            return v

        bias = view(0, HEADS, 384)
        pT = view(0, 6, CH)
        prob = view(3072, 6, CH)
        qT = view(6144, 4, T)
        yaT = view(6144, 4, T)
        kT = view(7168, T)
        v_tok = view(7424, TT, P)
        gv = view(7680, TT, 512)
        guT = view(8704, 4, T)
        gaT = view(9728, KD, T)
        gbT = view(11776, KD, T)
        dist = view(3584, 384)
        mask_v = view(3968, 384)
        mask_w = rowB[:, 1, 0:384]
        pool_add = (view(4352, 384), view(4736, 384))
        ada_row = view(7680, 2, CH)
        posf = view(10880, 4, T)
        posrow = view(11904, T).bitcast(I32)
        relB = view(12160, BUCKETS * HEADS)
        wsT = view(5120, 4, P)
        bsB = view(5632, 4, P)
        vecA = arena[0:104, 13312:13440]
        vecB = arena[0:96, 13440:13568]
        cbT = view(0, 4, T)
        ccT = view(1024, 4, T)
        ygT = view(1024, 4, T)
        zT = view(2048, 4, T + 2)
        q2T = view(3080, 2, T)
        k2T = view(3592, 2, T)
        k_tok = view(4104, TT, T)
        v2 = view(4616, TT, 512)
        sg_tok = view(5640, TT, 512)
        gk = view(6664, TT, T)
        gkt = view(7176, TT, T)
        gku = view(7688, TT, T)
        ebT = view(8200, 2, T)
        enbT = view(8712, 2, T)
        er = view(9224, TT, T)
        scT = view(9736, 2, 4, P)
        state = view(10760, 3, 2, DV)
        o_tok = view(11528, TT, 512)
        conv = view(11528, 4, T)
        glT = arena[0:16, 12552:12552 + T]
        silu_g = view(0, 2, 2 * T)
        hid = view(1024, 2, 2 * T)

        h_tok = view(2048, TT, D)
        xT = view(4096, KD, SL)
        y_slot = view(5120, D)
        pick = view(6144, TT, SL)
        pickw = view(6400, TT, SL)
        pickT = view(6656, TT, P)
        ada_w = view(6912, KD, AW)
        ada_part = view(13056, AW)

        ps = ctx.enter_context(nc.psum_tensor("ps", [P, 8, CH], F32))

        ring_full = [sem(f"ring_full{i}") for i in range(SLOTS)]
        ring_free = sem("ring_free")
        v_full, v_free, a_full, a_free = sem("v_full"), sem("v_free"), sem("a_full"), sem("a_free")
        PH = [{n: sem(f"{n}_{ph}") for n in ("gate_full", "up_full", "silu_done", "hid_ready", "y_free", "unit_full",
                                             "side_full", "side_free", "pick_ready")}
              for ph in ("moe1", "ffn", "moe2")]
        ada_full, ada_step, row_copied, mod_full = (
            sem(s) for s in ("ada_full", "ada_step", "row_copied", "mod_full"))
        got_x, got_vec, got_pos, got_spatial, got_router, got_rows = (
            sem(s) for s in ("got_x", "got_vec", "got_pos", "got_spatial", "got_router", "got_rows"))
        got_layer, got_gains = sem("got_layer"), sem("got_gains")
        stored = sem("stored")
        consts_step, first_consts, bias_started, consts_ready = (
            sem(s) for s in ("consts_step", "first_consts", "bias_started", "consts_ready"))
        dist_ready, bias_pool, pool_step = sem("dist_ready"), sem("bias_pool"), sem("pool_step")
        act_step = sem("act_step")
        names = ("cols_ready", "gate_cols", "tokens_normed", "hT_ready", "qkv_ready", "vn_ready", "scores_ready",
                 "probs_ready", "pT_ready", "ya_ready", "yb_ready", "merged_ready", "rows_used",
                 "router_logits", "glow_ready", "gk_abs", "gk_exp1", "gk_ready", "gla_in", "gla_scores",
                 "states_ready", "o_normed", "mix_ready", "sink_ready", "dve_step", "layer_used", "x_ready", "mod_read", "scale_ready", "chosen_ready", "fits_ready")
        S = {s: Count(sem(s)) for s in names}
        H = {s: c.sem for s, c in S.items()}
        silu_c, exps_done, sink_exp, gk_e, gk_l, router_exp = (
            sem(s) for s in ("silu_c", "exps_done", "sink_exp", "gk_e", "gk_l", "router_exp"))

        block = ctx.enter_context(nc.Block())

        def chunk_k(w, c0, c1):
            return w.rearrange("(k p) n -> p k n", p=P)[:, :, c0:c1]

        def slot(s, kt, cols):
            return ring[:, s, 0:kt * cols].rearrange("p (k n) -> p k n", k=kt)

        def slot_gate(s):
            return ring[:, s, 0:KD * FU].rearrange("p (k n) -> p k n", k=KD)

        def slot_up(s):
            return ring[:, s, KD * FU:2 * KD * FU].rearrange("p (k n) -> p k n", k=KD)

        def slot_down(s):
            return ring[:, s, 2 * KD * FU:3 * KD * FU].rearrange("p (k n) -> p k n", k=2)

        MOE1_SEQ = 12 + 7 + 5
        FFN_SEQ = MOE1_SEQ + NE1 * U1 + 9
        MOE2_SEQ = FFN_SEQ + U2 + 8
        C_IN2 = [(0, 512), (512, 1024), (1024, 1536), (1536, 2048), (2048, 2560), (2560, 3088)]
        A_FIRST = 2 + 12 + 2 + 4
        A_DECAYS = [A_FIRST + 12 * layer + 6 for layer in range(2)]
        W_OUT_CUTS = [[(0, 512), (512, 768), (768, 1024)], [(0, 512), (512, 1024)]]

        @block.sync
        def _(sp):
            r = Ring()

            def load(parts):
                s, _, free = r.take(len(parts))
                if free is not None:
                    sp.wait_ge(ring_free, free)
                at = 0
                for src in parts:
                    kt, n = src.shape[1], src.shape[2]
                    sp.dma_start(ring[:, s, at:at + kt * n].rearrange("p (k n) -> p k n", k=kt), src)\
                      .then_inc(ring_full[s], 16)
                    at += kt * n

            def load_ada(w):
                wk = w.rearrange("(k p) n -> p k n", p=P)
                for c in range(4):
                    load([wk[:, :, c * CH:(c + 1) * CH]])
                    if c == 0:
                        sp.wait_ge(got_vec, 112)
                        sp.wait_ge(got_pos, 64)
                        sp.wait_ge(got_spatial, 32)
                with sp.Fori(0, 2) as h:
                    for c in range(4):
                        sp.wait_ge(ring_free, h * SLOTS + (c + 1))
                        sp.dma_start(slot(c, KD, CH), wk[:, :, bass.ds(h * (4 * CH) + (4 + c) * CH, CH)])\
                          .then_inc(ring_full[c], 16)
                for _ in range(8):
                    r.take(1)

            def load_units(gate, up, down, c0):
                return [chunk_k(gate, c0, c0 + FU), chunk_k(up, c0, c0 + FU),
                        down[c0:c0 + FU, :].rearrange("(k p) n -> p k n", p=P)]

            def load_experts(gate, up, down, ne, body_e, units, ada=None):
                body = body_e * units
                at = r.loop(ne // body_e, body)
                with sp.Fori(0, ne // body_e) as i:
                    for j in range(body):
                        if ada is not None and j == 2:
                            sp.wait_ge(ada_step, i * KD + 1)
                            rounds = 6 * D // AW
                            src = ada[bass.ds(i // rounds, 1), :, bass.ds((i % rounds) * AW, AW)]
                            sp.dma_start(ada_w, src.rearrange("o (k p) n -> p (o k) n", p=P)).then_inc(ada_full, 16)
                        s, _, free = at(i, j)
                        e, c0 = i * body_e + j // units, (j % units) * FU
                        sp.wait_ge(ring_free, free)
                        g = gate[bass.ds(e, 1), :, c0:c0 + FU].rearrange("o (k p) n -> p (o k) n", p=P)
                        u = up[bass.ds(e, 1), :, c0:c0 + FU].rearrange("o (k p) n -> p (o k) n", p=P)
                        d = down[bass.ds(e, 1), c0:c0 + FU, :].rearrange("o (k p) n -> p (o k) n", p=P)
                        sp.dma_start(slot_gate(s), g).then_inc(ring_full[s], 16)
                        sp.dma_start(slot_up(s), u).then_inc(ring_full[s], 16)
                        sp.dma_start(slot_down(s), d).then_inc(ring_full[s], 16)

            load_ada(a["w_ada"][0])
            w = a["w_in"][0]
            s, _, free = r.take(10)
            sp.wait_ge(ring_free, free)
            for half in range(2):
                q_src = w[:, half * 256:half * 256 + 256].rearrange("(k p) (j d) -> p j k d", p=P, d=HD)
                for j in range(4):
                    sp.dma_start(slot(s, KD, 768)[:, :, j * P + half * HD:j * P + half * HD + HD], q_src[:, j])\
                      .then_inc(ring_full[s], 16)
            sp.dma_start(slot(s, KD, 768)[:, :, 512:640], chunk_k(w, SK, SV)).then_inc(ring_full[s], 16)
            sp.dma_start(slot(s, KD, 768)[:, :, 640:768], chunk_k(w, SV, SGU)).then_inc(ring_full[s], 16)
            for c in range(6):
                load([chunk_k(w, SGU + c * CH, SGU + (c + 1) * CH)])
            load([chunk_k(a["p_b"][0], 0, D)])
            for c in range(2):
                load([chunk_k(a["p_a"][0], c * CH, (c + 1) * CH)])
            for c in range(2):
                load([chunk_k(a["w_o"][0], c * CH, (c + 1) * CH)])
            load_experts(a["w_gate"][0], a["w_up"][0], a["w_down"][0], NE1, 2, U1, a["ada_w_2"])
            for layer in range(2):
                w = a["w_in_2"][layer]
                for c0, c1 in C_IN2:
                    load([chunk_k(w, c0, c1)])
                for c0, c1 in W_OUT_CUTS[layer]:
                    load([chunk_k(a["w_out_2"][layer], c0, c1)])
                if layer == 0:
                    for u in range(U2):
                        load(load_units(a["ffn_w_gate_2"][0], a["ffn_w_up_2"][0], a["ffn_w_down_2"][0], u * FU))
            load_experts(a["moe_w_gate_2"][0], a["moe_w_up_2"][0], a["moe_w_down_2"][0], NE2, 4, U2)
            sp.wait_ge(H["x_ready"], 1)
            sp.dma_start(out[0].rearrange("(t p) d -> p t d", p=P), x[:, :, :]).then_inc(stored, 16)
            sp.wait_ge(stored, 16)

        @block.gpsimd
        def _(pool):
            n = [0]

            def const(ins, wait=True):
                n[0] += 1
                ins.then_inc(consts_step, 1)
                if wait:
                    pool.wait_ge(consts_step, n[0])

            const(pool.memset(ident[:, :], 0.0))
            const(pool.affine_select(out=ident[:, :], in_=ident[:, :], compare_op=ALU.not_equal, fill=1.0, base=0,
                                     pattern=[[-1, P]], channel_multiplier=1), wait=False)
            const(pool.memset(ones[:, :], 1.0), wait=False)
            const(pool.memset(triu[:, :], 1.0))
            const(pool.affine_select(out=triu[:, :], in_=triu[:, :], compare_op=ALU.is_ge, fill=0.0, base=0,
                                     pattern=[[1, P]], channel_multiplier=-1))
            pool.memset(stat[:, 117:118], 1.0).then_inc(first_consts, 1)
            const(pool.iota(starts[:, 0:MAX_EXACT], [[1, MAX_EXACT]], base=0, channel_multiplier=0,
                            allow_small_or_imprecise_dtypes=True))
            const(pool.memset(starts[:, 0:1], -3e38), wait=False)
            for b, s in enumerate(bucket_starts()[MAX_EXACT - 1:] + [3e38]):
                const(pool.memset(starts[:, b + MAX_EXACT:b + MAX_EXACT + 1], s), wait=False)
            const(pool.memset(bias[:, :, :], 0.0))
            for h in range(HEADS):
                for part in range(3):
                    lo = part * P
                    sign, base = (-1, 0) if part != 1 else (1, -1)
                    const(pool.affine_select(out=bias[:, h, lo:lo + P], in_=bias[:, h, lo:lo + P],
                                             compare_op=ALU.is_ge, fill=NEG, base=base,
                                             pattern=[[sign, P]], channel_multiplier=-sign), wait=False)
            pool.wait_ge(consts_step, n[0])
            pool.memset(stat[:, 118:119], 1.0).then_inc(bias_started, 1)
            pool.dma_start(rowB[:, 0, 0:512], a["gm_ln_g"][0].partition_broadcast(P)).then_inc(got_rows, 16)
            pool.dma_start(rowB[:, 0, 512:1024], a["gm_ln_b"][0].partition_broadcast(P)).then_inc(got_rows, 16)
            const(pool.memset(chunk_triu[:, :], 1.0))
            const(pool.affine_select(out=chunk_triu[:, :], in_=chunk_triu[:, :], compare_op=ALU.is_ge, fill=0.0,
                                     base=0, pattern=[[1, P]], channel_multiplier=-1))
            const(pool.memset(chunk_triu[0:CK, CK:P], 0.0))
            const(pool.memset(chunk_tril[:, :], 1.0))
            const(pool.affine_select(out=chunk_tril[:, :], in_=chunk_tril[:, :], compare_op=ALU.is_ge, fill=0.0,
                                     base=-1, pattern=[[-1, P]], channel_multiplier=1))
            const(pool.memset(chunk_tril[CK:P, 0:CK], 0.0))
            const(pool.iota(iota[:, :], [[1, SL]], base=0, channel_multiplier=0, allow_small_or_imprecise_dtypes=True))
            const(pool.memset(strict[:, :], 1.0))
            const(pool.affine_select(out=strict[:, :], in_=strict[:, :], compare_op=ALU.is_ge, fill=0.0, base=-1,
                                     pattern=[[1, P]], channel_multiplier=-1))
            for i in range(8):
                const(pool.memset(rev[:, i:i + 1], float(8 - i)), wait=False)
            pool.wait_ge(consts_step, n[0])
            pool.memset(stat[:, 127:128], 1.0).then_inc(consts_ready, 1)
            pool.wait_ge(dist_ready, 1)
            k = 0
            for b in range(BUCKETS):
                for i, h in enumerate(POOL_HEADS):
                    ins = pool.tensor_scalar(pool_add[i], dist, starts[:, b:b + 1],
                                             relD[:, b * HEADS + h:b * HEADS + h + 1], ALU.is_ge, ALU.mult)
                ins.then_inc(pool_step, 1)
                k += 1
                pool.wait_ge(pool_step, k)
                for i, h in enumerate(POOL_HEADS):
                    ins = pool.tensor_tensor(bias[:, h, :], bias[:, h, :], pool_add[i], ALU.add)
                ins.then_inc(pool_step, 1)
                k += 1
                pool.wait_ge(pool_step, k)
            pool.memset(stat[:, 119:120], 0.0).then_inc(bias_pool, 1)
            pool.wait_ge(H["rows_used"], 1)
            pool.dma_start(rowB[:, 0, :], a["final_g"].partition_broadcast(P)).then_inc(got_rows, 16)
            used = 2
            for layer in range(2):
                for one, two in ((a["ln1_g_2"][layer], a["ln1_b_2"][layer]),
                                 (a["ln2_g_2"][layer], a["ln2_b_2"][layer])):
                    pool.wait_ge(H["rows_used"], used)
                    for i, v in enumerate((one, two)):
                        pool.dma_start(rowB[:, i, :], v.partition_broadcast(P)).then_inc(got_rows, 16)
                    used += 1

        @block.scalar
        def _(act):
            def load(dst, src, s):
                act.dma_start(dst, src, allow_slow_non_contiguous=True).then_inc(s, 16)

            load(vecA[0:48, :], a["b_ada"][0].rearrange("(r p) -> r p", p=P), got_vec)
            load(vecA[48:56, :], a["c"][0].rearrange("(r p) -> r p", p=P), got_vec)
            load(vecA[56:64, :], a["norm1_g"][0].rearrange("(r p) -> r p", p=P), got_vec)
            load(vecA[64:72, :], a["norm2_g"][0].rearrange("(r p) -> r p", p=P), got_vec)
            load(vecA[72:80, :], a["c_2"][0].rearrange("(r p) -> r p", p=P), got_vec)
            load(vecA[80:104, :], a["conv_w_2"].rearrange("l j (r p) -> (l j r) p", p=P), got_vec)
            load(vecB, a["ada_b_2"].rearrange("l (r p) -> (l r) p", p=P), got_vec)
            load(posrow, a["positions"][0].partition_broadcast(P), got_pos)
            load(poscol[:, :], a["positions"][0].rearrange("(t p) -> p t", p=P), got_pos)
            load(relB, a["rel_bias"].rearrange("b h -> (b h)").partition_broadcast(P), got_pos)
            load(sinkB[:, :], a["sinks"][0].partition_broadcast(P), got_pos)
            ws = prob[:, 0, :].rearrange("p (g s) -> p g s", g=4)
            load(ws, a["gm_w_s"][0].rearrange("g t s -> t g s"), got_spatial)
            load(bsB[:, :, :], a["gm_b_s"][0].rearrange("g t -> (g t)").partition_broadcast(P)
                 .rearrange("p (g t) -> p g t", g=4), got_spatial)
            load(x[:, :, :], a["x"][0].rearrange("(t p) d -> p t d", p=P), got_x)
            for i, v in enumerate((a["final_g"], a["ln1_g_2"][0], a["ln1_b_2"][0], a["ln2_g_2"][0], a["ln2_b_2"][0])):
                load(vecC[i * KD:(i + 1) * KD, :], v.rearrange("(r p) -> r p", p=P), got_gains)
            load(w_router[:, :, 0:4], a["w_router_g"][0].rearrange("(k p) n -> p k n", p=P), got_router)
            load(w_router[:, :, 4:36], a["w_router_e"][0].rearrange("(k p) n -> p k n", p=P), got_router)
            load(w_router2[:, :, :], a["router_w_2"][0].rearrange("(k p) n -> p k n", p=P), got_router)
            load(b_router[:, 0:4], a["b_router_g"][0].partition_broadcast(P), got_router)
            load(b_router[:, 4:36], a["b_router_e"][0].partition_broadcast(P), got_router)

            def load_layer(layer):
                load(gkw2[:, :], a["gk_w2_2"][layer], got_layer)
                load(gkbB[:, :], a["gk_b_2"][layer].partition_broadcast(P), got_layer)
                load(glnB[:, :], a["gla_norm_w_2"][layer].partition_broadcast(P), got_layer)

            load_layer(0)
            na = [0]

            def group():
                act.wait_ge(a_full, na[0] + 1)
                na[0] += 1
                return 4 + (na[0] - 1) % 4

            act.wait_ge(H["cols_ready"], 1)
            act.activation(csT[:, 0, :], colA[:, 48:56], ACT.Silu)
            act.activation(csT[:, 1, :], colA[:, 72:80], ACT.Silu).then_inc(silu_c, 1)
            def transposed(shift):
                for t in range(TT):
                    bank = group()
                    for j in range(4):
                        ins = act.activation(hT[:, 4 + j, t * P:(t + 1) * P], ps[:, bank, j * P:(j + 1) * P],
                                             ACT.Identity, scale=scale_col[:, 4 + j:5 + j], bias=shift[:, 4 + j:5 + j])
                    ins.then_inc(a_free, 1)

            def sec(s, m=0):
                return modT[:, m, s * KD:(s + 1) * KD]

            with act.Fori(0, 3) as h:
                for c in range(4):
                    act.wait_ge(ring_free, h * 4 + (c + 1))
                    act.activation(ada_row[0:1, c % 2, :], ps[0:1, 4 + c % 2, :], ACT.Copy).then_inc(row_copied, 1)
            act.wait_ge(H["scale_ready"], 1)
            transposed(sec(SH1))
            for g in range(2):
                bank = group()
                act.activation(guT[:, 2 * g:2 * g + 2, :], ps[:, bank, :].rearrange("p (a b) -> p a b", a=2),
                               ACT.Gelu_apprx_tanh).then_inc(a_free, 1)
            for t in range(TT):
                bank = group()
                act.activation(gv[:, t, :], ps[:, bank, :], ACT.Gelu_apprx_tanh).then_inc(a_free, 1)
            for g in range(4):
                bank = group()
                act.activation(gaT[:, 2 * g:2 * g + 2, :], ps[:, bank, :].rearrange("p (a b) -> p a b", a=2),
                               ACT.Sigmoid).then_inc(a_free, 1)
            for g in range(4):
                bank = group()
                act.activation(gbT[:, 2 * g:2 * g + 2, :], ps[:, bank, :].rearrange("p (a b) -> p a b", a=2),
                               ACT.Sigmoid).then_inc(a_free, 1)
            for g in range(6):
                act.wait_ge(H["scores_ready"], g + 1)
                nh = 4 if g < 2 else 2
                st = 4 * g if g < 2 else 8 + 2 * (g - 2)
                for i in range(nh):
                    w = CH // nh
                    ins = act.activation(prob[:, g, i * w:(i + 1) * w], prob[:, g, i * w:(i + 1) * w], ACT.Exp,
                                         bias=stat[:, 16 + st + i:17 + st + i], accum_out=stat[:, 32 + st + i:33 + st + i])
                ins.then_inc(exps_done, 1)
            act.wait_ge(H["sink_ready"], 1)
            act.activation(stat[:, 64:80], stat[:, 48:64], ACT.Exp).then_inc(sink_exp, 1)

            def experts(layer, q, n, body, cap):
                act.wait_ge(H["fits_ready"], layer + 1)
                flag = act.value_load(fits[0:1, layer:layer + 1], min_val=0, max_val=1)
                with act.If(flag == 1):
                    with act.Fori(0, n) as i:
                        for j in range(body):
                            act.wait_ge(q["unit_full"], i * body + (j + 1))
                            if j >= 2:
                                act.wait_ge(q["hid_ready"], i * body + (j - 1))
                            act.activation(silu_g[:, j % 2, 0:2 * cap], ps[:, 6 + j % 2, 0:2 * cap], ACT.Silu)\
                               .then_inc(q["silu_done"], 1)
                with act.Else():
                    with act.Fori(0, n) as i:
                        for j in range(body):
                            act.wait_ge(q["gate_full"], i * body + (j + 1))
                            if j >= 2:
                                act.wait_ge(q["hid_ready"], i * body + (j - 1))
                            act.activation(silu_g[:, j % 2, :], ps[:, 4 + 2 * (j % 2), :], ACT.Silu)\
                               .then_inc(q["silu_done"], 1)

            def tokens():
                for t in range(TT):
                    for half in range(2):
                        bank = group()
                        act.activation(h_tok[:, t, half * CH:(half + 1) * CH], ps[:, bank, :], ACT.Copy)\
                           .then_inc(a_free, 1)

            act.wait_ge(H["scale_ready"], 2)
            transposed(sec(SH2))
            tokens()
            act.wait_ge(H["router_logits"], 1)
            act.activation(rt[:, 96:104], rt[:, 80:88], ACT.Exp)
            act.activation(rt[:, 144:160], rt[:, 128:144], ACT.Exp).then_inc(router_exp, 1)
            act.wait_ge(H["mix_ready"], 1)
            experts(0, PH[0], NE1 // 2, 2 * U1, CAP1)
            for layer in range(2):
                transposed(shift_col)
                for t in range(TT):
                    bank = group()
                    act.activation(sg_tok[:, t, :], ps[:, bank, :], ACT.Silu).then_inc(a_free, 1)
                act.wait_ge(H["gk_abs"], layer + 1)
                act.activation(gku, gku, ACT.Exp).then_inc(gk_e, 1)
                act.wait_ge(H["gk_exp1"], layer + 1)
                act.activation(gku, gku, ACT.Ln).then_inc(gk_l, 1)
                bank = group()
                act.activation(ebT, ps[:, bank, :].rearrange("p (a b) -> p a b", a=2), ACT.Exp).then_inc(act_step, 1)
                act.wait_ge(act_step, layer + 1)
                act.activation(enbT, ps[:, bank, :].rearrange("p (a b) -> p a b", a=2), ACT.Exp, scale=-1.0)\
                   .then_inc(a_free, 1)
                bank = group()
                act.activation(er, ps[:, bank, :].rearrange("p (a b) -> p a b", a=2), ACT.Exp).then_inc(a_free, 1)
                na[0] += 4
                if layer == 0:
                    act.wait_ge(H["layer_used"], 1)
                    load_layer(1)
                    transposed(shift_col)
                    act.wait_ge(H["mix_ready"], 2)
                    for j in range(U2):
                        act.wait_ge(PH[1]["gate_full"], j + 1)
                        if j >= 2:
                            act.wait_ge(PH[1]["hid_ready"], j - 1)
                        act.activation(silu_g[:, j % 2, :], ps[:, 4 + 2 * (j % 2), :], ACT.Silu)\
                           .then_inc(PH[1]["silu_done"], 1)
                else:
                    transposed(sec(SH2, 2))
                    tokens()
                    act.wait_ge(H["router_logits"], 2)
                    act.activation(rt[:, 32:48], rt[:, 16:32], ACT.Exp).then_inc(router_exp, 1)
                    act.wait_ge(H["mix_ready"], 3)
                    experts(1, PH[2], NE2 // 4, 4 * U2, CAP2)

        @block.vector
        def _(dve):
            nv, nf = [0], [0]

            def step(ins, name="dve_step", wait=True):
                c = S[name]
                c.n += 1
                ins.then_inc(c.sem, 1)
                if wait:
                    dve.wait_ge(c.sem, c.n)
                return ins

            def group():
                nf[0] += 1
                dve.wait_ge(v_full, nf[0])
                nv[0] += 1
                return (nv[0] - 1) % 4

            def freed(ins):
                ins.then_inc(v_free, 1)

            def freed_wait(ins):
                ins.then_inc(v_free, 1)
                dve.wait_ge(v_free, nv[0])

            def bank2(b):
                return ps[:, b, :].rearrange("p (a b) -> p a b", a=2)

            def bank4(b):
                return ps[:, b, :].rearrange("p (a b) -> p a b", a=4)

            dve.wait_ge(got_pos, 64)
            posi = posf[:, 0:2, :].bitcast(I32)
            hi_r, lo_r = posi[:, 0, :], posi[:, 1, :]
            step(dve.tensor_scalar(hi_r, posrow, 16, None, ALU.arith_shift_right))
            step(dve.tensor_scalar(lo_r, posrow, 65535, None, ALU.bitwise_and))
            ci = stat[:, 0:4].bitcast(I32)
            step(dve.tensor_scalar(ci[:, 0:2], poscol[:, :], 16, None, ALU.arith_shift_right))
            step(dve.tensor_scalar(ci[:, 2:4], poscol[:, :], 65535, None, ALU.bitwise_and))
            step(dve.tensor_copy(stat[:, 4:8], ci))
            step(dve.tensor_copy(posf[:, 2, :], hi_r))
            step(dve.tensor_copy(posf[:, 3, :], lo_r))
            for t, (lo, w) in enumerate(((0, P), (P, T))):
                step(dve.tensor_scalar(dist[:, lo:lo + w], posf[:, 2, 0:w], stat[:, 4 + t:5 + t], -65536.0,
                                       ALU.subtract, ALU.mult))
                step(dve.tensor_scalar(mask_v[:, lo:lo + w], posf[:, 3, 0:w], stat[:, 6 + t:7 + t], -1.0,
                                       ALU.subtract, ALU.mult))
            step(dve.tensor_copy(relD[:, 0:HEADS], relB[:, 0:HEADS]), wait=False)
            step(dve.tensor_tensor(relD[:, HEADS:], relB[:, HEADS:], relB[:, 0:(BUCKETS - 1) * HEADS], ALU.subtract))
            dve.tensor_tensor(dist, dist, mask_v, ALU.add).then_inc(dist_ready, 1)
            dve.wait_ge(dist_ready, 1)
            b = group()
            freed(dve.tensor_copy(colA[:, :], ps[:, b, 0:104]))
            b = group()
            freed_wait(dve.tensor_copy(colB[:, :], ps[:, b, 0:96]))
            step(dve.tensor_copy(stat[:, 120:121], colA[:, 0:1]), "cols_ready")
            for t in range(2):
                b = group()
                freed_wait(dve.tensor_tensor(wsT[:, 2 * t:2 * t + 2, :], ps[:, b, 0:256].rearrange("p (a b) -> p a b", a=2),
                                             triu[:, :].unsqueeze(1).to_broadcast([P, 2, P]), ALU.mult))

            def gates(m, one):
                for g, s in enumerate((G1, G2)):
                    step(dve.tensor_copy(colsB[:, :, :], sec(s, m).unsqueeze(2).to_broadcast([P, KD, P])),
                         "gate_cols", wait=False)
                    for half in range(2):
                        b = group()
                        freed_wait(dve.tensor_scalar(gB[:, g, half * CH:(half + 1) * CH], ps[:, b, :], one, None, ALU.add))

            EARLY = 5

            def relative_bias(lo, hi):
                base = S["dve_step"].n

                def mask(bk, m):
                    dve.tensor_scalar(m, dist, starts[:, bass.ds(bk, 1)], None, ALU.is_ge).then_inc(H["dve_step"], 1)

                dve.tensor_scalar(mask_v, dist, starts[:, 4 * lo:4 * lo + 1], None, ALU.is_ge).then_inc(H["dve_step"], 1)
                base += 1
                with dve.Fori(0, hi - lo) as r_:
                    for i in range(4):
                        bk = r_ * 4 + (4 * lo + i)
                        m, other = ((mask_v, mask_w), (mask_w, mask_v))[i % 2]
                        dve.wait_ge(H["dve_step"], r_ * 8 + (base + 2 * i))
                        mask(bk + 1, other)
                        for hd in range(6):
                            ins = dve.scalar_tensor_tensor(
                                out=bias[:, hd, :], in0=m, scalar=relD[:, bass.ds(bk * HEADS + hd, 1)],
                                in1=bias[:, hd, :], op0=ALU.mult, op1=ALU.add)
                        ins.then_inc(H["dve_step"], 1)
                S["dve_step"].n = base + 8 * (hi - lo)
                dve.wait_ge(H["dve_step"], S["dve_step"].n)

            rows_got = 0

            def rstd(dst, src, mul, eps):
                n = src.shape[1]
                v, bits, t = (newton[:, 8 * i:8 * i + n] for i in range(3))
                step(dve.tensor_scalar(v, src, mul, eps, ALU.mult, ALU.add))
                step(dve.tensor_scalar(bits.bitcast(I32), v.bitcast(I32), 1, None, ALU.arith_shift_right))
                step(dve.tensor_scalar(dst.bitcast(I32), bits.bitcast(I32), -1.0, float(0x5f3759df),
                                       ALU.mult, ALU.add))
                for _ in range(3):
                    step(dve.tensor_tensor(t, dst, dst, ALU.mult))
                    step(dve.scalar_tensor_tensor(out=t, in0=t, scalar=-0.5, in1=v, op0=ALU.mult, op1=ALU.mult))
                    step(dve.scalar_tensor_tensor(out=dst, in0=t, scalar=1.5, in1=dst, op0=ALU.add, op1=ALU.mult))

            def rms(dst):
                for t in range(TT):
                    step(dve.tensor_tensor_reduce(out=tok[:, t, :], in0=x[:, t, :], in1=x[:, t, :], scale=1.0,
                                                  scalar=0.0, op0=ALU.mult, op1=ALU.add, accum_out=stat[:, 80 + t:81 + t]))
                rstd(stat[:, 82:84], stat[:, 80:82], 1.0 / D, RMS_EPS)
                for t in range(TT):
                    ins = dve.tensor_scalar(dst[:, t, :], x[:, t, :], stat[:, 82 + t:83 + t], None, ALU.mult)
                return ins

            def transposed(scale, shift):
                for t in range(TT):
                    b = group()
                    for k in range(4):
                        ins = dve.tensor_scalar(hT[:, k, t * P:(t + 1) * P], ps[:, b, k * P:(k + 1) * P],
                                                scale[:, k:k + 1], shift[:, k:k + 1], ALU.mult, ALU.add)
                    freed(ins)
                dve.wait_ge(v_free, nv[0])
                step(dve.memset(stat[:, 122:123], 0.0), "hT_ready", wait=False)

            def sec(s, m=0):
                return modT[:, m, s * KD:(s + 1) * KD]

            dve.wait_ge(bias_started, 1)
            dve.wait_ge(consts_ready, 1)
            relative_bias(0, EARLY)
            dve.wait_ge(got_x, 16)
            step(rms(tok), "tokens_normed", wait=False)
            dve.wait_ge(mod_full, 3)
            step(dve.tensor_tensor(modT[:, 0, :], ps[:, 7, 0:48], colA[:, 0:48], ALU.add), "mod_read")
            b = group()
            freed_wait(dve.tensor_copy(colC[:, :, :], ps[:, b, 0:5 * KD].rearrange("p (a b) -> p a b", a=5)))
            step(dve.scalar_tensor_tensor(out=scale_col[:, :], in0=sec(SC1), scalar=1.0, in1=colA[:, 56:64],
                                          op0=ALU.add, op1=ALU.mult), "scale_ready")
            transposed(scale_col, sec(SH1))
            gates(0, 0.0)
            for g in range(2):
                b = group()
                freed(dve.tensor_copy(qT[:, 2 * g:2 * g + 2, :], bank2(b)))
            b = group()
            freed(dve.tensor_copy(kT, ps[:, b, 0:T]))
            b = group()
            freed(dve.tensor_copy(v_tok, ps[:, b, 0:T].rearrange("p (a b) -> p a b", a=2)))
            dve.wait_ge(v_free, nv[0])
            step(dve.memset(stat[:, 123:124], 0.0), "qkv_ready", wait=False)

            def affine(v, g, b):
                for t in range(TT):
                    step(dve.tensor_tensor(v[:, t, :], v[:, t, :], g, ALU.mult))
                    if b is not None:
                        step(dve.tensor_tensor(v[:, t, :], v[:, t, :], b, ALU.add))

            def modulate(gain, shift, s_scale, s_shift, m):
                step(dve.tensor_scalar(scale_col[:, :], sec(s_scale, m), 1.0, None, ALU.add))
                if shift is None:
                    step(dve.tensor_copy(shift_col[:, :], sec(s_shift, m)))
                else:
                    step(dve.tensor_tensor(shift_col[:, :], scale_col[:, :], shift, ALU.mult))
                    step(dve.tensor_tensor(shift_col[:, :], shift_col[:, :], sec(s_shift, m), ALU.add))
                step(dve.tensor_tensor(scale_col[:, :], scale_col[:, :], gain, ALU.mult), "tokens_normed")
                transposed(scale_col, shift_col)

            def layer_norm(w, v, eps):
                m = w // 512
                for t in range(TT):
                    for i in range(m):
                        at = 84 + 12 * t + 6 * i
                        ins = dve.bn_stats(stat[:, at:at + 6], v[:, t, i * 512:(i + 1) * 512])
                step(ins)
                for t in range(TT):
                    ins = dve.bn_aggr(stat[:, 108 + 2 * t:110 + 2 * t], stat[:, 84 + 12 * t:84 + 12 * t + 6 * m]
                                      .rearrange("p (a b) -> p a b", b=6))
                step(ins)
                step(dve.tensor_copy(stat[:, 80:82], stat[:, 108:112].rearrange("p (a b) -> p a b", b=2)[:, :, 1]))
                rstd(stat[:, 82:84], stat[:, 80:82], 1.0, eps)
                for t in range(TT):
                    step(dve.tensor_scalar(v[:, t, :], v[:, t, :], stat[:, 108 + 2 * t:109 + 2 * t],
                                           stat[:, 82 + t:83 + t], ALU.subtract, ALU.mult))

            relative_bias(EARLY, EARLY + 1)
            dve.wait_ge(a_free, 6)
            rows_got += 32
            dve.wait_ge(got_rows, rows_got)
            layer_norm(512, gv, RMS_EPS)
            affine(gv, rowB[:, 0, 0:512], rowB[:, 0, 512:1024])
            step(dve.memset(stat[:, 124:125], 0.0), "vn_ready")
            step(dve.memset(stat[:, 121:122], 0.0), "rows_used")
            relative_bias(EARLY + 1, 8)
            dve.wait_ge(got_spatial, 32)
            for t in range(TT):
                b = group()
                step(dve.tensor_tensor(tok[:, t, 0:512].rearrange("p (a b) -> p a b", a=4), bank4(b), bsB[:, :, :], ALU.add))
                freed(dve.tensor_tensor(guT[:, :, t * P:(t + 1) * P], guT[:, :, t * P:(t + 1) * P],
                                        tok[:, t, 0:512].rearrange("p (a b) -> p a b", a=4), ALU.mult))
            dve.wait_ge(v_free, nv[0])
            step(dve.memset(stat[:, 125:126], 0.0), "yb_ready", wait=False)
            dve.wait_ge(bias_pool, 1)
            for g in range(6):
                nh = 4 if g < 2 else 2
                w = CH // nh
                h0 = 4 * g if g < 2 else 2 * (g - 2)
                st = h0 if g < 2 else 8 + h0
                bv = bias[:, h0:h0 + nh, 0:P] if g < 2 else bias[:, h0:h0 + nh, P:384]
                b = group()
                pg = prob[:, g, :].rearrange("p (a b) -> p a b", a=nh)
                freed_wait(dve.scalar_tensor_tensor(out=pg, in0=ps[:, b, :].rearrange("p (a b) -> p a b", a=nh),
                                                    scalar=ATTN_SCALE, in1=bv, op0=ALU.mult, op1=ALU.add))
                step(dve.tensor_reduce(stat[:, st:st + nh], pg, AX, ALU.max))
                step(dve.tensor_tensor(stat[:, st:st + nh], stat[:, st:st + nh], sinkB[:, h0:h0 + nh], ALU.max))
                step(dve.tensor_scalar(stat[:, 16 + st:16 + st + nh], stat[:, st:st + nh], -1.0, None, ALU.mult),
                     "scores_ready")
            for blk in range(2):
                ins = dve.tensor_tensor(stat[:, 48 + 8 * blk:56 + 8 * blk], sinkB[:, :],
                                        stat[:, 16 + 8 * blk:24 + 8 * blk], ALU.add)
            step(ins, "sink_ready")
            dve.wait_ge(a_free, 14)
            for g in range(4):
                b = group()
                freed(dve.tensor_tensor(gbT[:, 2 * g:2 * g + 2, :], gbT[:, 2 * g:2 * g + 2, :], bank2(b), ALU.mult))
            dve.wait_ge(sink_exp, 1)
            step(dve.tensor_tensor(stat[:, 32:48], stat[:, 32:48], stat[:, 64:80], ALU.add))
            step(dve.reciprocal(stat[:, 32:48], stat[:, 32:48]))
            for g in range(6):
                nh = 4 if g < 2 else 2
                st = 4 * g if g < 2 else 8 + 2 * (g - 2)
                pg = prob[:, g, :].rearrange("p (a b) -> p a b", a=nh)
                step(dve.tensor_tensor(pg, pg, stat[:, 32 + st:32 + st + nh].unsqueeze(2)
                                       .to_broadcast([P, nh, CH // nh]), ALU.mult), "probs_ready", wait=False)
            for g in range(6):
                b = group()
                freed_wait(dve.tensor_copy(pT[:, g, :], ps[:, b, :]))
                step(dve.memset(stat[:, 126:127], 0.0), "pT_ready", wait=False)
            for blk in range(2):
                b = group()
                freed(dve.tensor_copy(yaT[:, :, blk * P:(blk + 1) * P], bank4(b)))
            dve.wait_ge(v_free, nv[0])
            step(dve.memset(stat[:, 120:121], 0.0), "ya_ready", wait=False)
            for g in range(4):
                b = group()
                freed_wait(dve.tensor_tensor(gaT[:, 2 * g:2 * g + 2, :], gaT[:, 2 * g:2 * g + 2, :], bank2(b), ALU.mult))
                ins = dve.tensor_tensor(gaT[:, 2 * g:2 * g + 2, :], gaT[:, 2 * g:2 * g + 2, :],
                                        gbT[:, 2 * g:2 * g + 2, :], ALU.add)
                step(ins, "merged_ready")

            def gated_sum(g, keep, cuts, a_groups=None):
                for i, (c0, c1) in enumerate(cuts):
                    for t in range(TT):
                        if a_groups is not None and i < 2:
                            n = a_groups + 2 * i + t
                            dve.wait_ge(a_full, n + 1)
                            step(dve.tensor_tensor(tok[:, t, c0:c1], ps[:, 4 + n % 4, 0:c1 - c0], gB[:, g, c0:c1],
                                                   ALU.mult))
                            dve.scalar_tensor_tensor(out=x[:, t, c0:c1], in0=x[:, t, c0:c1], scalar=keep,
                                                     in1=tok[:, t, c0:c1], op0=ALU.mult, op1=ALU.add)\
                               .then_inc(a_free, 1)
                            dve.wait_ge(a_free, n + 1)
                            continue
                        b = group()
                        freed_wait(dve.tensor_tensor(tok[:, t, c0:c1], ps[:, b, 0:c1 - c0], gB[:, g, c0:c1], ALU.mult))
                        step(dve.scalar_tensor_tensor(out=x[:, t, c0:c1], in0=x[:, t, c0:c1], scalar=keep,
                                                      in1=tok[:, t, c0:c1], op0=ALU.mult, op1=ALU.add))

            gated_sum(0, 1.0, [(0, 512), (512, 1024)])
            step(rms(tok), "tokens_normed", wait=False)
            step(dve.scalar_tensor_tensor(out=scale_col[:, :], in0=sec(SC2), scalar=1.0, in1=colA[:, 64:72],
                                          op0=ALU.add, op1=ALU.mult), "scale_ready")
            transposed(scale_col, sec(SH2))

            def first_max(dst, src, val, n, scratch, g):
                step(dve.tensor_reduce(val, src, AX, ALU.max))
                step(dve.tensor_tensor(dst, src, val.unsqueeze(2).to_broadcast([P, g, n]), ALU.is_equal))
                step(dve.tensor_tensor(dst, dst, rev[:, 8 - n:8].unsqueeze(1).to_broadcast([P, g, n]), ALU.mult))
                step(dve.tensor_reduce(scratch, dst, AX, ALU.max))
                step(dve.tensor_tensor(dst, dst, scratch.unsqueeze(2).to_broadcast([P, g, n]), ALU.is_equal))

            def r2(lo, n):
                return rt[:, lo:lo + 2 * n].rearrange("p (a b) -> p a b", a=2)

            b = group()
            logits = r2(0, 36)
            dve.wait_ge(got_router, 80)
            freed_wait(dve.tensor_tensor(logits, ps[:, b, 0:72].rearrange("p (a b) -> p a b", a=2),
                                         b_router[:, :].unsqueeze(1).to_broadcast([P, 2, 36]), ALU.add))
            sc2 = rt[:, 300:302]
            gmax = rt[:, 302:304]
            first_max(r2(72, 4), logits[:, :, 0:4], gmax, 4, sc2, 2)
            step(dve.tensor_tensor(r2(80, 4), logits[:, :, 0:4], gmax.unsqueeze(2).to_broadcast([P, 2, 4]), ALU.subtract))
            chosen = r2(112, 8)
            step(dve.tensor_tensor(chosen, logits[:, :, 4:12], r2(72, 4)[:, :, 0:1].to_broadcast([P, 2, 8]), ALU.mult))
            for g in range(1, NG):
                step(dve.tensor_tensor(r2(192, 8), logits[:, :, 4 + 8 * g:12 + 8 * g],
                                       r2(72, 4)[:, :, g:g + 1].to_broadcast([P, 2, 8]), ALU.mult))
                step(dve.tensor_tensor(chosen, chosen, r2(192, 8), ALU.add))
            emax = rt[:, 304:306]
            step(dve.tensor_reduce(emax, chosen, AX, ALU.max))
            step(dve.tensor_tensor(r2(128, 8), chosen, emax.unsqueeze(2).to_broadcast([P, 2, 8]), ALU.subtract),
                 "router_logits")
            dve.wait_ge(router_exp, 1)
            pg_ = rt[:, 306:308]
            step(dve.tensor_reduce(pg_, r2(96, 4), AX, ALU.add))
            step(dve.reciprocal(pg_, pg_))
            esum = rt[:, 308:310]
            step(dve.tensor_reduce(esum, r2(144, 8), AX, ALU.add))
            step(dve.reciprocal(esum, esum))
            pr = r2(144, 8)
            step(dve.tensor_tensor(pr, pr, esum.unsqueeze(2).to_broadcast([P, 2, 8]), ALU.mult))

            def top2(pr, oh1, oh2, tmp, w1, w2, sc):
                first_max(oh1, pr, w1, 8, sc, 2)
                step(dve.scalar_tensor_tensor(out=tmp, in0=oh1, scalar=-3e38, in1=pr, op0=ALU.mult, op1=ALU.add))
                first_max(oh2, tmp, w2, 8, sc, 2)

            w1, w2 = rt[:, 310:312], rt[:, 312:314]
            top2(pr, r2(160, 8), r2(176, 8), r2(192, 8), w1, w2, sc2)
            den = rt[:, 314:316]
            step(dve.tensor_tensor(den, w1, w2, ALU.add))
            step(dve.reciprocal(den, den))
            step(dve.tensor_tensor(w1, w1, den, ALU.mult))
            step(dve.tensor_tensor(w2, w2, den, ALU.mult))
            step(dve.tensor_tensor(w1, w1, pg_, ALU.mult))
            step(dve.tensor_tensor(w2, w2, pg_, ALU.mult))
            step(dve.tensor_tensor(r2(160, 8), r2(160, 8), w1.unsqueeze(2).to_broadcast([P, 2, 8]), ALU.mult))
            step(dve.tensor_tensor(r2(176, 8), r2(176, 8), w2.unsqueeze(2).to_broadcast([P, 2, 8]), ALU.mult))
            step(dve.tensor_tensor(r2(160, 8), r2(160, 8), r2(176, 8), ALU.add))
            for g in range(NG):
                step(dve.tensor_tensor(combine[:, :, 8 * g:8 * g + 8], r2(160, 8),
                                       r2(72, 4)[:, :, g:g + 1].to_broadcast([P, 2, 8]), ALU.mult))
            def slots(layer, ne, cap, extra):
                step(dve.tensor_scalar(chosen_by[:, :, 0:ne], combine[:, :, 0:ne], 0.0, None, ALU.is_gt),
                     "chosen_ready")
                step(dve.memset(tok[:, :, :], 0.0), wait=False)
                step(dve.memset(y_slot, 0.0), wait=False)
                step(dve.memset(pickT, 0.0), wait=False)
                b = group()
                step(dve.memset(slot_of[:, :, ne:ne + extra], -1.0), wait=False)
                step(dve.memset(combine[:, :, ne:ne + extra], 0.0))
                place = slot_of[:, :, 0:ne]
                step(dve.tensor_scalar(place, ps[:, b, 0:2 * ne].rearrange("p (a b) -> p a b", a=2), 1.0, None, ALU.add))
                step(dve.tensor_tensor(place, place, chosen_by[:, :, 0:ne], ALU.mult))
                step(dve.tensor_scalar(place, place, -1.0, None, ALU.add))
                freed_wait(dve.tensor_reduce(stat[:, 112:113], ps[:, b, 2 * ne:3 * ne], AX, ALU.max))
                step(dve.tensor_scalar(fits[:, layer:layer + 1], stat[:, 112:113], float(cap), None, ALU.is_le))
                step(dve.memset(stat[:, 113:114], 0.0), "fits_ready")

            slots(0, NE1, CAP1, EPG1)
            step(dve.memset(stat[:, 120:121], 0.0), "mix_ready")
            dve.memset(ada_part[:, 0:1], 0.0).then_inc(ada_step, 1)
            dve.wait_ge(ada_step, 1)

            def ada_sums(i):
                dve.wait_ge(ada_full, i * 16 + 16)
                for k in range(KD):
                    if k == 0:
                        ins = dve.tensor_scalar(ada_part, ada_w[:, 0, :], csT[:, 1, 0:1], None, ALU.mult)
                    else:
                        ins = dve.scalar_tensor_tensor(out=ada_part, in0=ada_w[:, k, :], scalar=csT[:, 1, k:k + 1],
                                                       in1=ada_part, op0=ALU.mult, op1=ALU.add)
                    ins.then_inc(ada_step, 1)
                    dve.wait_ge(ada_step, i * KD + (k + 2))

            def ada_mod(i, bank):
                n = AW // P
                return dve.tensor_tensor(modT[:, 1:3, :].rearrange("p m c -> p (m c)")[:, bass.ds(i * n, n)],
                                         ps[:, bank, 0:n], colB[:, bass.ds(i * n, n)], ALU.add)

            def unit(q, u, j, e, last, weight, seq, first):
                dve.wait_ge(q["silu_done"], u + 1)
                dve.wait_ge(q["up_full"], u + 1)
                if not first:
                    dve.wait_ge(ring_free, seq - 1)
                dve.tensor_tensor(hid[:, j % 2, :], silu_g[:, j % 2, :], ps[:, 5 + 2 * (j % 2), :], ALU.mult)\
                   .then_inc(q["hid_ready"], 1)
                if last:
                    dve.wait_ge(ring_free, seq + 1)
                    for t in range(TT):
                        for half in range(2):
                            dst = tok[:, t, half * CH:(half + 1) * CH]
                            if weight is None:
                                ins = dve.tensor_copy(dst, ps[:, 2 * t + half, :])
                            else:
                                ins = dve.scalar_tensor_tensor(out=dst, in0=ps[:, 2 * t + half, :], scalar=weight(t),
                                                               in1=dst, op0=ALU.mult, op1=ALU.add)
                    ins.then_inc(q["y_free"], 1)
                    dve.wait_ge(q["y_free"], e + 1)

            def experts_all(q, n, body_e, units, seq, with_ada):
                body = body_e * units
                with dve.Fori(0, n) as i:
                    for j in range(body):
                        e = i * body_e + j // units
                        unit(q, i * body + j, j, e, j % units == units - 1,
                             lambda t: combine[:, t, bass.ds(e, 1)], i * body + (seq + j), j < 2)
                    if with_ada:
                        ada_sums(i)
                        dve.wait_ge(q["side_full"], i + 1)
                        ada_mod(i, 0).then_inc(q["side_free"], 1)

            def experts_slots(q, n, body_e, units, seq, cap, epg, with_ada):
                body, groups = body_e * units, body_e // epg
                per = epg * units
                steps = 8 * groups

                def side(i, k):
                    dve.wait_ge(q["side_full"], i * steps + (k + 1))

                def side_free(ins, i, k):
                    ins.then_inc(q["side_free"], 1)
                    dve.wait_ge(q["side_free"], i * steps + (k + 1))

                def build(g):
                    for a_ in range(epg):
                        for t in range(TT):
                            place = slot_of[:, t, bass.ds(g * epg + a_, 1)]
                            weight = combine[:, t, bass.ds(g * epg + a_, 1)]
                            dve.tensor_scalar(pickw[:, t, a_ * cap:(a_ + 1) * cap], iota[:, 0:cap], place, weight,
                                              ALU.is_equal, ALU.mult)
                            ins = dve.tensor_scalar(pick[:, t, a_ * cap:(a_ + 1) * cap], iota[:, 0:cap], place, None,
                                                    ALU.is_equal)
                    ins.then_inc(q["pick_ready"], 1)

                def dispatched(i, k):
                    for c in range(2):
                        side(i, k + c)
                        side_free(dve.tensor_copy(xT[:, 4 * c:4 * c + 4, :],
                                                  ps[:, (k + c) % 4, :].rearrange("p (a b) -> p a b", a=4)), i, k + c)

                def combined(i, k):
                    for c in range(4):
                        t, half = c // 2, c % 2
                        side(i, k + c)
                        dst = tok[:, t, half * CH:(half + 1) * CH]
                        side_free(dve.tensor_tensor(dst, dst, ps[:, (k + c) % 4, :], ALU.add), i, k + c)

                build(0)
                dispatched(0, 0)
                dve.memset(stat[:, 127:128], 0.0).then_inc(q["y_free"], 1)
                with dve.Fori(0, n) as i:
                    for gi in range(groups):
                        k = 2 + 8 * gi
                        for jj in range(per):
                            j = gi * per + jj
                            dve.wait_ge(q["silu_done"], i * body + (j + 1))
                            dve.wait_ge(ring_free, i * body + (seq + j - 1))
                            dve.tensor_tensor(hid[:, j % 2, 0:2 * cap], silu_g[:, j % 2, 0:2 * cap],
                                              ps[:, 6 + j % 2, 2 * cap:4 * cap], ALU.mult).then_inc(q["hid_ready"], 1)
                            if jj == 1:
                                combined(i, k)
                                if with_ada:
                                    side(i, k + 4)
                                    side_free(dve.tensor_copy(pickT, ps[:, (k + 4) % 4, 0:TT * P]
                                                              .rearrange("p (a b) -> p a b", a=TT)), i, k + 4)
                                else:
                                    for t in range(TT):
                                        side(i, k + 4 + t)
                                        side_free(dve.tensor_copy(pickT[:, t, :], ps[:, (k + 4 + t) % 4, 0:P]),
                                                  i, k + 4 + t)
                                build(i * groups + (gi + 1))
                                if with_ada:
                                    ada_sums(i)
                        if with_ada:
                            side(i, k + 5)
                            side_free(ada_mod(i, (k + 5) % 4), i, k + 5)
                        dispatched(i, k + 6)
                        dve.wait_ge(ring_free, i * body + (seq + (gi + 1) * per))
                        for half in range(2):
                            ins = dve.tensor_copy(y_slot[:, half * CH:(half + 1) * CH], ps[:, 4 + half, :])
                        ins.then_inc(q["y_free"], 1)
                combined(n - 1, 2 + 8 * groups)

            def experts(layer, q, n, body_e, units, seq, cap, epg, with_ada):
                flag = dve.value_load(fits[0:1, layer:layer + 1], min_val=0, max_val=1)
                with dve.If(flag == 1):
                    experts_slots(q, n, body_e, units, seq, cap, epg, with_ada)
                with dve.Else():
                    experts_all(q, n, body_e, units, seq, with_ada)

            experts(0, PH[0], NE1 // 2, 2, U1, MOE1_SEQ, CAP1, EPG1, True)

            def gated_ffn(keep):
                for t in range(TT):
                    step(dve.tensor_tensor(tok[:, t, :], tok[:, t, :], gB[:, 1, :], ALU.mult))
                    step(dve.scalar_tensor_tensor(out=x[:, t, :], in0=x[:, t, :], scalar=keep, in1=tok[:, t, :],
                                                  op0=ALU.mult, op1=ALU.add))

            gated_ffn(1.0)
            rms(x)
            step(dve.memset(stat[:, 126:127], 0.0))
            dve.wait_ge(v_free, nv[0])
            for layer in range(2):
                if layer == 0:
                    modulate(colC[:, 0, :], None, SC1, SH1, 1)
                else:
                    modulate(colC[:, 3, :], colC[:, 4, :], SC1, SH1, 2)
                gates(layer + 1, 1.0)
                rows_got += 16 if layer == 0 else 32
                dve.wait_ge(got_rows, rows_got)
                dve.wait_ge(a_free, A_DECAYS[layer] - 4)
                affine(x, rowB[:, 0, :], None if layer == 0 else rowB[:, 1, :])
                step(dve.memset(stat[:, 121:122], 0.0), "rows_used")
                for g in range(2):
                    b = group()
                    freed(dve.tensor_copy(cbT[:, 2 * g:2 * g + 2, :], bank2(b)))
                for g in range(2):
                    b = group()
                    freed_wait(dve.tensor_copy(ccT[:, 2 * g:2 * g + 2, :], bank2(b)))
                step(dve.memset(zT[:, :, 0:2], 0.0))
                for g in range(2):
                    b = group()
                    freed_wait(dve.tensor_tensor(zT[:, 2 * g:2 * g + 2, 2:T + 2], ccT[:, 2 * g:2 * g + 2, :], bank2(b), ALU.mult))
                for dst in (q2T, k2T, k_tok):
                    b = group()
                    freed_wait(dve.tensor_copy(dst, bank2(b)))
                for t in range(TT):
                    b = group()
                    freed_wait(dve.tensor_copy(v2[:, t, :], ps[:, b, :]))
                b = group()
                freed_wait(dve.tensor_copy(glT, ps[0:16, b, 0:T]))
                step(dve.memset(stat[:, 124:125], 0.0), "glow_ready", wait=False)
                b = group()
                dve.wait_ge(got_layer, 48 * (layer + 1))
                freed_wait(dve.tensor_tensor(gk, bank2(b), gkbB[:, :].unsqueeze(1).to_broadcast([P, 2, T]), ALU.add))
                step(dve.tensor_scalar(gkt, gk, -1.0, None, ALU.mult))
                step(dve.tensor_tensor(gku, gk, gkt, ALU.min), "gk_abs")
                dve.wait_ge(gk_e, layer + 1)
                step(dve.tensor_scalar(gku, gku, 1.0, None, ALU.add), "gk_exp1")
                dve.wait_ge(gk_l, layer + 1)
                step(dve.scalar_tensor_tensor(out=gk, in0=gk, scalar=0.0, in1=gku, op0=ALU.min, op1=ALU.subtract))
                step(dve.tensor_scalar(gk, gk, 1.0 / GK_DIV, GK_MIN, ALU.mult, ALU.max), "gk_ready")
                for tap in range(3):
                    for c in range(4):
                        w = colA[:, 80 + layer * 12 + tap * 4 + c:81 + layer * 12 + tap * 4 + c]
                        src = zT[:, c, tap:tap + T]
                        if tap == 0:
                            ins = dve.tensor_scalar(conv[:, c, :], src, w, None, ALU.mult)
                        else:
                            ins = dve.scalar_tensor_tensor(out=conv[:, c, :], in0=src, scalar=w, in1=conv[:, c, :],
                                                           op0=ALU.mult, op1=ALU.add)
                    step(ins)
                step(dve.tensor_tensor(cbT, cbT, conv, ALU.mult))
                dve.wait_ge(a_free, A_DECAYS[layer])
                step(dve.scalar_tensor_tensor(out=q2T, in0=q2T, scalar=DK ** -0.5, in1=ebT, op0=ALU.mult, op1=ALU.mult),
                     wait=False)
                step(dve.tensor_tensor(k2T, k2T, enbT, ALU.mult), wait=False)
                step(dve.tensor_tensor(k_tok, k_tok, er, ALU.mult), "gla_in")
                for par in range(2):
                    b = group()
                    freed_wait(dve.tensor_tensor(scT[:, par, :, :], bank4(b),
                                                 chunk_triu[:, :].unsqueeze(1).to_broadcast([P, 4, P]), ALU.mult))
                step(dve.memset(stat[:, 125:126], 0.0), "gla_scores", wait=False)
                sg8 = sg_tok.rearrange("p t (a v) -> p (t a) v", v=DV)
                step(dve.tensor_tensor(sg8, sg8,
                                       glnB[:, :].unsqueeze(1).to_broadcast([P, TT * GH, DV]), ALU.mult), wait=False)
                for c in range(3):
                    b = group()
                    if c == 0:
                        freed_wait(dve.tensor_copy(state[:, 0, :, :], ps[:, b, 0:2 * DV].rearrange("p (a b) -> p a b", a=2)))
                    else:
                        for f in range(2):
                            ins = dve.scalar_tensor_tensor(out=state[:, c, f, :], in0=state[:, c - 1, f, :],
                                                           scalar=ebT[:, f, c * CK + CK - 1:c * CK + CK],
                                                           in1=ps[:, b, f * DV:(f + 1) * DV], op0=ALU.mult, op1=ALU.add)
                        freed_wait(ins)
                step(dve.memset(stat[:, 126:127], 0.0), "states_ready", wait=False)
                for par in range(2):
                    b = group()
                    freed_wait(dve.tensor_copy(
                        o_tok.rearrange("p t (f a v) -> p t f a v", a=2, v=DV)[:, :, :, par, :],
                        ps[:, b, :].rearrange("p (t f v) -> p t f v", t=2, f=2)))
                o8 = o_tok.rearrange("p t (a v) -> p (t a) v", v=DV)
                t8 = tok[:, 0, :].rearrange("p (a v) -> p a v", v=DV)
                step(dve.tensor_tensor(t8, o8, o8, ALU.mult))
                step(dve.tensor_reduce(stat[:, 0:8], t8, AX, ALU.add))
                rstd(stat[:, 8:16], stat[:, 0:8], 1.0 / DV, RMS_EPS)
                step(dve.tensor_tensor(o_tok, o_tok, sg_tok, ALU.mult))
                for t in range(TT):
                    step(dve.tensor_tensor(o8[:, GH * t:GH * t + GH, :], o8[:, GH * t:GH * t + GH, :],
                                           stat[:, 8 + GH * t:8 + GH * t + GH].unsqueeze(2).to_broadcast([P, GH, DV]),
                                           ALU.mult), "o_normed", wait=False)
                step(dve.memset(stat[:, 121:122], 0.0), "layer_used")
                for t in range(TT):
                    b = group()
                    freed_wait(dve.tensor_copy(ygT[:, :, t * P:(t + 1) * P], bank4(b)))
                step(dve.memset(stat[:, 120:121], 0.0), "ya_ready", wait=False)
                gated_sum(0, ALPHA, W_OUT_CUTS[layer], A_DECAYS[layer])

                def gain_x():
                    nonlocal rows_got
                    rows_got += 32
                    dve.wait_ge(got_rows, rows_got)
                    affine(x, rowB[:, 0, :], rowB[:, 1, :])

                layer_norm(D, x, LN_EPS)
                if layer == 0:
                    modulate(colC[:, 1, :], colC[:, 2, :], SC2, SH2, 1)
                else:
                    gain_x()
                    step(dve.memset(stat[:, 121:122], 0.0), "rows_used")
                    step(dve.tensor_scalar(scale_col[:, :], sec(SC2, 2), 1.0, None, ALU.add), "tokens_normed")
                    transposed(scale_col, sec(SH2, 2))
                if layer == 0:
                    step(dve.memset(stat[:, 124:125], 0.0), "mix_ready")
                    dve.wait_ge(a_free, A_DECAYS[layer] + 6)
                    gain_x()
                    step(dve.memset(stat[:, 121:122], 0.0), "rows_used")
                    for j in range(U2):
                        unit(PH[1], j, j, 0, j == U2 - 1, None, FFN_SEQ + j, j < 2)
                else:
                    b = group()
                    freed_wait(dve.tensor_copy(r2(0, 8), ps[:, b, 0:16].rearrange("p (a b) -> p a b", a=2)))
                    m1, m2 = rt[:, 310:312], rt[:, 312:314]
                    top2(r2(0, 8), r2(160, 8), r2(176, 8), r2(192, 8), m1, m2, sc2)
                    step(dve.tensor_tensor(rt[:, 16:18], m2, m1, ALU.subtract), wait=False)
                    step(dve.memset(rt[:, 18:32], 0.0), "router_logits")
                    dve.wait_ge(router_exp, 2)
                    e2 = rt[:, 32:34]
                    step(dve.tensor_scalar(w1, e2, 1.0, None, ALU.add))
                    step(dve.reciprocal(w1, w1))
                    step(dve.tensor_tensor(w2, e2, w1, ALU.mult))
                    step(dve.tensor_tensor(r2(160, 8), r2(160, 8), w1.unsqueeze(2).to_broadcast([P, 2, 8]), ALU.mult))
                    step(dve.tensor_tensor(r2(176, 8), r2(176, 8), w2.unsqueeze(2).to_broadcast([P, 2, 8]), ALU.mult))
                    step(dve.tensor_tensor(combine[:, :, 0:8], r2(160, 8), r2(176, 8), ALU.add))
                    slots(1, NE2, CAP2, EPG2)
                    step(dve.memset(stat[:, 120:121], 0.0), "mix_ready")
                    experts(1, PH[2], NE2 // 4, 4, U2, MOE2_SEQ, CAP2, EPG2, False)
                gated_ffn(ALPHA)
                layer_norm(D, x, LN_EPS)
                if layer == 1:
                    gain_x()
                    step(dve.memset(stat[:, 121:122], 0.0), "x_ready")

        @block.tensor
        def _(pe):
            r = Ring()
            nv, na = [0], [0]
            owed = [False]

            def mm(*args, **kw):
                ins = pe.matmul(*args, **kw)
                if owed[0]:
                    ins.then_inc(ring_free, 1)
                    owed[0] = False
                    return None
                return ins

            def tr(*args):
                ins = pe.transpose(*args)
                if owed[0]:
                    ins.then_inc(ring_free, 1)
                    owed[0] = False
                    return None
                return ins

            def free():
                assert not owed[0]
                owed[0] = True

            def gv_():
                if nv[0] >= 4:
                    pe.wait_ge(v_free, nv[0] - 3)
                nv[0] += 1
                return (nv[0] - 1) % 4

            def ga_():
                if na[0] >= 4:
                    pe.wait_ge(a_free, na[0] - 3)
                na[0] += 1
                return 4 + (na[0] - 1) % 4

            def take(dmas=1):
                s, full, _ = r.take(dmas)
                pe.wait_ge(ring_full[s], full)
                return s

            def transposes(src, n, rows_, bank, rid=P):
                for j in range(n):
                    last = tr(ps[0:P, bank, j * rows_:(j + 1) * rows_], src(j), ident[0:rid, 0:rid])
                return last

            pe.wait_ge(first_consts, 1)
            pe.wait_ge(got_vec, 112)
            pe.transpose(ps[:, gv_(), 0:104], vecA, ident[0:104, 0:104]).then_inc(v_full, 1)
            pe.transpose(ps[:, gv_(), 0:96], vecB, ident[0:96, 0:96]).then_inc(v_full, 1)
            pe.wait_ge(got_spatial, 32)
            for t in range(2):
                transposes(lambda j: prob[:, 0, (2 * t + j) * P:(2 * t + j + 1) * P], 2, P, gv_()).then_inc(v_full, 1)

            def ada():
                pe.wait_ge(silu_c, 1)
                assert r.seq == 0
                with pe.Fori(0, 3) as h:
                    def columns(c):
                        pe.wait_ge(row_copied, h * 4 + (c + 1))
                        for f in range(4):
                            last = mm(ps[:, 7, bass.ds(h * 16 + (4 * c + f), 1)],
                                      ada_row[0:1, c % 2, f * P:(f + 1) * P], ones[0:1, 0:1], start=True, stop=True)
                        return last

                    for c in range(4):
                        pe.wait_ge(ring_full[c], h * 16 + 16)
                        for k in range(KD):
                            last = mm(ps[0:1, 4 + c % 2, :], csT[:, 0, k:k + 1], slot(c, KD, CH)[:, k, :],
                                      start=(k == 0), stop=(k == KD - 1))
                        last.then_inc(ring_free, 1)
                        if c:
                            columns(c - 1)
                    columns(3).then_inc(mod_full, 1)
                for _ in range(12):
                    r.take(1)

            def gates(m):
                for g in range(2):
                    pe.wait_ge(H["gate_cols"], 2 * m + g + 1)
                    for half in range(2):
                        bank = gv_()
                        for j in range(4):
                            last = mm(ps[:, bank, j * P:(j + 1) * P], colsB[:, 4 * half + j, :], ident[:, :],
                                      start=True, stop=True)
                        last.then_inc(v_full, 1)

            def token_transposes(src):
                for t in range(TT):
                    for half, (bank, full) in enumerate(((gv_(), v_full), (ga_(), a_full))):
                        transposes(lambda j: src[:, t, (4 * half + j) * P:(4 * half + j + 1) * P], 4, P, bank)\
                            .then_inc(full, 1)

            def hT_ready(n):
                pe.wait_ge(H["hT_ready"], n)
                pe.wait_ge(a_free, na[0])

            def feature_major(w, rhs, tiles, bank, cols=lambda f: f * P, kt=KD, m=P):
                for i, f in enumerate(tiles):
                    for k in range(kt):
                        last = mm(ps[0:m, bank, i * T:(i + 1) * T], w[:, k, cols(f):cols(f) + m], rhs(k),
                                         start=(k == 0), stop=(k == kt - 1))
                return last

            def token_major(lhs, w, t, c0, c1, bank, at=0, kt=KD):
                for k in range(kt):
                    last = mm(ps[:, bank, at:at + c1 - c0], lhs(k, t), w[:, k, c0:c1],
                                     start=(k == 0), stop=(k == kt - 1))
                return last

            def h_rhs(k):
                return hT[:, k, :]

            def h_lhs(k, t):
                return hT[:, k, t * P:(t + 1) * P]

            ada()
            pe.wait_ge(consts_ready, 1)
            pe.wait_ge(got_gains, 80)
            pe.transpose(ps[:, gv_(), 0:5 * KD], vecC, ident[0:5 * KD, 0:5 * KD]).then_inc(v_full, 1)
            pe.wait_ge(H["tokens_normed"], 1)
            token_transposes(tok)
            hT_ready(1)
            gates(0)
            s = take(10)
            w = slot(s, KD, 768)
            for g in range(2):
                feature_major(w, h_rhs, (2 * g, 2 * g + 1), gv_()).then_inc(v_full, 1)
            feature_major(w, h_rhs, (4,), gv_()).then_inc(v_full, 1)
            bank = gv_()
            token_major(h_lhs, w, 0, 640, 768, bank)
            token_major(h_lhs, w, 1, 640, 768, bank, at=P).then_inc(v_full, 1)
            free()
            pe.wait_ge(H["mod_read"], 1)
            s = take()
            for g in range(2):
                feature_major(slot(s, KD, CH), h_rhs, (2 * g, 2 * g + 1), ga_()).then_inc(a_full, 1)
            free()
            s = take()
            for t in range(TT):
                token_major(h_lhs, slot(s, KD, CH), t, 0, CH, ga_()).then_inc(a_full, 1)
            free()
            for c in range(4):
                s = take()
                for g in range(2):
                    feature_major(slot(s, KD, CH), h_rhs, (2 * g, 2 * g + 1), ga_()).then_inc(a_full, 1)
                free()
            pe.wait_ge(H["vn_ready"], 1)
            for t in range(TT):
                bank = gv_()
                for g in range(4):
                    last = mm(ps[:, bank, g * P:(g + 1) * P], gv[:, t, g * P:(g + 1) * P], wsT[:, g, :],
                                     start=True, stop=True)
                last.then_inc(v_full, 1)
            pe.wait_ge(H["qkv_ready"], 1)
            for g in range(6):
                nh = 4 if g < 2 else 2
                h0 = 4 * g if g < 2 else 2 * (g - 2)
                bank = gv_()
                for i in range(nh):
                    hd = h0 + i
                    base, j = HD * (hd // GROUP_HEADS), hd % GROUP_HEADS
                    q0, keys = (0, P) if g < 2 else (P, T)
                    last = mm(ps[:, bank, i * keys:(i + 1) * keys], qT[base:base + HD, j, q0:q0 + P],
                                     kT[base:base + HD, 0:keys], start=True, stop=True)
                last.then_inc(v_full, 1)
            pe.wait_ge(H["yb_ready"], 1)
            s = take()
            for g in range(4):
                feature_major(slot(s, 4, D), lambda k: guT[:, k, :], (2 * g, 2 * g + 1), gv_(), kt=4).then_inc(v_full, 1)
            free()
            for g in range(6):
                pe.wait_ge(H["probs_ready"], g + 1)
                transposes(lambda j: prob[:, g, j * P:(j + 1) * P], 4, P, gv_()).then_inc(v_full, 1)
            for blk in range(2):
                pe.wait_ge(H["pT_ready"], 2 + 4 * blk)
                bank = gv_()
                for hd in range(HEADS):
                    base, kv = HD * (hd % 2), hd // GROUP_HEADS
                    dst = ps[base:base + HD, bank, (hd // 2) * P:(hd // 2 + 1) * P]
                    if blk == 0:
                        last = mm(dst, v_tok[:, 0, kv * HD:(kv + 1) * HD],
                                         pT[:, hd // 4, (hd % 4) * P:(hd % 4 + 1) * P], start=True, stop=True)
                    else:
                        for kt in range(2):
                            at = (2 * (hd % 2) + kt) * P
                            last = mm(dst, v_tok[:, kt, kv * HD:(kv + 1) * HD],
                                             pT[:, 2 + hd // 2, at:at + P], start=(kt == 0), stop=(kt == 1))
                last.then_inc(v_full, 1)
            pe.wait_ge(H["ya_ready"], 1)
            for c in range(2):
                s = take()
                for g in range(2):
                    feature_major(slot(s, 4, CH), lambda k: yaT[:, k, :], (2 * g, 2 * g + 1), gv_(), kt=4)\
                        .then_inc(v_full, 1)
                free()
            pe.wait_ge(H["merged_ready"], 4)
            for c in range(2):
                s = take()
                for t in range(TT):
                    token_major(lambda k, t: gaT[:, k, t * P:(t + 1) * P], slot(s, KD, CH), t, 0, CH, gv_())\
                        .then_inc(v_full, 1)
                free()
            pe.wait_ge(H["tokens_normed"], 2)
            token_transposes(tok)
            hT_ready(2)
            pe.wait_ge(got_router, 80)

            def router(w, n):
                bank = gv_()
                for t in range(TT):
                    last = token_major(h_lhs, w, t, 0, n, bank, at=t * n)
                last.then_inc(v_full, 1)

            router(w_router, 36)

            def unit_in(q, s, u, full, j, first):
                pe.wait_ge(ring_full[s], full)
                if not first:
                    pe.wait_ge(q["hid_ready"], u - 1)
                b = 4 + 2 * (j % 2)
                feature_major(slot_gate(s), h_rhs, (0, 1), b).then_inc(q["gate_full"], 1)
                feature_major(slot_up(s), h_rhs, (0, 1), b + 1).then_inc(q["up_full"], 1)

            def unit_down(q, s, u, j, opens, closes):
                pe.wait_ge(q["hid_ready"], u + 1)
                for t in range(TT):
                    for half in range(2):
                        for f in range(2):
                            last = mm(ps[:, 2 * t + half, :], hid[:, j % 2, f * T + t * P:f * T + (t + 1) * P],
                                      slot_down(s)[:, f, half * CH:(half + 1) * CH],
                                      start=(opens and f == 0), stop=(closes and f == 1))
                last.then_inc(ring_free, 1)

            def ada_columns(q, i, bank):
                pe.wait_ge(ada_step, i * KD + (KD + 1))
                for f in range(AW // P):
                    last = mm(ps[:, bank, f:f + 1], ada_part[:, f * P:(f + 1) * P], ones[:, 0:1], start=True, stop=True)
                last.then_inc(q["side_full"], 1)

            def experts_all(q, at, n, body_e, units, with_ada):
                body = body_e * units
                with pe.Fori(0, n) as i:
                    def down(j):
                        k = j % units
                        unit_down(q, j % SLOTS, i * body + j, j, k == 0, k == units - 1)
                    for j in range(body):
                        s, full, _ = at(i, j)
                        unit_in(q, s, i * body + j, full, j, j < 2)
                        if j:
                            down(j - 1)
                    down(body - 1)
                    if with_ada:
                        pe.wait_ge(q["y_free"], i * body_e + body_e)
                        ada_columns(q, i, 0)
                pe.wait_ge(q["y_free"], n * body_e)
                if with_ada:
                    pe.wait_ge(q["side_free"], n)

            def experts_slots(q, at, n, body_e, units, cap, epg, with_ada):
                body, groups, per = body_e * units, body_e // epg, epg * units
                steps = 8 * groups

                def side(i, k):
                    pe.wait_ge(q["side_free"], i * steps + (k - 3))
                    return k % 4

                def dispatch(i, k, picks, first=False):
                    pe.wait_ge(q["pick_ready"], picks)
                    for c in range(2):
                        bank = c if first else side(i, k + c)
                        for kt in range(4):
                            for t in range(TT):
                                last = mm(ps[:, bank, kt * SL:(kt + 1) * SL],
                                          h_tok[:, t, (4 * c + kt) * P:(4 * c + kt + 1) * P], pick[:, t, :],
                                          start=(t == 0), stop=(t == TT - 1))
                        last.then_inc(q["side_full"], 1)

                def combine_(i, k, done, first=False):
                    pe.wait_ge(q["y_free"], done)
                    for c in range(4):
                        t, half = c // 2, c % 2
                        bank = c + 2 if first and c < 2 else side(i, k + c)
                        mm(ps[:, bank, :], pickT[:, t, :], y_slot[:, half * CH:(half + 1) * CH],
                           start=True, stop=True).then_inc(q["side_full"], 1)

                def gate_up(i, j, full):
                    s, a_ = j % SLOTS, (j % per) // units
                    pe.wait_ge(ring_full[s], full)
                    if j >= 2:
                        pe.wait_ge(q["hid_ready"], i * body + (j - 1))
                    for part, w in enumerate((slot_gate(s), slot_up(s))):
                        for f in range(2):
                            o = (2 * part + f) * cap
                            for k in range(KD):
                                last = mm(ps[:, 6 + j % 2, o:o + cap], w[:, k, f * P:(f + 1) * P],
                                          xT[:, k, a_ * cap:(a_ + 1) * cap], start=(k == 0), stop=(k == KD - 1))
                    last.then_inc(q["unit_full"], 1)

                def down(i, j):
                    a_, k = (j % per) // units, j % units
                    pe.wait_ge(q["hid_ready"], i * body + (j + 1))
                    for half in range(2):
                        for f in range(2):
                            last = mm(ps[a_ * cap:(a_ + 1) * cap, 4 + half, :], hid[:, j % 2, f * cap:(f + 1) * cap],
                                      slot_down(j % SLOTS)[:, f, half * CH:(half + 1) * CH],
                                      start=(k == 0 and f == 0), stop=(k == units - 1 and f == 1))
                    last.then_inc(ring_free, 1)

                dispatch(0, 0, 1, first=True)
                with pe.Fori(0, n) as i:
                    for gi in range(groups):
                        k = 2 + 8 * gi
                        pe.wait_ge(q["side_free"], i * steps + k)
                        for jj in range(per):
                            j = gi * per + jj
                            gate_up(i, j, at(i, j)[1])
                            if jj == 1:
                                pe.wait_ge(q["y_free"], i * groups + (gi + 1))
                            if jj:
                                down(i, j - 1)
                            if jj == 1:
                                combine_(i, k, i * groups + (gi + 1), first=gi == 0)
                                if with_ada:
                                    bank = side(i, k + 4)
                                    for t in range(TT):
                                        last = tr(ps[:, bank, t * P:(t + 1) * P], pickw[:, t, :], ident[:, :])
                                    last.then_inc(q["side_full"], 1)
                                else:
                                    for t in range(TT):
                                        tr(ps[:, side(i, k + 4 + t), 0:P], pickw[:, t, :], ident[:, :])\
                                            .then_inc(q["side_full"], 1)
                            if jj == per - 1:
                                if with_ada:
                                    ada_columns(q, i, side(i, k + 5))
                                dispatch(i, k + 6, i * groups + (gi + 2))
                        down(i, gi * per + per - 1)
                combine_(n - 1, 2 + 8 * groups, n * groups + 1)
                pe.wait_ge(q["side_free"], 2 + 8 * groups * n + 4)

            def experts(layer, q, n, body_e, units, cap, epg, with_ada):
                at = r.loop(n, body_e * units)
                assert not owed[0]
                pe.wait_ge(v_free, nv[0])
                pe.wait_ge(a_free, na[0])
                flag = pe.value_load(fits[0:1, layer:layer + 1], min_val=0, max_val=1)
                with pe.If(flag == 1):
                    experts_slots(q, at, n, body_e, units, cap, epg, with_ada)
                with pe.Else():
                    experts_all(q, at, n, body_e, units, with_ada)

            def find_slots(layer, ne):
                for t in range(TT):
                    for half in range(2):
                        bank = ga_()
                        for j in range(4):
                            last = tr(ps[:, bank, j * P:(j + 1) * P], hT[:, 4 * half + j, t * P:(t + 1) * P], ident[:, :])
                        last.then_inc(a_full, 1)
                pe.wait_ge(H["chosen_ready"], layer + 1)
                bank = gv_()
                mm(ps[:, bank, 0:ne], strict[:, :], chosen_by[:, 0, 0:ne], start=True, stop=True)
                for at, m1 in ((ne, strict), (2 * ne, ones)):
                    mm(ps[:, bank, at:at + ne], ones[:, :], chosen_by[:, 0, 0:ne], start=True, stop=False)
                    last = mm(ps[:, bank, at:at + ne], m1[:, :], chosen_by[:, 1, 0:ne], start=False, stop=True)
                last.then_inc(v_full, 1)

            find_slots(0, NE1)
            pe.wait_ge(H["mix_ready"], 1)
            experts(0, PH[0], NE1 // 2, 2, U1, CAP1, EPG1, True)
            for layer in range(2):
                pe.wait_ge(H["tokens_normed"], 3 + 2 * layer)
                token_transposes(x)
                hT_ready(3 + 2 * layer)
                gates(layer + 1)
                for c in range(3):
                    s = take()
                    for g in range(2):
                        feature_major(slot(s, KD, CH), h_rhs, (2 * g, 2 * g + 1), gv_()).then_inc(v_full, 1)
                    free()
                s = take()
                w = slot(s, KD, CH)
                for g in range(2):
                    feature_major(w, h_rhs, (2 * g, 2 * g + 1), gv_()).then_inc(v_full, 1)
                bank = gv_()
                token_major(h_lhs, w, 0, T, 2 * T, bank)
                token_major(h_lhs, w, 1, T, 2 * T, bank, at=T).then_inc(v_full, 1)
                free()
                s = take()
                for t in range(TT):
                    token_major(h_lhs, slot(s, KD, CH), t, 0, CH, gv_()).then_inc(v_full, 1)
                free()
                s = take()
                w = slot(s, KD, 528)
                for t in range(TT):
                    token_major(h_lhs, w, t, 0, CH, ga_()).then_inc(a_full, 1)
                feature_major(w, h_rhs, (0,), gv_(), cols=lambda f: CH, m=16).then_inc(v_full, 1)
                free()
                pe.wait_ge(H["glow_ready"], layer + 1)
                pe.wait_ge(got_layer, 48 * (layer + 1))
                bank = gv_()
                for t in range(TT):
                    last = mm(ps[:, bank, t * T:(t + 1) * T], glT[:, t * P:(t + 1) * P], gkw2[:, :],
                                     start=True, stop=True)
                last.then_inc(v_full, 1)
                pe.wait_ge(H["gk_ready"], layer + 1)
                bank = ga_()
                for f in range(2):
                    for t in range(TT):
                        last = mm(ps[:, bank, f * T + t * P:f * T + (t + 1) * P], gk[:, t, f * P:(f + 1) * P],
                                         chunk_triu[:, :], start=True, stop=True)
                last.then_inc(a_full, 1)
                bank = ga_()
                for t in range(TT):
                    last = mm(ps[:, bank, t * T:(t + 1) * T], chunk_tril[:, :], gk[:, t, :], start=True, stop=True)
                last.then_inc(a_full, 1)
                pe.wait_ge(H["gla_in"], layer + 1)
                for par in range(2):
                    base, bank = DK * par, gv_()
                    for t in range(TT):
                        for f in range(2):
                            at = (2 * t + f) * P
                            last = mm(ps[:, bank, at:at + P], k2T[base:base + DK, f, t * P:(t + 1) * P],
                                             q2T[base:base + DK, f, t * P:(t + 1) * P], start=True, stop=True)
                    last.then_inc(v_full, 1)
                for c in range(3):
                    bank, rb, t = gv_(), CK * (c % 2), c // 2
                    for hd in range(GH):
                        ob, f = DK * (hd % 2), hd // 2
                        last = mm(ps[ob:ob + DK, bank, f * DV:(f + 1) * DV],
                                         k_tok[rb:rb + CK, t, hd * DK:(hd + 1) * DK],
                                         v2[rb:rb + CK, t, hd * DV:(hd + 1) * DV], start=True, stop=True)
                    last.then_inc(v_full, 1)
                pe.wait_ge(H["gla_scores"], layer + 1)
                pe.wait_ge(H["states_ready"], layer + 1)
                for par in range(2):
                    base, bank = DK * par, gv_()
                    for t in range(TT):
                        for f in range(2):
                            at = (2 * t + f) * P
                            hd = 2 * f + par
                            last = mm(ps[:, bank, at:at + DV], scT[:, par, 2 * t + f, :],
                                      v2[:, t, hd * DV:(hd + 1) * DV], start=True, stop=False,
                                      skip_group_check=True)
                            for c in (2 * t, 2 * t + 1):
                                if c == 0:
                                    continue
                                ob = CK * (c % 2)
                                last = mm(ps[ob:ob + CK, bank, at:at + DV],
                                          q2T[base:base + DK, f, c * CK:(c + 1) * CK],
                                          state[base:base + DK, c - 1, f, :], start=False, stop=True,
                                          skip_group_check=True)
                    last.then_inc(v_full, 1)
                projected = []
                for c0, c1 in W_OUT_CUTS[layer][:2]:
                    s = take()
                    for t in range(TT):
                        bank = ga_()
                        for k in range(4):
                            mm(ps[:, bank, 0:c1 - c0], cbT[:, k, t * P:(t + 1) * P], slot(s, KD, c1 - c0)[:, k, :],
                               start=(k == 0), stop=False, skip_group_check=True)
                        projected.append((s, t, c1 - c0, bank))
                for t in range(TT):
                    pe.wait_ge(H["o_normed"], 2 * layer + t + 1)
                    transposes(lambda j: o_tok[:, t, j * P:(j + 1) * P], 4, P, gv_()).then_inc(v_full, 1)
                pe.wait_ge(H["ya_ready"], 2 + layer)
                for s, t, n, bank in projected:
                    for k in range(4):
                        last = mm(ps[:, bank, 0:n], ygT[:, k, t * P:(t + 1) * P], slot(s, KD, n)[:, 4 + k, :],
                                  start=False, stop=(k == 3), skip_group_check=True)
                    last.then_inc(a_full, 1)
                    if t == TT - 1:
                        free()
                for c0, c1 in W_OUT_CUTS[layer][2:]:
                    s = take()
                    for t in range(TT):
                        token_major(lambda k, t: (cbT if k < 4 else ygT)[:, k % 4, t * P:(t + 1) * P],
                                    slot(s, KD, c1 - c0), t, 0, c1 - c0, gv_()).then_inc(v_full, 1)
                    free()
                pe.wait_ge(H["tokens_normed"], 4 + 2 * layer)
                token_transposes(x)
                hT_ready(4 + 2 * layer)
                if layer == 0:
                    pe.wait_ge(H["mix_ready"], 2)
                    pe.wait_ge(v_free, nv[0])
                    pe.wait_ge(a_free, na[0])
                    prev = None
                    for j in range(U2):
                        s, full, _ = r.take(3)
                        unit_in(PH[1], s, j, full, j, j < 2)
                        if prev is not None:
                            unit_down(PH[1], prev, j - 1, j - 1, j == 1, False)
                        prev = s
                    unit_down(PH[1], prev, U2 - 1, U2 - 1, False, True)
                    pe.wait_ge(PH[1]["y_free"], 1)
                else:
                    router(w_router2, NE2)
                    find_slots(1, NE2)
                    pe.wait_ge(H["mix_ready"], 3)
                    experts(1, PH[2], NE2 // 4, 4, U2, CAP2, EPG2, False)


_INS = ['x', 'c', 'positions', 'rel_bias', 'w_ada', 'b_ada', 'norm1_g', 'w_in', 'sinks', 'gm_ln_g', 'gm_ln_b',
        'gm_w_s', 'gm_b_s', 'p_a', 'p_b', 'w_o', 'norm2_g', 'w_router_g', 'b_router_g', 'w_router_e', 'b_router_e',
        'w_gate', 'w_up', 'w_down', 'final_g', 'c_2', 'ada_w_2', 'ada_b_2', 'w_in_2', 'conv_w_2', 'gk_w2_2',
        'gk_b_2', 'gla_norm_w_2', 'w_out_2', 'ln1_g_2', 'ln1_b_2', 'ln2_g_2', 'ln2_b_2', 'ffn_w_gate_2',
        'ffn_w_up_2', 'ffn_w_down_2', 'router_w_2', 'moe_w_gate_2', 'moe_w_up_2', 'moe_w_down_2']


def kernel(**inputs):
    import numpy as _np
    import concourse.bacc as _bacc
    from concourse import mybir as _mybir
    from concourse.bass_utils import run_bass_kernel_spmd as _run

    nc = _bacc.Bacc("TRN2", target_bir_lowering=False, num_devices=1)
    arrays, aps = {}, {}
    for name in _INS:
        v = _np.ascontiguousarray(inputs[name])
        arrays[f"in_{name}_dram"] = v
        aps[name] = nc.dram_tensor(f"in_{name}_dram", v.shape, _mybir.dt.from_np(v.dtype), kind="ExternalInput").ap()
    out = nc.dram_tensor("out_0_dram", (1, T, D), F32, kind="ExternalOutput").ap()
    build(nc, aps, out)
    r = _run(nc, [arrays], core_ids=[0])
    return r.results[0]["out_0_dram"]
```
